# Optimizing a Trainium2 kernel written in Bass

```python
import math
import jax, jax.numpy as jnp
from jax import lax
import numpy as np

D_MODEL = 1024
BATCH = 1
SEQ = 256
DEPTH = 1

GRID_W = 64
CTX_LEN = 256
N_HEADS = 8
HEAD_DIM = 128
D_GDN = N_HEADS * HEAD_DIM
CONV_K = 5
GDN_CHUNK = 64
SGU_GROUPS = 8
SGU_GROUP_DIM = 128
D_SGU = SGU_GROUPS * SGU_GROUP_DIM
SGU_CHUNK = 128
ROWS_PER_CHUNK = SGU_CHUNK // GRID_W
N_EXPERT_GROUPS = 4
EXPERTS_PER_GROUP = 8
N_EXPERTS = N_EXPERT_GROUPS * EXPERTS_PER_GROUP
TOP_K = 2
D_EXPERT = 256
N_MOD = 6
EPS = 1e-6
COL_BETA = 3 * D_GDN
COL_A = COL_BETA + 2 * N_HEADS
COL_Z = COL_A + 2 * N_HEADS
COL_U = COL_Z + D_GDN
COL_V = COL_U + D_SGU
COL_GATE = COL_V + D_SGU
D_IN = COL_GATE + 2 * D_MODEL


def rms_norm(x, gain):
    xf = x.astype(jnp.float32)
    y = xf * lax.rsqrt(jnp.mean(xf * xf, axis=-1, keepdims=True) + EPS)
    return (y * gain.astype(jnp.float32)).astype(x.dtype)

def layer_norm(x, gain, bias):
    xf = x.astype(jnp.float32)
    mu = jnp.mean(xf, axis=-1, keepdims=True)
    var = jnp.mean(jnp.square(xf - mu), axis=-1, keepdims=True)
    y = (xf - mu) * lax.rsqrt(var + EPS)
    return (y * gain.astype(jnp.float32) + bias.astype(jnp.float32)).astype(x.dtype)

def l2_normalize(t):
    return t * lax.rsqrt(jnp.sum(t * t, axis=-1, keepdims=True) + EPS)

def modulate(h, shift, scale):
    return h * (1.0 + scale[:, None, :]) + shift[:, None, :]

def adaln_params(cond, w, b):
    m = jax.nn.silu(cond) @ w + b
    return m.reshape(cond.shape[0], N_MOD, D_MODEL)

def centred_depthwise_conv(x, w):
    C = x.shape[-1]
    pad = CONV_K // 2
    return lax.conv_general_dilated(
        x, w.reshape(CONV_K, 1, C).astype(x.dtype), window_strides=(1,), padding=((pad, pad),),
        dimension_numbers=('NWC', 'WIO', 'NWC'), feature_group_count=C)

def gated_delta_chunked(q, k, v, g, beta, s0):
    B, H, L, dk = q.shape
    n = L // GDN_CHUNK
    C = GDN_CHUNK
    rs = lambda t: t.reshape(B, H, n, C, *t.shape[3:])
    q, k, v, g, beta = rs(q), rs(k), rs(v), rs(g), rs(beta)
    G = jnp.cumsum(g, axis=-1)
    incl = jnp.tril(jnp.ones((C, C), dtype=bool))
    strict = jnp.tril(jnp.ones((C, C), dtype=bool), -1)
    decay = jnp.exp(jnp.where(incl, G[..., :, None] - G[..., None, :], -jnp.inf))
    kb = k * beta[..., None]
    low = jnp.where(strict, jnp.einsum('bhncd,bhnsd->bhncs', kb, k) * decay, 0.0)
    eye = jnp.eye(C, dtype=q.dtype)
    T = lax.linalg.triangular_solve(eye + low, jnp.broadcast_to(eye, low.shape), left_side=True, lower=True)
    u = T @ (v * beta[..., None])
    w = T @ (kb * jnp.exp(G)[..., None])
    qk_intra = jnp.einsum('bhncd,bhnsd->bhncs', q, k) * decay
    q_dec = q * jnp.exp(G)[..., None]
    k_dec = k * jnp.exp(G[..., -1:] - G)[..., None]
    g_last = jnp.exp(G[..., -1])

    def step(s, inp):
        u_c, w_c, qk_c, qd_c, kd_c, gl_c = inp
        v_new = u_c - w_c @ s
        o_c = qd_c @ s + qk_c @ v_new
        s = s * gl_c[..., None, None] + jnp.swapaxes(kd_c, -1, -2) @ v_new
        return s, o_c

    xs = tuple(jnp.moveaxis(t, 2, 0) for t in (u, w, qk_intra, q_dec, k_dec, g_last))
    s_final, o = lax.scan(step, s0, xs)
    o = jnp.moveaxis(o, 0, 2).reshape(B, H, L, v.shape[-1])
    return o, s_final

def gdn_scan(p_qkv, p_beta, p_a, conv_w, a_log, dt_bias, s_init):
    B, L, _ = p_qkv.shape
    qkv = jax.nn.silu(centred_depthwise_conv(p_qkv, conv_w)).astype(jnp.float32)
    heads = lambda t: jnp.swapaxes(t.reshape(B, L, N_HEADS, HEAD_DIM), 1, 2)
    q, k, v = (heads(t) for t in jnp.split(qkv, 3, axis=-1))
    q = l2_normalize(q) * (HEAD_DIM ** -0.5)
    k = l2_normalize(k)
    dirs = lambda t: t.astype(jnp.float32).reshape(B, L, 2, N_HEADS).transpose(2, 0, 3, 1)
    beta = jax.nn.sigmoid(dirs(p_beta))
    g = -jnp.exp(a_log.astype(jnp.float32))[:, None, :, None] * jax.nn.softplus(
        dirs(p_a) + dt_bias.astype(jnp.float32)[:, None, :, None])
    o_f, s_f = gated_delta_chunked(q, k, v, g[0], beta[0], s_init[0])
    flip = lambda t: jnp.flip(t, axis=2)
    o_b, s_b = gated_delta_chunked(flip(q), flip(k), flip(v), flip(g[1]), flip(beta[1]), s_init[1])
    o = jnp.swapaxes(o_f + flip(o_b), 1, 2)
    return o, jnp.stack([s_f, s_b])

def gdn_output(o, p_z, norm_g):
    B, L = o.shape[:2]
    z = p_z.astype(jnp.float32).reshape(B, L, N_HEADS, HEAD_DIM)
    y = rms_norm(o, norm_g) * jax.nn.silu(z)
    return y.reshape(B, L, D_GDN).astype(p_z.dtype)

def sgu_mixer(p_u, p_v, n_chunks, ln_g, ln_b, w_s, b_s):
    B, L, _ = p_u.shape
    u = jax.nn.gelu(p_u)
    v = layer_norm(jax.nn.gelu(p_v), ln_g, ln_b).reshape(B, n_chunks, SGU_CHUNK, SGU_GROUPS, SGU_GROUP_DIM)
    mixed = jnp.einsum('gpq,bnqgc->bnpgc', w_s, v) + b_s.T[:, :, None]
    return u * mixed.reshape(B, L, D_SGU)

def merge_branches(y_gdn, y_sgu, p_gates, w_a, w_b, w_o):
    g_a, g_b = jnp.split(jax.nn.sigmoid(p_gates), 2, axis=-1)
    return (g_a * (y_gdn @ w_a) + g_b * (y_sgu @ w_b)) @ w_o

def hier_moe(h, w_rg, b_rg, w_re, b_re, w1, w3, w2):
    B, L, D = h.shape
    t = h.reshape(B * L, D)
    p_group = jax.nn.softmax((t @ w_rg + b_rg).astype(jnp.float32), axis=-1)
    grp = jnp.argmax(p_group, axis=-1)
    p_g = jnp.take_along_axis(p_group, grp[:, None], axis=-1)
    logits_e = (t @ w_re + b_re).astype(jnp.float32).reshape(-1, N_EXPERT_GROUPS, EXPERTS_PER_GROUP)
    logits_in = jnp.take_along_axis(logits_e, grp[:, None, None], axis=1)[:, 0]
    top_p, top_i = lax.top_k(jax.nn.softmax(logits_in, axis=-1), TOP_K)
    top_p = top_p / jnp.sum(top_p, axis=-1, keepdims=True) * p_g
    expert_id = grp[:, None] * EXPERTS_PER_GROUP + top_i
    gate = jnp.sum(jax.nn.one_hot(expert_id, N_EXPERTS, dtype=jnp.float32) * top_p[..., None], axis=1)
    gate = gate.astype(h.dtype).reshape(-1, N_EXPERT_GROUPS, EXPERTS_PER_GROUP)
    out = jnp.zeros_like(t)
    for gi in range(N_EXPERT_GROUPS):
        sl = slice(gi * EXPERTS_PER_GROUP, (gi + 1) * EXPERTS_PER_GROUP)
        hid = jax.nn.silu(jnp.einsum('td,edf->tef', t, w1[sl])) * jnp.einsum('td,edf->tef', t, w3[sl])
        out = out + jnp.einsum('tef,efd->td', hid * gate[:, gi, :, None], w2[sl])
    return out.reshape(B, L, D)

def first_inputs(seed: int = 0) -> dict:
    key = jax.random.key(seed)
    ks = jax.random.split(key, 32)
    f32 = jnp.float32
    nrm = lambda k, shape, scale: jax.random.normal(k, shape, f32) * scale
    gain = lambda k, shape: 1.0 + 0.1 * jax.random.normal(k, shape, f32)
    dt = jnp.exp(jax.random.uniform(ks[9], (DEPTH, 2, N_HEADS), f32, math.log(1e-3), math.log(1e-1)))
    return {
        'x': nrm(ks[0], (BATCH, SEQ, D_MODEL), 1.0),
        'c': nrm(ks[1], (BATCH, D_MODEL), 1.0),
        'ctx': nrm(ks[2], (BATCH, CTX_LEN, D_MODEL), 1.0),
        'c_ctx': nrm(ks[3], (D_MODEL,), 1.0),
        'ada_w': nrm(ks[4], (DEPTH, D_MODEL, N_MOD * D_MODEL), 0.5 * D_MODEL ** -0.5),
        'ada_b': nrm(ks[5], (DEPTH, N_MOD * D_MODEL), 0.02),
        'norm_mix_g': gain(ks[6], (DEPTH, D_MODEL)),
        'w_in': nrm(ks[7], (DEPTH, D_MODEL, D_IN), D_MODEL ** -0.5),
        'conv_w': nrm(ks[8], (DEPTH, CONV_K, 3 * D_GDN), CONV_K ** -0.5),
        'a_log': jnp.log(jax.random.uniform(ks[10], (DEPTH, 2, N_HEADS), f32, 1.0, 16.0)),
        'dt_bias': dt + jnp.log(-jnp.expm1(-dt)),
        'gdn_norm_g': gain(ks[11], (DEPTH, HEAD_DIM)),
        'sgu_ln_g': gain(ks[12], (DEPTH, D_SGU)),
        'sgu_ln_b': nrm(ks[13], (DEPTH, D_SGU), 0.02),
        'sgu_w': nrm(ks[14], (DEPTH, SGU_GROUPS, SGU_CHUNK, SGU_CHUNK), SGU_CHUNK ** -0.5),
        'sgu_b': gain(ks[15], (DEPTH, SGU_GROUPS, SGU_CHUNK)),
        'w_branch_a': nrm(ks[16], (DEPTH, D_GDN, D_MODEL), D_GDN ** -0.5),
        'w_branch_b': nrm(ks[17], (DEPTH, D_SGU, D_MODEL), D_SGU ** -0.5),
        'w_out': nrm(ks[18], (DEPTH, D_MODEL, D_MODEL), D_MODEL ** -0.5),
        'norm_ffn_g': gain(ks[19], (DEPTH, D_MODEL)),
        'router_group_w': nrm(ks[20], (DEPTH, D_MODEL, N_EXPERT_GROUPS), D_MODEL ** -0.5),
        'router_group_b': nrm(ks[21], (DEPTH, N_EXPERT_GROUPS), 0.01),
        'router_expert_w': nrm(ks[22], (DEPTH, D_MODEL, N_EXPERTS), D_MODEL ** -0.5),
        'router_expert_b': nrm(ks[23], (DEPTH, N_EXPERTS), 0.01),
        'expert_w1': nrm(ks[24], (DEPTH, N_EXPERTS, D_MODEL, D_EXPERT), D_MODEL ** -0.5),
        'expert_w3': nrm(ks[25], (DEPTH, N_EXPERTS, D_MODEL, D_EXPERT), D_MODEL ** -0.5),
        'expert_w2': nrm(ks[26], (DEPTH, N_EXPERTS, D_EXPERT, D_MODEL), D_EXPERT ** -0.5),
        'final_norm_g': gain(ks[27], (D_MODEL,)),
    }

def first_block(x, c, ctx, c_ctx, ada_w, ada_b, norm_mix_g, w_in, conv_w, a_log, dt_bias, gdn_norm_g,
              sgu_ln_g, sgu_ln_b, sgu_w, sgu_b, w_branch_a, w_branch_b, w_out, norm_ffn_g,
              router_group_w, router_group_b, router_expert_w, router_expert_b,
              expert_w1, expert_w3, expert_w2, final_norm_g):
    B = x.shape[0]
    rows = x.shape[1] // GRID_W
    lat_chunks = rows // ROWS_PER_CHUNK
    ctx_chunks = ctx.shape[1] // SGU_CHUNK
    s_zero = jnp.zeros((2, B, N_HEADS, HEAD_DIM, HEAD_DIM), jnp.float32)
    for l in range(DEPTH):
        mod_x = adaln_params(c, ada_w[l], ada_b[l])
        mod_c = adaln_params(c_ctx[None, :], ada_w[l], ada_b[l])
        hc = modulate(rms_norm(ctx, norm_mix_g[l]), mod_c[:, 0], mod_c[:, 1])
        hx = modulate(rms_norm(x, norm_mix_g[l]), mod_x[:, 0], mod_x[:, 1])
        c_qkv, c_beta, c_a = jnp.split(hc @ w_in[l][:, :COL_Z], (COL_BETA, COL_A), axis=-1)
        o_c, s_ctx = gdn_scan(c_qkv, c_beta, c_a, conv_w[l], a_log[l], dt_bias[l], s_zero)
        x_qkv, x_beta, x_a, x_z, x_u, x_v, x_gates = jnp.split(
            hx @ w_in[l], (COL_BETA, COL_A, COL_Z, COL_U, COL_V, COL_GATE), axis=-1)
        o_x, _ = gdn_scan(x_qkv, x_beta, x_a, conv_w[l], a_log[l], dt_bias[l], s_ctx)
        y_gdn = gdn_output(o_x, x_z, gdn_norm_g[l])
        y_sgu = sgu_mixer(x_u, x_v, lat_chunks, sgu_ln_g[l], sgu_ln_b[l], sgu_w[l], sgu_b[l])
        x = x + mod_x[:, 2][:, None, :] * merge_branches(y_gdn, y_sgu, x_gates, w_branch_a[l], w_branch_b[l], w_out[l])
        hx = modulate(rms_norm(x, norm_ffn_g[l]), mod_x[:, 3], mod_x[:, 4])
        x = x + mod_x[:, 5][:, None, :] * hier_moe(hx, router_group_w[l], router_group_b[l], router_expert_w[l],
                                                   router_expert_b[l], expert_w1[l], expert_w3[l], expert_w2[l])
        if l < DEPTH - 1:
            c_z, c_u, c_v, c_gates = jnp.split(hc @ w_in[l][:, COL_Z:], (D_GDN, D_GDN + D_SGU, D_GDN + 2 * D_SGU), axis=-1)
            yc_gdn = gdn_output(o_c, c_z, gdn_norm_g[l])
            yc_sgu = sgu_mixer(c_u, c_v, ctx_chunks, sgu_ln_g[l], sgu_ln_b[l], sgu_w[l], sgu_b[l])
            ctx = ctx + mod_c[:, 2][:, None, :] * merge_branches(yc_gdn, yc_sgu, c_gates, w_branch_a[l], w_branch_b[l], w_out[l])
            hc = modulate(rms_norm(ctx, norm_ffn_g[l]), mod_c[:, 3], mod_c[:, 4])
            ctx = ctx + mod_c[:, 5][:, None, :] * hier_moe(hc, router_group_w[l], router_group_b[l], router_expert_w[l],
                                                           router_expert_b[l], expert_w1[l], expert_w3[l], expert_w2[l])
    return rms_norm(x, final_norm_g)


DEPTH_2 = 2

N_AB = (DEPTH_2 + 1) // 2
N_C = DEPTH_2 // 2
A_HEADS = 8
A_KV_HEADS = 2
A_HEAD_DIM = 64
A_WIDTH = A_HEADS * A_HEAD_DIM
A_KV_WIDTH = A_KV_HEADS * A_HEAD_DIM
WINDOW = 128
Q_BLOCK = WINDOW
ROPE_BASE = 10000.0
B_WIDTH = D_MODEL // 2
CONV_W = 3
AB_IN_WIDTH = 2 * A_WIDTH + 2 * A_KV_WIDTH + 4 * B_WIDTH
AB_OUT_WIDTH = A_WIDTH + B_WIDTH
C_HEADS = 8
C_KEY_DIM = 128
C_VAL_DIM = D_MODEL // C_HEADS
C_F_WIDTH = C_HEADS * C_KEY_DIM
C_I_WIDTH = C_HEADS * C_VAL_DIM
C_IN_WIDTH = 3 * C_F_WIDTH + 2 * C_I_WIDTH
CHUNK = 32
DEEPNORM_ALPHA = (2 * DEPTH_2) ** 0.25
DEEPNORM_BETA = (8 * DEPTH_2) ** -0.25
LN_EPS = 1e-5
RMS_EPS = 1e-6


def split_cols(p, widths):
    idx = [int(v) for v in np.cumsum(widths)[:-1]]
    return jnp.split(p, idx, axis=-1)

def layer_norm_2(x, g, b):
    xf = x.astype(jnp.float32)
    mu = xf.mean(-1, keepdims=True)
    var = jnp.square(xf - mu).mean(-1, keepdims=True)
    return ((xf - mu) * lax.rsqrt(var + LN_EPS) * g + b).astype(x.dtype)

def modulate_2(h, shift, scale):
    return h * (1 + scale) + shift

def rope_1d(x, pos):
    half = x.shape[-1] // 2
    freqs = ROPE_BASE ** (-jnp.arange(half, dtype=jnp.float32) / half)
    ang = pos.astype(jnp.float32)[:, None] * freqs[None, :]
    cos = jnp.cos(ang)[:, None, :].astype(x.dtype)
    sin = jnp.sin(ang)[:, None, :].astype(x.dtype)
    x1, x2 = x[..., :half], x[..., half:]
    return jnp.concatenate([x1 * cos - x2 * sin, x1 * sin + x2 * cos], axis=-1)

def axial_rope(x, row, col):
    half = x.shape[-1] // 2
    return jnp.concatenate([rope_1d(x[..., :half], row), rope_1d(x[..., half:], col)], axis=-1)

def heads(t, n_heads):
    return t.reshape(t.shape[0], t.shape[1], n_heads, A_HEAD_DIM)

def short_conv(u, w):
    pad = CONV_W // 2
    L = u.shape[1]
    up = jnp.pad(u, ((0, 0), (pad, pad), (0, 0)))
    y = up[:, 0:L] * w[0]
    for j in range(1, CONV_W):
        y = y + up[:, j:j + L] * w[j]
    return y

def window_attention(q, k, v, kc, vc, sink):
    B, L = q.shape[:2]
    n_blk = L // Q_BLOCK
    G = A_HEADS // A_KV_HEADS
    scale = A_HEAD_DIM ** -0.5
    lc = kc.shape[1]
    span = Q_BLOCK + 2 * WINDOW
    qb = q.reshape(B, n_blk, Q_BLOCK, A_KV_HEADS, G, A_HEAD_DIM).swapaxes(0, 1)
    kp = jnp.pad(k, ((0, 0), (WINDOW, WINDOW), (0, 0), (0, 0)))
    vp = jnp.pad(v, ((0, 0), (WINDOW, WINDOW), (0, 0), (0, 0)))
    rel = jnp.arange(span)[None, :] - WINDOW - jnp.arange(Q_BLOCK)[:, None]
    in_win = jnp.abs(rel) <= WINDOW
    sink_l = jnp.broadcast_to(sink.astype(jnp.float32).reshape(1, A_KV_HEADS, G, 1, 1),
                              (B, A_KV_HEADS, G, Q_BLOCK, 1))

    def one_block(args):
        n, q_n = args
        start = n * Q_BLOCK
        k_n = lax.dynamic_slice_in_dim(kp, start, span, axis=1)
        v_n = lax.dynamic_slice_in_dim(vp, start, span, axis=1)
        key_pos = start - WINDOW + jnp.arange(span)
        valid = in_win & ((key_pos >= 0) & (key_pos < L))[None, :]
        s_loc = jnp.einsum('bikgd,bjkd->bkgij', q_n, k_n).astype(jnp.float32) * scale
        s_loc = jnp.where(valid, s_loc, -jnp.inf)
        s_ctx = jnp.einsum('bikgd,bjkd->bkgij', q_n, kc).astype(jnp.float32) * scale
        p = jax.nn.softmax(jnp.concatenate([sink_l, s_ctx, s_loc], axis=-1), axis=-1).astype(v.dtype)
        return (jnp.einsum('bkgij,bjkd->bikgd', p[..., 1:1 + lc], vc)
                + jnp.einsum('bkgij,bjkd->bikgd', p[..., 1 + lc:], v_n))

    out = lax.map(one_block, (jnp.arange(n_blk), qb))
    return out.swapaxes(0, 1).reshape(B, L, A_WIDTH)

def context_attention(qc, kc, vc, sink):
    B, lc = qc.shape[:2]
    G = A_HEADS // A_KV_HEADS
    q = qc.reshape(B, lc, A_KV_HEADS, G, A_HEAD_DIM)
    s = jnp.einsum('bikgd,bjkd->bkgij', q, kc).astype(jnp.float32) * (A_HEAD_DIM ** -0.5)
    sink_l = jnp.broadcast_to(sink.astype(jnp.float32).reshape(1, A_KV_HEADS, G, 1, 1),
                              (B, A_KV_HEADS, G, lc, 1))
    p = jax.nn.softmax(jnp.concatenate([sink_l, s], axis=-1), axis=-1).astype(vc.dtype)
    return jnp.einsum('bkgij,bjkd->bikgd', p[..., 1:], vc).reshape(B, lc, A_WIDTH)

def ab_layer(x, xc, mod, mod_c, w_in, w_out, sink, conv_w, ln_g, ln_b, row, col, ctx_out):
    shift, scale, gate = jnp.split(mod, 3, axis=-1)
    shift_c, scale_c, gate_c = jnp.split(mod_c, 3, axis=-1)
    widths = (A_WIDTH, A_KV_WIDTH, A_KV_WIDTH, A_WIDTH, B_WIDTH, B_WIDTH, B_WIDTH, B_WIDTH)
    q, k, v, g_a, xb, b_g, c_g, g_b = split_cols(modulate_2(x, shift, scale) @ w_in, widths)
    hc = modulate_2(xc, shift_c, scale_c)
    if ctx_out:
        qc, kc, vc, g_ac, xbc, b_gc, c_gc, g_bc = split_cols(hc @ w_in, widths)
    else:
        kc, vc = split_cols(hc @ w_in[:, A_WIDTH:A_WIDTH + 2 * A_KV_WIDTH], (A_KV_WIDTH, A_KV_WIDTH))
    kc, vc = heads(kc, A_KV_HEADS), heads(vc, A_KV_HEADS)
    q = axial_rope(heads(q, A_HEADS), row, col)
    k = axial_rope(heads(k, A_KV_HEADS), row, col)
    o_a = window_attention(q, k, heads(v, A_KV_HEADS), kc, vc, sink)
    o_b = b_g * short_conv(c_g * xb, conv_w)
    y = jnp.concatenate([o_a * jax.nn.silu(g_a), o_b * jax.nn.silu(g_b)], axis=-1) @ w_out
    x_new = layer_norm_2(DEEPNORM_ALPHA * x + gate * y, ln_g, ln_b)
    if not ctx_out:
        return x_new, None
    o_ac = context_attention(heads(qc, A_HEADS), kc, vc, sink)
    o_bc = b_gc * short_conv(c_gc * xbc, conv_w)
    yc = jnp.concatenate([o_ac * jax.nn.silu(g_ac), o_bc * jax.nn.silu(g_bc)], axis=-1) @ w_out
    xc_new = layer_norm_2(DEEPNORM_ALPHA * xc + gate_c * yc, ln_g, ln_b)
    return x_new, xc_new

def to_heads(t, d):
    B, L, _ = t.shape
    return t.reshape(B, L, -1, d).transpose(0, 2, 1, 3).astype(jnp.float32)

def forget_terms(z, lb):
    lb = jnp.clip(lb.astype(jnp.float32), 0.0, 1.0).reshape(C_HEADS, 1, C_KEY_DIM)
    log_f = jnp.logaddexp(jnp.log(lb), jnp.log1p(-lb) + jax.nn.log_sigmoid(z))
    k = (1 - lb) * jax.nn.sigmoid(-z)
    return k, log_f

def hgrn2_scan(q, k, v, log_f, s0, with_outputs):
    B, H, L, dk = k.shape
    n = L // CHUNK
    chunks = lambda t: t.reshape(B, H, n, CHUNK, t.shape[-1])
    to_scan = lambda t: jnp.moveaxis(t, 2, 0)
    k, v, log_f = chunks(k), chunks(v), chunks(log_f)
    b = jnp.cumsum(log_f, axis=3)
    b_last = b[:, :, :, -1:, :]
    k_state = k * jnp.exp(b_last - b)
    decay = jnp.exp(b_last[:, :, :, 0, :])
    if with_outputs:
        q = chunks(q)
        q_inter = q * jnp.exp(b)
        tri = jnp.tril(jnp.ones((CHUNK, CHUNK), dtype=bool))[:, :, None]

        def step(s, xs):
            q_n, k_n, v_n, b_n, qi_n, ks_n, d_n = xs
            o_inter = jnp.einsum('bhcd,bhde->bhce', qi_n, s)
            diff = b_n[:, :, :, None, :] - b_n[:, :, None, :, :]
            w = jnp.exp(jnp.where(tri, diff, -jnp.inf))
            scores = jnp.einsum('bhcd,bhsd,bhcsd->bhcs', q_n, k_n, w)
            o_n = o_inter + jnp.einsum('bhcs,bhse->bhce', scores, v_n)
            return d_n[..., None] * s + jnp.einsum('bhcd,bhce->bhde', ks_n, v_n), o_n

        s_final, o = lax.scan(step, s0, (to_scan(q), to_scan(k), to_scan(v), to_scan(b),
                                         to_scan(q_inter), to_scan(k_state), to_scan(decay)))
        o = jnp.moveaxis(o, 0, 2).reshape(B, H, L, v.shape[-1])
        return o, s_final

    def step_state(s, xs):
        k_n, v_n, d_n = xs
        return d_n[..., None] * s + jnp.einsum('bhcd,bhce->bhde', k_n, v_n), None

    s_final, _ = lax.scan(step_state, s0, (to_scan(k_state), to_scan(v), to_scan(decay)))
    return None, s_final

def hgrn2_direction(q, i, z, lb, qc, ic, zc, ctx_out, reverse):
    flip = (lambda t: jnp.flip(t, axis=2)) if reverse else (lambda t: t)
    B = i.shape[0]
    kc, lfc = forget_terms(zc, lb)
    s0 = jnp.zeros((B, C_HEADS, C_KEY_DIM, C_VAL_DIM), jnp.float32)
    oc, s_ctx = hgrn2_scan(flip(qc) if ctx_out else None, flip(kc), flip(ic), flip(lfc), s0, ctx_out)
    k, lf = forget_terms(z, lb)
    o, _ = hgrn2_scan(flip(q), flip(k), flip(i), flip(lf), s_ctx, True)
    return flip(o), (flip(oc) if ctx_out else None)

def hgrn2_readout(o, g, g_norm, w_out):
    on = o * lax.rsqrt(jnp.mean(o * o, axis=-1, keepdims=True) + RMS_EPS) * g_norm
    B, H, L, dv = on.shape
    return (on.transpose(0, 2, 1, 3).reshape(B, L, H * dv).astype(g.dtype) * jax.nn.silu(g)) @ w_out

def c_layer(x, xc, mod, mod_c, w_in, w_out, lb_f, lb_b, g_norm, ln_g, ln_b, ctx_out):
    shift, scale, gate = jnp.split(mod, 3, axis=-1)
    shift_c, scale_c, gate_c = jnp.split(mod_c, 3, axis=-1)
    widths = (C_F_WIDTH, C_F_WIDTH, C_F_WIDTH, C_I_WIDTH, C_I_WIDTH)
    q, zf, zb, i, g = split_cols(modulate_2(x, shift, scale) @ w_in, widths)
    hc = modulate_2(xc, shift_c, scale_c)
    if ctx_out:
        qc, zfc, zbc, ic, gc = split_cols(hc @ w_in, widths)
        qc = jax.nn.silu(to_heads(qc, C_KEY_DIM)) * (C_KEY_DIM ** -0.5)
    else:
        zfc, zbc, ic = split_cols(hc @ w_in[:, C_F_WIDTH:3 * C_F_WIDTH + C_I_WIDTH],
                                  (C_F_WIDTH, C_F_WIDTH, C_I_WIDTH))
        qc = None
    q = jax.nn.silu(to_heads(q, C_KEY_DIM)) * (C_KEY_DIM ** -0.5)
    i, zf, zb = to_heads(i, C_VAL_DIM), to_heads(zf, C_KEY_DIM), to_heads(zb, C_KEY_DIM)
    ic, zfc, zbc = to_heads(ic, C_VAL_DIM), to_heads(zfc, C_KEY_DIM), to_heads(zbc, C_KEY_DIM)
    o_f, oc_f = hgrn2_direction(q, i, zf, lb_f, qc, ic, zfc, ctx_out, reverse=False)
    o_b, oc_b = hgrn2_direction(q, i, zb, lb_b, qc, ic, zbc, ctx_out, reverse=True)
    y = hgrn2_readout(o_f + o_b, g, g_norm, w_out)
    x_new = layer_norm_2(DEEPNORM_ALPHA * x + gate * y, ln_g, ln_b)
    if not ctx_out:
        return x_new, None
    yc = hgrn2_readout(oc_f + oc_b, gc, g_norm, w_out)
    xc_new = layer_norm_2(DEEPNORM_ALPHA * xc + gate_c * yc, ln_g, ln_b)
    return x_new, xc_new

def second_inputs(seed: int = 0) -> dict:
    key = jax.random.key(seed)
    ks = jax.random.split(key, 16)
    nrm = lambda k, shape, s: jax.random.normal(k, shape, jnp.float32) * s
    ab_col_scale = jnp.concatenate([
        jnp.ones((A_WIDTH + A_KV_WIDTH,), jnp.float32),
        jnp.full((A_KV_WIDTH,), DEEPNORM_BETA, jnp.float32),
        jnp.ones((A_WIDTH + 4 * B_WIDTH,), jnp.float32)])
    c_col_scale = jnp.concatenate([
        jnp.ones((3 * C_F_WIDTH,), jnp.float32),
        jnp.full((C_I_WIDTH,), DEEPNORM_BETA, jnp.float32),
        jnp.ones((C_I_WIDTH,), jnp.float32)])
    return {
        "x": nrm(ks[0], (BATCH, SEQ, D_MODEL), 1.0),
        "c": nrm(ks[1], (BATCH, D_MODEL), 1.0),
        "ctx": nrm(ks[2], (BATCH, CTX_LEN, D_MODEL), 1.0),
        "c_ctx": nrm(ks[3], (D_MODEL,), 1.0),
        "w_ada": nrm(ks[4], (DEPTH_2, D_MODEL, 3 * D_MODEL), D_MODEL ** -0.5),
        "b_ada": nrm(ks[5], (DEPTH_2, 3 * D_MODEL), 0.02),
        "ln_g": 1.0 + nrm(ks[6], (DEPTH_2, D_MODEL), 0.02),
        "ln_b": nrm(ks[7], (DEPTH_2, D_MODEL), 0.02),
        "w_in_ab": nrm(ks[8], (N_AB, D_MODEL, AB_IN_WIDTH), D_MODEL ** -0.5) * ab_col_scale,
        "w_out_ab": nrm(ks[9], (N_AB, AB_OUT_WIDTH, D_MODEL), AB_OUT_WIDTH ** -0.5 * DEEPNORM_BETA),
        "sink_ab": nrm(ks[10], (N_AB, A_HEADS), 0.5),
        "conv_ab": nrm(ks[11], (N_AB, CONV_W, B_WIDTH), CONV_W ** -0.5),
        "w_in_c": nrm(ks[12], (N_C, D_MODEL, C_IN_WIDTH), D_MODEL ** -0.5) * c_col_scale,
        "w_out_c": nrm(ks[13], (N_C, C_I_WIDTH, D_MODEL), C_I_WIDTH ** -0.5 * DEEPNORM_BETA),
        "lb_c": nrm(ks[14], (2, N_C, C_F_WIDTH), 0.5),
        "gnorm_c": 1.0 + nrm(ks[15], (N_C, C_VAL_DIM), 0.02),
    }

def second_block(x, c, ctx, c_ctx, w_ada, b_ada, ln_g, ln_b, w_in_ab, w_out_ab, sink_ab, conv_ab,
              w_in_c, w_out_c, lb_c, gnorm_c):
    L = x.shape[1]
    rows = L // GRID_W
    row = jnp.repeat(jnp.arange(rows), GRID_W)
    col = jnp.tile(jnp.arange(GRID_W), rows)
    lb_p = jax.nn.softmax(lb_c.astype(jnp.float32), axis=1)
    lb_all = jnp.cumsum(lb_p, axis=1) - lb_p[:, :1]
    silu_c = jax.nn.silu(c)
    silu_cc = jax.nn.silu(c_ctx)
    xc = ctx
    for l in range(DEPTH_2):
        mod = (silu_c @ w_ada[l] + b_ada[l])[:, None, :]
        mod_c = silu_cc @ w_ada[l] + b_ada[l]
        ctx_out = l < DEPTH_2 - 1
        j = l // 2
        if l % 2 == 0:
            x, xc = ab_layer(x, xc, mod, mod_c, w_in_ab[j], w_out_ab[j], sink_ab[j], conv_ab[j],
                             ln_g[l], ln_b[l], row, col, ctx_out)
        else:
            x, xc = c_layer(x, xc, mod, mod_c, w_in_c[j], w_out_c[j], lb_all[0, j], lb_all[1, j],
                            gnorm_c[j], ln_g[l], ln_b[l], ctx_out)
    return x


def setup_inputs(seed=0):
    out = dict(first_inputs(seed))
    for name, value in second_inputs(seed + 1).items():
        if name != "x":
            out[name + "_2"] = value
    return out


def reference(
    x, c, ctx, c_ctx, ada_w, ada_b, norm_mix_g, w_in, conv_w, a_log, dt_bias, gdn_norm_g,
    sgu_ln_g, sgu_ln_b, sgu_w, sgu_b, w_branch_a, w_branch_b, w_out, norm_ffn_g, router_group_w,
    router_group_b, router_expert_w, router_expert_b, expert_w1, expert_w3, expert_w2,
    final_norm_g, c_2, ctx_2, c_ctx_2, w_ada_2, b_ada_2, ln_g_2, ln_b_2, w_in_ab_2, w_out_ab_2,
    sink_ab_2, conv_ab_2, w_in_c_2, w_out_c_2, lb_c_2, gnorm_c_2,
):
    x = first_block(
        x, c, ctx, c_ctx, ada_w, ada_b, norm_mix_g, w_in, conv_w, a_log, dt_bias, gdn_norm_g,
        sgu_ln_g, sgu_ln_b, sgu_w, sgu_b, w_branch_a, w_branch_b, w_out, norm_ffn_g,
        router_group_w, router_group_b, router_expert_w, router_expert_b, expert_w1, expert_w3,
        expert_w2, final_norm_g,
    )
    return second_block(
        x, c_2, ctx_2, c_ctx_2, w_ada_2, b_ada_2, ln_g_2, ln_b_2, w_in_ab_2, w_out_ab_2,
        sink_ab_2, conv_ab_2, w_in_c_2, w_out_c_2, lb_c_2, gnorm_c_2,
    )


_drawn_inputs = setup_inputs


def setup_inputs(seed=0):
    import zlib

    import numpy as np

    out = dict(_drawn_inputs(seed))
    spreads = {}
    factors = {'ctx': 3.47,
     'c_ctx': 4.837,
     'gdn_norm_g': 3.363,
     'sgu_ln_g': 3.5,
     'sgu_ln_b': 8.0,
     'sgu_b': 3.494,
     'router_group_b': 45.946,
     'router_expert_b': 16.329,
     'ctx_2': 6.731,
     'b_ada_2': 3.404,
     'sink_ab_2': 64.0,
     'gnorm_c_2': 142.631}
    for name, (base, spread) in spreads.items():
        noise = np.random.default_rng([zlib.crc32(name.encode()), seed]).standard_normal(out[name].shape)
        drawn = base * np.exp(spread * noise) if base else spread * noise
        out[name] = __import__('jax').numpy.asarray(drawn.astype(out[name].dtype))
    for name, factor in factors.items():
        out[name] = (out[name] * factor).astype(out[name].dtype)
    return out
```

```python
import math
from contextlib import ExitStack

import numpy as np
import concourse.bass as bass
import concourse.mybir as mybir

F32 = mybir.dt.float32
I32 = mybir.dt.int32
ALU = mybir.AluOpType
ACT = mybir.ActivationFunctionType
AX = mybir.AxisListType

P = 128
D = 1024
KT = D // P
L = 256
TT = L // P
H = 8
PANEL = 512
HALF = PANEL // 2
RING = 3
CONV_K = 5
N_QKV = 3 * D
COL_BA = N_QKV
COL_Z = COL_BA + 4 * H
EPS = 1e-6
LN_EPS = 1e-5
LEVELS = 7
GROUPS = 4
PER_GROUP = 8
N_EXPERTS = GROUPS * PER_GROUP
D_EXPERT = 256
ROUTER = GROUPS + N_EXPERTS
A_HEADS, A_DIM = 8, 64
KV_HEADS = 2
WINDOW = 128
GRID_W = 64
ROPE_BASE = 10000.0
DEEPNORM_ALPHA = 4.0 ** 0.25
MASKED = -1e30


def shape_constants():
    parts, at = {}, 0
    cols = []

    def put(name, a):
        nonlocal at
        a = np.asarray(a, np.float32).reshape(P, -1)
        parts[name] = (at, a.shape[1])
        cols.append(a)
        at += a.shape[1]

    i = np.arange(P)
    put("ident", np.eye(P))
    put("ones", np.ones((P, P)))
    put("tri", np.stack([i[:, None] <= i[None, :], i[:, None] >= i[None, :]], 1))
    lev = np.zeros((P, 2, LEVELS, P // 2))
    for lv in range(LEVELS):
        b = 1 << lv
        blk = np.arange(P // 2) // b
        low, high = blk * 2 * b, blk * 2 * b + b
        lev[:, 0, lv] = (i[:, None] >= high) & (i[:, None] < high + b)
        lev[:, 1, lv] = (i[:, None] >= low) & (i[:, None] < high)
    put("lev", lev)
    small = at
    tok = np.arange(L)
    half = A_DIM // 4
    freq = np.power(np.float32(ROPE_BASE), -np.arange(half, dtype=np.float32) / np.float32(half)).astype(np.float32)
    d = i % A_DIM
    pos = np.where((d < A_DIM // 2)[:, None], (tok // GRID_W)[None], (tok % GRID_W)[None]).astype(np.float32)
    ang = pos * freq[d % half][:, None]
    put("cos", np.cos(ang))
    put("sin", np.sin(ang))
    rot = np.zeros((P, P))
    first = (d % (2 * half)) < half
    rot[(i + half)[first], i[first]] = -1
    rot[(i - half)[~first], i[~first]] = 1
    put("rot", rot)
    q, k = tok[:, None], tok[None, :]
    win = np.where(np.abs(q - k) <= WINDOW, 0.0, MASKED)
    put("kdup", np.stack([i[:, None] == g * A_DIM + i[None, :] % A_DIM for g in range(KV_HEADS)], 1))
    put("win", np.concatenate([np.zeros((L, L)), win], 1).reshape(TT, P, 2 * L).transpose(1, 0, 2))
    return np.concatenate(cols, 1), parts, small


def row_bcast(ap, n=P):
    return ap.unsqueeze(0).to_broadcast([n, ap.shape[0]])


def half_cols(ap, lv, side):
    b = 1 << lv
    if len(ap.shape) == 2:
        return ap.rearrange("p (n s j) -> p n s j", s=2, j=b)[:, :, side, :]
    return ap.rearrange("p u (n s j) -> p u n s j", s=2, j=b)[:, :, :, side, :]


def packed_cols(ap, lv):
    b = 1 << lv
    if len(ap.shape) == 2:
        return ap.rearrange("p (n j) -> p n j", j=b)
    return ap.rearrange("p u (n j) -> p u n j", j=b)


class Stream:

    def __init__(self, ring, loaded, used):
        self.ring, self.loaded, self.used = ring, loaded, used
        self.panels = []
        self.issued = 0
        self.taken = 0

    def slot(self, n):
        return self.ring[:, n % RING]

    def issue(self, sp, upto):
        while self.issued < min(upto, len(self.panels)):
            n = self.issued
            if n >= RING:
                sp.wait_ge(self.used, n - RING + 1)
            self.load(sp, n)
            self.issued += 1

    def load(self, sp, n):
        for src, dst in self.panels[n](self.slot(n)):
            sp.dma_start(dst, src).then_inc(self.loaded[n % RING], 16)

    def arrive(self, n):
        parts = sum(len(self.panels[m](self.slot(m))) for m in range(n % RING, n + 1, RING))
        return self.loaded[n % RING], 16 * parts


def build(nc, w, out, const_dram):
    _, parts, small = shape_constants()
    with ExitStack() as whole:
        def sem(name):
            return whole.enter_context(nc.semaphore(name))

        def sb(scope, name, shape, dt=F32):
            return scope.enter_context(nc.sbuf_tensor(name, shape, dt))

        def stage_sems(scope, prefix):
            held = []

            def clear():
                nc.clear_and_free_semaphores(held)
                nc.all_engine_barrier(sem_only=True)

            scope.callback(clear)

            def make(what):
                held.append(nc.alloc_semaphore(prefix + what))
                return held[-1]

            return make

        ps = whole.enter_context(nc.psum_tensor("ps", [P, 8, 512], F32))
        ring = sb(whole, "ring", [P, RING, KT, PANEL])
        consts = sb(whole, "consts", [P, small])

        def const(name):
            at, n = parts[name]
            return consts[:, at:at + n]

        ident, ones = const("ident"), const("ones")
        tri = const("tri").rearrange("p (d t) -> p d t", d=2)
        lev = const("lev").rearrange("p (d l c) -> p d l c", d=2, l=LEVELS)
        xs = sb(whole, "xs", [P, TT, D])
        stat = sb(whole, "stat", [P, 16])

        stream = Stream(ring, [sem(f"panel_loaded{i}") for i in range(RING)], sem("panel_used"))
        add = stream.panels.append

        def add_cols(src, cols, width=PANEL):
            add(lambda slot: [(src[:, :, cols:cols + width], slot[:, :, 0:width])])

        ktp = lambda a: a.rearrange("(kt p) n -> p kt n", p=P)
        pkt = lambda a: a.rearrange("(p kt) n -> p kt n", kt=KT)
        w_in, ada = ktp(w["w_in"][0]), pkt(w["ada_w"][0])
        ADA_MIX = 0
        for i in range(4):
            add_cols(ada, i * PANEL)
        QKV = len(stream.panels)
        for i in range(N_QKV // PANEL):
            add_cols(w_in, i * PANEL)
        ZUVG = len(stream.panels)
        for i in range(10):
            add_cols(w_in, COL_Z + i * PANEL)
        ADA_REST = len(stream.panels)
        for i in range(4, 12):
            add_cols(ada, i * PANEL)
        MERGE = len(stream.panels)
        for name in ("w_branch_a", "w_branch_b", "w_out"):
            for i in range(2):
                add_cols(ktp(w[name][0]), i * PANEL)
        MOE = len(stream.panels)
        w1 = w["expert_w1"][0].rearrange("e (kt p) f -> e p kt f", p=P)
        w3 = w["expert_w3"][0].rearrange("e (kt p) f -> e p kt f", p=P)
        w2 = w["expert_w2"][0].rearrange("e (ft p) n -> e p ft n", p=P)

        def add_up(e):
            add(lambda slot: [(w1[e], slot[:, :, 0:D_EXPERT]), (w3[e], slot[:, :, D_EXPERT:])])

        def add_down(e):
            view = lambda slot: slot.rearrange("p (e f c) n -> p e f (c n)", e=2, f=2)
            add(lambda slot: [(w2[e + j], view(slot)[:, j]) for j in range(2)])

        for e in range(0, N_EXPERTS, 2):
            add_up(e)
            add_up(e + 1)
            add_down(e)
        ADA2 = len(stream.panels)
        for layer in range(2):
            for i in range(6):
                add_cols(pkt(w["w_ada_2"][layer]), i * PANEL)
        AB_IN = len(stream.panels)
        for i in range(6):
            add_cols(ktp(w["w_in_ab_2"][0]), i * PANEL)
        add_cols(ktp(w["w_in_ab_2"][0]), 6 * PANEL, HALF)
        AB_OUT = len(stream.panels)
        for i in range(2):
            add_cols(ktp(w["w_out_ab_2"][0]), i * PANEL)
        C_IN = len(stream.panels)
        for i in range(10):
            add_cols(ktp(w["w_in_c_2"][0]), i * PANEL)
        C_OUT = len(stream.panels)
        for i in range(2):
            add_cols(ktp(w["w_out_c_2"][0]), i * PANEL)
        END = len(stream.panels)


        def chained(eng, done):
            count = [0]

            def link(ins):
                count[0] += 1
                ins.then_inc(done, 1)
                eng.wait_ge(done, count[0])

            return link

        def ada_dot(eng, n, acc, cvec, done, count):
            slot = stream.slot(n)
            for kt in range(KT):
                if kt == 0:
                    ins = eng.tensor_scalar(acc, slot[:, 0], cvec[:, 0:1], None, ALU.mult)
                else:
                    eng.wait_ge(done, count + kt)
                    ins = eng.scalar_tensor_tensor(out=acc, in0=slot[:, kt], scalar=cvec[:, kt:kt + 1],
                                                   in1=acc, op0=ALU.mult, op1=ALU.add)
                ins.then_inc(done, 1)

        def ada_block(name, first, n_panels, cx, cc, dest_x, dest_c, loads, n_loads, upto, scope, prepare=None):
            acc = sb(scope, f"{name}_acc", [P, 2, PANEL])
            sem = stage_sems(scope, name + "_")
            dot_x, mod_done, summed = sem("dot_x"), sem("mod_done"), sem("summed")
            loaded, c_ready = sem("loaded"), sem("c_ready")
            has_c = [i for i in range(n_panels) if dest_c(i) is not None]
            dests = [[d for d in (dest_x(i), dest_c(i)) if d is not None] for i in range(n_panels)]
            evacs = [sum(len(d) for d in dests[:i + 1]) for i in range(n_panels)]
            with nc.Block() as block:
                @block.sync
                def _(sp):
                    loads(sp, loaded)
                    stream.issue(sp, upto)

                @block.scalar
                def _(act):
                    if prepare:
                        act.wait_ge(loaded, 16 * n_loads)
                        prepare(act).then_inc(c_ready, 1)

                @block.vector
                def _(dve):
                    if prepare:
                        dve.wait_ge(c_ready, 1)
                    dve.wait_ge(loaded, 16 * n_loads)

                    def finish(i):
                        dve.wait_ge(summed, evacs[i])
                        for j, d in enumerate(dests[i]):
                            dve.tensor_tensor(d, ps[:, 2 * j + i % 2], d, ALU.add).then_inc(mod_done, 1)

                    for i in range(n_panels):
                        dve.wait_ge(*stream.arrive(first + i))
                        if i >= 2:
                            dve.wait_ge(summed, evacs[i - 2])
                        ada_dot(dve, first + i, acc[:, i % 2], cx, dot_x, KT * i)
                        if i >= 1:
                            finish(i - 1)
                    finish(n_panels - 1)

                @block.tensor
                def _(pe):
                    if prepare:
                        pe.wait_ge(c_ready, 1)
                    for i in range(n_panels):
                        if i >= 2:
                            pe.wait_ge(mod_done, evacs[i - 2])
                        if i in has_c:
                            pe.wait_ge(*stream.arrive(first + i))
                            for kt in range(KT):
                                ins = pe.matmul(ps[:, 2 + i % 2], cc[:, kt:kt + 1].to_broadcast([P, P]), stream.slot(first + i)[:, kt],
                                                start=(kt == 0), stop=(kt == KT - 1))
                            ins.then_inc(summed, 1)
                        pe.wait_ge(dot_x, KT * (i + 1))
                        pe.matmul(ps[:, i % 2], ones, acc[:, i % 2], start=True, stop=True).then_inc(summed, 1)
                        pe.drain().then_inc(stream.used, 1)

        def transpose_in(pe, bank, src, n, name=None):
            for i in range(n):
                ins = pe.transpose(ps[:, bank, i * P:(i + 1) * P], src(i), ident)
            return ins

        def norm_modulate(eng, done, base, x, rstd, gm, shift, tmp, out_t):
            eng.scalar_tensor_tensor(out=tmp, in0=x, scalar=rstd, in1=gm, op0=ALU.mult, op1=ALU.mult).then_inc(done, 1)
            eng.wait_ge(done, base + 1)
            return eng.tensor_tensor(out_t, tmp, shift, ALU.add)

        eps = sb(whole, "eps", [P, 2])
        cact = sb(whole, "cact", [P, 4, KT])
        with ExitStack() as first:
            hTx = sb(first, "hTx", [P, KT, L])
            otok = sb(first, "otok", [P, TT, D])

            qkv = first.enter_context(ExitStack())
            kT = sb(qkv, "kT", [P, H, 2 * L])
            qT = sb(qkv, "qT", [P, H, L])
            beta = sb(qkv, "beta", [P, 2 * TT, 2 * H])
            glog = sb(qkv, "glog", [P, 2 * TT, 2 * H])
            ktok = sb(qkv, "ktok", [P, 2 * TT, D])
            vtok = sb(qkv, "vtok", [P, 2 * TT, D])
            proj_in = qkv.enter_context(ExitStack())
            hTc = sb(proj_in, "hTc", [P, KT, L])

            with ExitStack() as scope:
                mix = sb(scope, "mix", [P, 2, 2, D])
                cs = sb(scope, "cs", [P, TT, D])
                gmix = sb(scope, "gmix", [P, D])
                craw = sb(scope, "craw", [P, 4, KT])

                def loads(sp, loaded):
                    for i, n in enumerate(("c", "c_ctx", "c_2", "c_ctx_2")):
                        src = w[n] if len(w[n].shape) == 1 else w[n][0]
                        sp.dma_start(craw[:, i], src.rearrange("(p kt) -> p kt", kt=KT)).then_inc(loaded, 16)
                    for j in range(2):
                        for r in range(2):
                            sp.dma_start(mix[:, j, r], row_bcast(w["ada_b"][0, r * D:(r + 1) * D])).then_inc(loaded, 16)
                    sp.dma_start(consts[:, :], const_dram[:, 0:small]).then_inc(loaded, 16)
                    sp.dma_start(xs[:, :, :], w["x"][0].rearrange("(t p) d -> p t d", p=P)).then_inc(loaded, 16)
                    sp.dma_start(cs[:, :, :], w["ctx"][0].rearrange("(t p) d -> p t d", p=P)).then_inc(loaded, 16)
                    sp.dma_start(gmix[:, :], row_bcast(w["norm_mix_g"][0])).then_inc(loaded, 16)

                with ExitStack() as inner:
                    ada_block("ada_mix", ADA_MIX, 4, cact[:, 0], cact[:, 1],
                              lambda i: mix[:, 0, i // 2, (i % 2) * PANEL:(i % 2 + 1) * PANEL],
                              lambda i: mix[:, 1, i // 2, (i % 2) * PANEL:(i % 2 + 1) * PANEL],
                              loads, 12, 4 + RING, inner,
                              lambda act: act.activation(cact[:, :, :], craw[:, :, :], ACT.Silu))

                gm = sb(scope, "gm", [P, 2, D])
                tmp = sb(scope, "tmp", [P, 2, D])
                ssem = stage_sems(scope, "norm_")
                squares, std, rstd_done = ssem("squares"), ssem("std"), ssem("rstd")
                gm_done, x_steps, c_steps = ssem("gm"), ssem("x_steps"), ssem("c_steps")
                turned, moved_a, moved_v = ssem("turned"), ssem("moved_a"), ssem("moved_v")
                seqs = (xs, cs)
                with nc.Block() as block:
                    @block.scalar
                    def _(act):
                        for j in range(2):
                            for t in range(TT):
                                act.activation(hTx[:, 4 * (t % 2):4 * (t % 2) + 4].rearrange("p a b -> p (a b)"), seqs[j][:, t],
                                               ACT.Square, accum_out=stat[:, 2 * j + t:2 * j + t + 1]).then_inc(squares, 1)
                                act.wait_ge(squares, 2 * j + t + 1)
                        act.wait_ge(rstd_done, 1)
                        act.activation(stat[:, 4:8], stat[:, 4:8], ACT.Sqrt).then_inc(std, 1)
                        for kt in range(0, KT, 2):
                            act.wait_ge(turned, kt + 1)
                            act.copy(hTx[:, kt], ps[:, kt, L:2 * L])
                            act.copy(hTc[:, kt], ps[:, kt, 0:L]).then_inc(moved_a, 1)

                    @block.vector
                    def _(dve):
                        dve.wait_ge(squares, 4)
                        dve.tensor_scalar(stat[:, 4:8], stat[:, 0:4], 1.0 / D, EPS, ALU.mult, ALU.add).then_inc(rstd_done, 1)
                        for j in range(2):
                            dve.scalar_tensor_tensor(out=gm[:, j], in0=mix[:, j, 1], scalar=1.0, in1=gmix[:, :],
                                                     op0=ALU.add, op1=ALU.mult).then_inc(gm_done, 1)
                        dve.wait_ge(std, 1)
                        dve.reciprocal(stat[:, 8:12], stat[:, 4:8]).then_inc(rstd_done, 1)
                        dve.wait_ge(rstd_done, 2)
                        dve.wait_ge(gm_done, 2)
                        for t in range(TT):
                            norm_modulate(dve, x_steps, 2 * t, xs[:, t], stat[:, 8 + t:9 + t], gm[:, 0], mix[:, 0, 0],
                                          tmp[:, t], tmp[:, t]).then_inc(x_steps, 1)
                        for kt in range(1, KT, 2):
                            dve.wait_ge(turned, kt + 1)
                            dve.tensor_copy(hTx[:, kt], ps[:, kt, L:2 * L])
                            dve.tensor_copy(hTc[:, kt], ps[:, kt, 0:L]).then_inc(moved_v, 1)

                    @block.gpsimd
                    def _(pool):
                        pool.memset(eps[:, 0:1], EPS)
                        pool.memset(eps[:, 1:2], LN_EPS)
                        pool.wait_ge(rstd_done, 2)
                        pool.wait_ge(gm_done, 2)
                        link = chained(pool, c_steps)
                        for t in range(TT):
                            link(pool.tensor_scalar(cs[:, t], cs[:, t], stat[:, 10 + t:11 + t], None, ALU.mult))
                            link(pool.tensor_tensor(cs[:, t], cs[:, t], gm[:, 1], ALU.mult))
                            link(pool.tensor_tensor(cs[:, t], cs[:, t], mix[:, 1, 0], ALU.add))

                    @block.tensor
                    def _(pe):
                        pe.wait_ge(x_steps, 2 * TT)
                        pe.wait_ge(c_steps, 3 * TT)
                        for kt in range(KT):
                            cols = slice(kt * P, kt * P + P)
                            transpose_in(pe, kt, lambda i: (cs, tmp)[i // TT][:, i % TT, cols], 2 * TT).then_inc(turned, 1)

            with ExitStack() as scope:
                vT = sb(scope, "vT", [P, H, 2 * L])
                wba = sb(scope, "wba", [P, KT, 4 * H])
                taps_row = sb(scope, "taps_row", [CONV_K, N_QKV])
                taps = sb(scope, "taps", [P, 24, CONV_K])
                xpad = sb(scope, "xpad", [P, 3, 2, L + CONV_K - 1])
                conv = sb(scope, "conv", [P, 3, 2, L])
                rows = sb(scope, "rows", [P, 2, 2 * H])
                sp1 = sb(scope, "sp1", [P, 3, 2 * TT, 2 * H])
                norm = sb(scope, "norm", [P, 2, 2 * L])
                sq = sb(scope, "sq", [P, 2, 2 * L])
                ssem = stage_sems(scope, "qkv_")
                loaded, proj, padded, conved, silued = ssem("loaded"), ssem("proj"), ssem("padded"), ssem("conved"), ssem("silued")
                pad_zero, taps_t, taps_done = ssem("pad_zero"), ssem("taps_t"), ssem("taps_done")
                ba_done, ba_chain, ba_act, ba_pool = ssem("ba_done"), ssem("ba_chain"), ssem("ba_act"), ssem("ba_pool")
                squared, sums, rooted, inverted, normed = ssem("squared"), ssem("sums"), ssem("rooted"), ssem("inverted"), ssem("normed")
                turned, moved_a, moved_v = ssem("turned"), ssem("moved_a"), ssem("moved_v")
                conv_step = ssem("conv_step")
                N_TILES = 24
                BANKS = 4

                def dest(j):
                    return qT[:, j, :] if j < H else (kT[:, j - H, :] if j < 2 * H else vT[:, j - 2 * H, :])

                def seq(j):
                    return slice(1, 2) if j < H else slice(0, 2)

                with nc.Block() as block:
                    @block.sync
                    def _(sp):
                        sp.dma_start(taps_row[:, :], w["conv_w"][0]).then_inc(loaded, 16)
                        sp.dma_start(wba[:, :, :], w_in[:, :, COL_BA:COL_Z]).then_inc(loaded, 16)
                        sp.dma_start(rows[:, 0], row_bcast(w["a_log"][0].rearrange("a b -> (a b)"))).then_inc(loaded, 16)
                        sp.dma_start(rows[:, 1], row_bcast(w["dt_bias"][0].rearrange("a b -> (a b)"))).then_inc(loaded, 16)
                        stream.issue(sp, ZUVG + RING)

                    @block.gpsimd
                    def _(pool):
                        pool.memset(xpad[:, :, :, :], 0.0).then_inc(pad_zero, 1)

                    @block.tensor
                    def _(pe):
                        pe.wait_ge(loaded, 64)
                        for j in range(N_TILES):
                            ins = pe.transpose(ps[:, 7, CONV_K * j:CONV_K * (j + 1)], taps_row[:, j * P:(j + 1) * P],
                                               ident[0:CONV_K, 0:CONV_K])
                        ins.then_inc(taps_t, 1)
                        for t in range(2 * TT):
                            lhs = (hTc, hTx)[t // TT]
                            for kt in range(KT):
                                ins = pe.matmul(ps[:, 6, 4 * H * t:4 * H * (t + 1)], lhs[:, kt, (t % TT) * P:(t % TT + 1) * P],
                                                wba[:, kt], start=(kt == 0), stop=(kt == KT - 1))
                        ins.then_inc(ba_done, 1)
                        for j in range(N_TILES):
                            n = QKV + j // 4
                            if j % 4 == 0:
                                pe.wait_ge(*stream.arrive(n))
                            if j >= BANKS:
                                pe.wait_ge(padded, j - BANKS + 1)
                            slot = stream.slot(n)
                            for s in range(2)[seq(j)]:
                                for kt in range(KT):
                                    ins = pe.matmul(ps[:, j % BANKS, s * L:(s + 1) * L], slot[:, kt, (j % 4) * P:(j % 4 + 1) * P],
                                                    (hTc, hTx)[s][:, kt], start=(kt == 0), stop=(kt == KT - 1))
                            ins.then_inc(proj, 1)
                            if j % 4 == 3:
                                pe.drain().then_inc(stream.used, 1)

                    @block.scalar
                    def _(act):
                        act.wait_ge(loaded, 64)
                        act.wait_ge(ba_chain, 1)
                        ba = ps[:, 6, 0:2 * TT * 4 * H].rearrange("p (t c) -> p t c", t=2 * TT)
                        act.activation(beta[:, :, :], ba[:, :, 0:2 * H], ACT.Sigmoid)
                        act.wait_ge(pad_zero, 1)

                        def pad(j):
                            act.wait_ge(proj, j + 1)
                            if j >= 3:
                                act.wait_ge(conved, j - 2)
                            act.copy(xpad[:, j % 3, seq(j), 2:2 + L],
                                     ps[:, j % BANKS].rearrange("p (s t) -> p s t", s=2)[:, seq(j)]).then_inc(padded, 1)

                        def silu(j):
                            act.wait_ge(conved, j + 1)
                            out_t = dest(j) if j < H else dest(j).rearrange("p (s t) -> p s t", s=2)
                            act.activation(out_t, conv[:, j % 3, 1] if j < H else conv[:, j % 3], ACT.Silu).then_inc(silued, 1)

                        for j in range(N_TILES + 1):
                            if j < N_TILES:
                                pad(j)
                            if j >= 1:
                                silu(j - 1)
                        act.wait_ge(ba_chain, 2)
                        act.activation(sp1[:, 1], sp1[:, 0], ACT.Abs).then_inc(ba_act, 1)
                        act.wait_ge(ba_act, 1)
                        act.activation(sp1[:, 1], sp1[:, 1], ACT.Exp, scale=-1.0)
                        act.activation(rows[:, 0], rows[:, 0], ACT.Exp).then_inc(ba_act, 1)
                        act.wait_ge(ba_act, 2)
                        act.activation(sp1[:, 1], sp1[:, 1], ACT.Ln, bias=1.0).then_inc(ba_act, 1)

                    @block.vector
                    def _(dve):
                        dve.wait_ge(loaded, 64)
                        dve.wait_ge(taps_t, 1)
                        dve.tensor_copy(taps[:, :, :], ps[:, 7, 0:N_TILES * CONV_K].rearrange("p (j c) -> p j c", c=CONV_K)).then_inc(taps_done, 1)
                        dve.wait_ge(ba_done, 1)
                        ba = ps[:, 6, 0:2 * TT * 4 * H].rearrange("p (t c) -> p t c", t=2 * TT)
                        dve.tensor_tensor(sp1[:, 0], ba[:, :, 2 * H:], rows[:, 1].unsqueeze(1).to_broadcast([P, 2 * TT, 2 * H]),
                                          ALU.add).then_inc(ba_chain, 1)
                        dve.wait_ge(ba_chain, 1)
                        dve.tensor_scalar(sp1[:, 2], sp1[:, 0], 0.0, None, ALU.max).then_inc(ba_chain, 1)
                        dve.wait_ge(taps_done, 1)
                        step = [0]
                        for j in range(N_TILES):
                            dve.wait_ge(padded, j + 1)
                            if j >= 3:
                                dve.wait_ge(silued, j - 2)
                            src, acc = xpad[:, j % 3, seq(j)], conv[:, j % 3, seq(j)]
                            for c in range(CONV_K):
                                if c == 0:
                                    ins = dve.tensor_scalar(acc, src[:, :, 0:L], taps[:, j, 0:1], None, ALU.mult)
                                else:
                                    dve.wait_ge(conv_step, step[0])
                                    ins = dve.scalar_tensor_tensor(out=acc, in0=src[:, :, c:c + L], scalar=taps[:, j, c:c + 1],
                                                                   in1=acc, op0=ALU.mult, op1=ALU.add)
                                if c < CONV_K - 1:
                                    step[0] += 1
                                    ins.then_inc(conv_step, 1)
                            ins.then_inc(conved, 1)
                        dve.wait_ge(ba_act, 3)
                        dve.tensor_tensor(sp1[:, 2], sp1[:, 2], sp1[:, 1], ALU.add).then_inc(ba_chain, 1)
                        dve.wait_ge(ba_chain, 3)
                        dve.scalar_tensor_tensor(out=glog[:, :, :], in0=sp1[:, 2], scalar=-1.0,
                                                 in1=rows[:, 0].unsqueeze(1).to_broadcast([P, 2 * TT, 2 * H]),
                                                 op0=ALU.mult, op1=ALU.mult).then_inc(ba_chain, 1)

                def span(j):
                    return (L, 2 * L) if j < H else (0, 2 * L)

                with nc.Block() as block:
                    @block.scalar
                    def _(act):
                        def square(j):
                            a, b = span(j)
                            if j >= 2:
                                act.wait_ge(sums, j - 1)
                            act.activation(sq[:, j % 2, a:b], dest(j), ACT.Square).then_inc(squared, 1)

                        def root(j):
                            a, b = span(j)
                            act.wait_ge(sums, j + 1)
                            if j >= 2:
                                act.wait_ge(normed, j - 1)
                            act.activation(norm[:, j % 2, a:b], ps[:, j % 2, a:b], ACT.Sqrt, bias=eps[:, 0:1]).then_inc(rooted, 1)

                        for j in range(2 * H + 1):
                            if j < 2 * H:
                                square(j)
                            if j >= 1:
                                root(j - 1)

                    @block.tensor
                    def _(pe):
                        for j in range(2 * H):
                            a, b = span(j)
                            pe.wait_ge(squared, j + 1)
                            if j >= 2:
                                pe.wait_ge(rooted, j - 1)
                            pe.matmul(ps[:, j % 2, a:b], ones, sq[:, j % 2, a:b], start=True, stop=True).then_inc(sums, 1)

                    @block.vector
                    def _(dve):
                        for j in range(2 * H):
                            a, b = span(j)
                            dve.wait_ge(rooted, j + 1)
                            dve.reciprocal(norm[:, j % 2, a:b], norm[:, j % 2, a:b]).then_inc(inverted, 1)
                            dve.wait_ge(inverted, j + 1)
                            dve.scalar_tensor_tensor(out=dest(j), in0=dest(j), scalar=P ** -0.5 if j < H else 1.0,
                                                     in1=norm[:, j % 2, a:b], op0=ALU.mult, op1=ALU.mult).then_inc(normed, 1)

                with nc.Block() as block:
                    @block.tensor
                    def _(pe):
                        for i in range(16):
                            src, t, half = (vT, kT)[i // 8], i % 8 // 2, i % 2
                            if i >= 4:
                                pe.wait_ge(moved_v if i % 2 else moved_a, (i - 4) // 2 + 1)
                            transpose_in(pe, i % 4, lambda m: src[:, 4 * half + m, t * P:(t + 1) * P], 4).then_inc(turned, 1)

                    def move(copy, i):
                        dst, t, half = (vtok, ktok)[i // 8], i % 8 // 2, i % 2
                        return copy(dst[:, t, half * 512:half * 512 + 512], ps[:, i % 4])

                    @block.scalar
                    def _(act):
                        for i in range(0, 16, 2):
                            act.wait_ge(turned, i + 1)
                            move(act.copy, i).then_inc(moved_a, 1)

                    @block.vector
                    def _(dve):
                        for i in range(1, 16, 2):
                            dve.wait_ge(turned, i + 1)
                            move(dve.tensor_copy, i).then_inc(moved_v, 1)
            proj_in.close()

            with ExitStack() as scope:
                dm = sb(scope, "dm", [P, 2 * H, P])
                nt = sb(scope, "nt", [P, 2 * H, P])
                tm = sb(scope, "tm", [P, 2 * H, P])
                tt = sb(scope, "tt", [P, 2 * H, P])
                qd = sb(scope, "qd", [P, 2 * H, P])
                sc = sb(scope, "sc", [P, 2 * H, P])
                state = sb(scope, "state", [P, 2 * H, P])
                xk = sb(scope, "xk", [P, 2 * H, P // 2])
                vn = sb(scope, "vn", [P, 2, 4, P])
                vdec = sb(scope, "vdec", [P, 2, 4, P])
                gsum = sb(scope, "gsum", [P, 2 * TT, 2 * H])
                nbeg = sb(scope, "nbeg", [P, 2 * TT, 2 * H])
                kdec = sb(scope, "kdec", [P, 2 * H])
                glast = sb(scope, "glast", [P, 2 * H])
                GRP = 4

                with ExitStack() as inner:
                    ssem = stage_sems(inner, "gsum_")
                    summed, copied, exped = ssem("summed"), ssem("copied"), ssem("exped")
                    with nc.Block() as block:
                        @block.tensor
                        def _(pe):
                            for t in range(2 * TT):
                                for d in range(2):
                                    ins = pe.matmul(ps[:, 0, (2 * t + d) * H:(2 * t + d + 1) * H], tri[:, d], glog[:, t, d * H:(d + 1) * H],
                                                    start=True, stop=True)
                            ins.then_inc(summed, 1)

                        @block.vector
                        def _(dve):
                            dve.wait_ge(summed, 1)
                            dve.tensor_copy(gsum[:, :, :], ps[:, 0, 0:4 * TT * H].rearrange("p (t u) -> p t u", t=2 * TT)).then_inc(copied, 1)
                            dve.wait_ge(exped, 1)
                            dve.scalar_tensor_tensor(out=nbeg[:, :, :], in0=nbeg[:, :, :], scalar=-1.0, in1=beta[:, :, :],
                                                     op0=ALU.mult, op1=ALU.mult)

                        @block.scalar
                        def _(act):
                            act.wait_ge(copied, 1)
                            act.activation(nbeg[:, :, :], gsum[:, :, :], ACT.Exp).then_inc(exped, 1)

                def unit(gi, m):
                    return 4 * gi + m

                def units(gi):
                    return slice(4 * gi, 4 * gi + 4)

                for step in range(2 * TT):
                    tiles = (step, step ^ 1)
                    on_x = step >= TT
                    tok = lambda gi: tiles[gi // 2]
                    head = lambda gi, m: 4 * (gi % 2) + m
                    cols = lambda gi, m: slice(head(gi, m) * P, head(gi, m) * P + P)
                    tcols = lambda gi: slice(tok(gi) * P, tok(gi) * P + P)
                    xcols = lambda gi: slice((tok(gi) - TT) * P, (tok(gi) - TT) * P + P)
                    quarter = lambda m: slice(m * P, m * P + P)

                    with ExitStack() as inner:
                        ssem = stage_sems(inner, f"chunk{step}_")
                        rowed, argued, dm_exp, dm_masked, erowed = (ssem(n) for n in ("rowed", "argued", "dm_exp", "dm_masked", "erowed"))
                        kk_done, qk_done, nt_done, sc_done = (ssem(n) for n in ("kk_done", "qk_done", "nt_done", "sc_done"))
                        with nc.Block() as block:
                            @block.tensor
                            def _(pe):
                                for gi in range(GRP):
                                    d, t = gi // 2, tok(gi)
                                    if gi >= 2:
                                        pe.wait_ge(erowed, gi - 1)
                                    for m in range(4):
                                        u = unit(gi, m)
                                        ins = pe.matmul(ps[:, gi % 2, quarter(m)], glog[:, t, u:u + 1].to_broadcast([P, P]), tri[:, d],
                                                        start=True, stop=True)
                                    ins.then_inc(rowed, 1)
                                    if gi >= 2:
                                        pe.wait_ge(nt_done, gi - 1)
                                    for m in range(4):
                                        k = kT[:, head(gi, m), tcols(gi)]
                                        ins = pe.matmul(ps[:, 2 + gi % 2, quarter(m)], k, k, start=True, stop=True)
                                    ins.then_inc(kk_done, 1)
                                    if on_x:
                                        if gi >= 2:
                                            pe.wait_ge(sc_done, gi - 1)
                                        for m in range(4):
                                            ins = pe.matmul(ps[:, 4 + gi % 2, quarter(m)], kT[:, head(gi, m), tcols(gi)],
                                                            qT[:, head(gi, m), xcols(gi)], start=True, stop=True)
                                        ins.then_inc(qk_done, 1)

                            @block.vector
                            def _(dve):
                                def products(gi):
                                    dve.wait_ge(dm_masked, gi + 1)
                                    dve.wait_ge(kk_done, gi + 1)
                                    dve.tensor_tensor(nt[:, units(gi)], ps[:, 2 + gi % 2].rearrange("p (u c) -> p u c", u=4), dm[:, units(gi)],
                                                      ALU.mult).then_inc(nt_done, 1)
                                    if on_x:
                                        dve.wait_ge(qk_done, gi + 1)
                                        dve.tensor_tensor(sc[:, units(gi)], ps[:, 4 + gi % 2].rearrange("p (u c) -> p u c", u=4), dm[:, units(gi)],
                                                          ALU.mult).then_inc(sc_done, 1)

                                for gi in range(GRP):
                                    dve.wait_ge(rowed, gi + 1)
                                    for m in range(4):
                                        u = unit(gi, m)
                                        ins = dve.tensor_scalar(dm[:, u], ps[:, gi % 2, quarter(m)], gsum[:, tok(gi), u:u + 1], 0.0,
                                                                ALU.subtract, ALU.min)
                                    ins.then_inc(argued, 1)
                                    if gi >= 1:
                                        products(gi - 1)
                                products(GRP - 1)

                            @block.scalar
                            def _(act):
                                for gi in range(GRP):
                                    last = P - 1 if gi < 2 else 0
                                    rows_t = ps[:, gi % 2].rearrange("p (u c) -> p u c", u=4)
                                    act.wait_ge(argued, gi + 1)
                                    act.activation(dm[:, units(gi)], dm[:, units(gi)], ACT.Exp).then_inc(dm_exp, 1)
                                    if on_x:
                                        act.activation(qd[:, units(gi)], rows_t, ACT.Exp)
                                    act.activation(glast[:, units(gi)], rows_t[:, :, last], ACT.Exp).then_inc(erowed, 1)

                            @block.gpsimd
                            def _(pool):
                                for gi in range(GRP):
                                    d, last = gi // 2, P - 1 if gi < 2 else 0
                                    pool.wait_ge(dm_exp, gi + 1)
                                    pool.tensor_tensor(dm[:, units(gi)], dm[:, units(gi)], tri[:, d].unsqueeze(1).to_broadcast([P, 4, P]),
                                                       ALU.mult).then_inc(dm_masked, 1)
                                    if on_x:
                                        pool.wait_ge(erowed, gi + 1)
                                        h0 = 4 * (gi % 2)
                                        pool.tensor_tensor(qd[:, units(gi)], qd[:, units(gi)], qT[:, h0:h0 + 4, xcols(gi)], ALU.mult)
                                    pool.wait_ge(dm_masked, gi + 1)
                                    pool.tensor_copy(kdec[:, units(gi)], dm[:, units(gi), last])

                    with ExitStack() as inner:
                        ssem = stage_sems(inner, f"inverse{step}_")
                        t_init, x_done, xk_done, tx_done = (ssem(n) for n in ("t_init", "x_done", "xk_done", "tx_done"))
                        t_done, turned, tt_done = (ssem(n) for n in ("t_done", "turned", "tt_done"))
                        with nc.Block() as block:
                            @block.tensor
                            def _(pe):
                                for lv in range(LEVELS):
                                    for gi in range(GRP):
                                        if lv:
                                            pe.wait_ge(t_done, GRP * (lv - 1) + gi + 1)
                                            pe.wait_ge(tt_done, GRP * (lv - 1) + gi + 1)
                                        for m in range(4):
                                            u = unit(gi, m)
                                            rhs = half_cols(tm[:, u] if lv else ident, lv, gi // 2)
                                            ins = pe.matmul(ps[:, gi, 64 * m:64 * m + 64], nt[:, u], rhs, start=True, stop=True)
                                        ins.then_inc(x_done, 1)
                                    if lv:
                                        for gi in range(GRP):
                                            pe.wait_ge(xk_done, GRP * lv + gi + 1)
                                            for m in range(4):
                                                u = unit(gi, m)
                                                ins = pe.matmul(ps[:, 4 + gi, 64 * m:64 * m + 64], tt[:, u], xk[:, u], start=True, stop=True)
                                            ins.then_inc(tx_done, 1)
                                    for gi in range(GRP):
                                        pe.wait_ge(t_done, GRP * lv + gi + 1)
                                        transpose_in(pe, gi, lambda m: tm[:, unit(gi, m)], 4).then_inc(turned, 1)

                            @block.vector
                            def _(dve):
                                dve.wait_ge(t_init, 1)
                                for lv in range(LEVELS):
                                    for gi in range(GRP):
                                        d, t = gi // 2, tok(gi)
                                        dve.wait_ge(x_done, GRP * lv + gi + 1)
                                        for m in range(4):
                                            u = unit(gi, m)
                                            ins = dve.scalar_tensor_tensor(out=xk[:, u], in0=ps[:, gi, 64 * m:64 * m + 64], scalar=beta[:, t, u:u + 1],
                                                                           in1=lev[:, d, lv], op0=ALU.mult, op1=ALU.mult)
                                        ins.then_inc(xk_done, 1)
                                    for gi in range(GRP):
                                        if lv:
                                            dve.wait_ge(tx_done, GRP * (lv - 1) + gi + 1)
                                            term = ps[:, 4 + gi, 0:4 * 64].rearrange("p (u c) -> p u c", u=4)
                                        else:
                                            dve.wait_ge(xk_done, gi + 1)
                                            term = xk[:, units(gi)]
                                        part = half_cols(tm[:, units(gi)], lv, gi // 2)
                                        dve.tensor_tensor(part, part, packed_cols(term, lv), ALU.subtract).then_inc(t_done, 1)
                                for gi in range(GRP):
                                    dve.wait_ge(tt_done, GRP * (LEVELS - 1) + gi + 1)
                                    for m in range(4):
                                        u = unit(gi, m)
                                        dve.tensor_scalar(tm[:, u], tt[:, u], beta[:, tok(gi), u:u + 1], None, ALU.mult)

                            @block.scalar
                            def _(act):
                                for n in range(GRP * LEVELS):
                                    gi = n % GRP
                                    act.wait_ge(turned, n + 1)
                                    act.copy(tt[:, units(gi)], ps[:, gi].rearrange("p (u c) -> p u c", u=4)).then_inc(tt_done, 1)

                            @block.gpsimd
                            def _(pool):
                                pool.tensor_copy(tm[:, :, :], ident.unsqueeze(1).to_broadcast([P, 2 * H, P])).then_inc(t_init, 1)
                                for gi in range(GRP):
                                    pool.wait_ge(tt_done, GRP * (LEVELS - 1) + gi + 1)
                                    for m in range(4):
                                        u = unit(gi, m)
                                        pool.tensor_scalar(nt[:, u], tt[:, u], nbeg[:, tok(gi), u:u + 1], None, ALU.mult)

                    with ExitStack() as inner:
                        ssem = stage_sems(inner, f"scan{step}_")
                        w_done, wt_done, vn_done, vdec_done, vn_copied = (ssem(n) for n in ("w_done", "wt_done", "vn_done", "vdec_done", "vn_copied"))
                        o_done, o_added, s_done, s_added = (ssem(n) for n in ("o_done", "o_added", "s_done", "s_added"))
                        more = step < 2 * TT - 1
                        with nc.Block() as block:
                            @block.tensor
                            def _(pe):
                                def new_v(gi):
                                    pe.wait_ge(wt_done, gi + 1)
                                    if gi >= 2:
                                        pe.wait_ge(vn_copied if on_x else vdec_done, gi - 1)
                                    for m in range(4):
                                        u = unit(gi, m)
                                        ins = pe.matmul(ps[:, 2 + gi % 2, quarter(m)], tm[:, u], vtok[:, tok(gi), cols(gi, m)], start=True, stop=step == 0)
                                        if step:
                                            ins = pe.matmul(ps[:, 2 + gi % 2, quarter(m)], dm[:, u], state[:, u], start=False, stop=True)
                                    ins.then_inc(vn_done, 1)

                                def outputs(gi):
                                    pe.wait_ge(vn_copied, gi + 1)
                                    if gi >= 2:
                                        pe.wait_ge(o_added, gi - 1)
                                    for m in range(4):
                                        u = unit(gi, m)
                                        pe.matmul(ps[:, 6 + gi % 2, quarter(m)], qd[:, u], state[:, u], start=True, stop=False)
                                        ins = pe.matmul(ps[:, 6 + gi % 2, quarter(m)], sc[:, u], vn[:, gi % 2, m], start=False, stop=True)
                                    ins.then_inc(o_done, 1)

                                def next_state(gi):
                                    pe.wait_ge(vdec_done, gi + 1)
                                    if gi >= 2:
                                        pe.wait_ge(s_added, gi - 1)
                                    for m in range(4):
                                        ins = pe.matmul(ps[:, 4 + gi % 2, quarter(m)], ktok[:, tok(gi), cols(gi, m)], vdec[:, gi % 2, m],
                                                        start=True, stop=True)
                                    ins.then_inc(s_done, 1)

                                for gi in range(GRP):
                                    if gi >= 2:
                                        pe.wait_ge(wt_done, gi - 1)
                                    for m in range(4):
                                        ins = pe.matmul(ps[:, gi % 2, quarter(m)], ktok[:, tok(gi), cols(gi, m)], nt[:, unit(gi, m)], start=True, stop=True)
                                    ins.then_inc(w_done, 1)
                                new_v(0)
                                new_v(1)
                                for gi in range(GRP):
                                    if on_x:
                                        outputs(gi)
                                    if more:
                                        next_state(gi)
                                    if gi + 2 < GRP:
                                        new_v(gi + 2)

                            @block.scalar
                            def _(act):
                                for gi in range(GRP):
                                    act.wait_ge(w_done, gi + 1)
                                    act.copy(dm[:, units(gi)], ps[:, gi % 2].rearrange("p (u c) -> p u c", u=4)).then_inc(wt_done, 1)
                                if on_x:
                                    for gi in range(GRP):
                                        if more:
                                            act.wait_ge(vdec_done, gi + 1)
                                        else:
                                            act.wait_ge(vn_done, gi + 1)
                                        if gi >= 2:
                                            act.wait_ge(o_done, gi - 1)
                                        act.copy(vn[:, gi % 2], ps[:, 2 + gi % 2].rearrange("p (u c) -> p u c", u=4)).then_inc(vn_copied, 1)

                            @block.vector
                            def _(dve):
                                def decayed(gi):
                                    dve.wait_ge(vn_done, gi + 1)
                                    if gi >= 2:
                                        dve.wait_ge(s_done, gi - 1)
                                    dve.tensor_tensor(vdec[:, gi % 2], ps[:, 2 + gi % 2].rearrange("p (u c) -> p u c", u=4),
                                                      kdec[:, units(gi)].unsqueeze(2).to_broadcast([P, 4, P]), ALU.mult).then_inc(vdec_done, 1)

                                def finish(gi):
                                    if on_x:
                                        x_tile, h0 = tok(gi) - TT, 4 * (gi % 2)
                                        o = otok[:, x_tile, h0 * P:(h0 + 4) * P]
                                        dve.wait_ge(o_done, gi + 1)
                                        if step == TT:
                                            dve.tensor_copy(o, ps[:, 6 + gi % 2]).then_inc(o_added, 1)
                                        else:
                                            dve.tensor_tensor(o, ps[:, 6 + gi % 2], o, ALU.add).then_inc(o_added, 1)
                                    if more:
                                        dve.wait_ge(s_done, gi + 1)
                                        for m in range(4):
                                            u = unit(gi, m)
                                            if step == 0:
                                                ins = dve.tensor_copy(state[:, u], ps[:, 4 + gi % 2, quarter(m)])
                                            else:
                                                ins = dve.scalar_tensor_tensor(out=state[:, u], in0=state[:, u], scalar=glast[:, u:u + 1],
                                                                               in1=ps[:, 4 + gi % 2, quarter(m)], op0=ALU.mult, op1=ALU.add)
                                        ins.then_inc(s_added, 1)

                                if more:
                                    decayed(0)
                                    decayed(1)
                                for gi in range(GRP):
                                    finish(gi)
                                    if more and gi + 2 < GRP:
                                        decayed(gi + 2)
            qkv.close()

            mods = sb(first, "mods", [P, 4, D])
            gates = sb(first, "gates", [P, 2, TT, D])
            ygT = sb(first, "ygT", [P, KT, L])
            ysT = sb(first, "ysT", [P, KT, L])
            with ExitStack() as scope:
                zs = sb(scope, "zs", [P, TT, D])
                uu = sb(scope, "uu", [P, TT, D])
                vv = sb(scope, "vv", [P, TT, D])
                spw = sb(scope, "spw", [P, H, P])
                spwT = sb(scope, "spwT", [P, H, P])
                spb_row = sb(scope, "spb_row", [H, P])
                spb = sb(scope, "spb", [P, H])
                ln_rows = sb(scope, "ln_rows", [P, 2, D])
                gn_row = sb(scope, "gn_row", [P, P])
                osq = sb(scope, "osq", [P, TT, D])
                orms = sb(scope, "orms", [P, TT * H])
                bn = sb(scope, "bn", [P, TT, 2, 6])
                mv = sb(scope, "mv", [P, TT, 2])
                ssem = stage_sems(scope, "zuvg_")
                loaded, turned, turned_copied, proj, moved = (ssem(n) for n in ("loaded", "turned", "turned_copied", "proj", "moved"))
                o_step, o_std, v_step, v_std, v_out = (ssem(n) for n in ("o_step", "o_std", "v_step", "v_std", "v_out"))
                BANKS = 6
                dests = [(zs, ACT.Silu)] * 2 + [(uu, ACT.Gelu_apprx_tanh)] * 2 + [(vv, ACT.Gelu_apprx_tanh)] * 2
                dests += [(gates[:, 0], ACT.Sigmoid)] * 2 + [(gates[:, 1], ACT.Sigmoid)] * 2
                oh = otok[:, :, :].rearrange("p t (h d) -> p (t h) d", h=H)
                with nc.Block() as block:
                    @block.sync
                    def _(sp):
                        sp.dma_start(spw[:, :, :], w["sgu_w"][0].rearrange("g p q -> p g q")).then_inc(loaded, 16)
                        sp.dma_start(spb_row[:, :], w["sgu_b"][0]).then_inc(loaded, 16)
                        sp.dma_start(ln_rows[:, 0], row_bcast(w["sgu_ln_g"][0])).then_inc(loaded, 16)
                        sp.dma_start(ln_rows[:, 1], row_bcast(w["sgu_ln_b"][0])).then_inc(loaded, 16)
                        sp.dma_start(gn_row[:, :], row_bcast(w["gdn_norm_g"][0])).then_inc(loaded, 16)
                        stream.issue(sp, ADA_REST + RING)

                    @block.tensor
                    def _(pe):
                        pe.wait_ge(loaded, 80)
                        transpose_in(pe, 0, lambda i: spw[:, i], 4)
                        transpose_in(pe, 1, lambda i: spw[:, 4 + i], 4)
                        pe.transpose(ps[:, 2, 0:H], spb_row[:, :], ident[0:H, 0:H]).then_inc(turned, 1)
                        for i in range(10 * TT):
                            n, t = ZUVG + i // TT, i % TT
                            if t == 0:
                                pe.wait_ge(*stream.arrive(n))
                            if i == 0:
                                pe.wait_ge(turned_copied, 1)
                            if i >= BANKS:
                                pe.wait_ge(moved, i - BANKS + 1)
                            for kt in range(KT):
                                ins = pe.matmul(ps[:, 2 + i % BANKS], hTx[:, kt, t * P:(t + 1) * P], stream.slot(n)[:, kt],
                                                start=(kt == 0), stop=(kt == KT - 1))
                            ins.then_inc(proj, 1)
                            if t == TT - 1:
                                pe.drain().then_inc(stream.used, 1)

                    @block.scalar
                    def _(act):
                        act.wait_ge(turned, 1)
                        for i in range(2):
                            act.copy(spwT[:, 4 * i:4 * i + 4], ps[:, i].rearrange("p (g q) -> p g q", g=4))
                        act.copy(spb[:, :], ps[:, 2, 0:H]).then_inc(turned_copied, 1)
                        act.wait_ge(o_step, 3)
                        act.activation(orms[:, :], orms[:, :], ACT.Sqrt).then_inc(o_std, 1)
                        for i in range(10 * TT):
                            dst, func = dests[i // TT]
                            half = slice(i // TT % 2 * PANEL, i // TT % 2 * PANEL + PANEL)
                            act.wait_ge(proj, i + 1)
                            act.activation(dst[:, i % TT, half], ps[:, 2 + i % BANKS], func).then_inc(moved, 1)
                        act.wait_ge(v_step, 2 * TT)
                        act.activation(mv[:, :, 1], mv[:, :, 1], ACT.Sqrt, bias=eps[:, 0:1]).then_inc(v_std, 1)

                    @block.vector
                    def _(dve):
                        dve.tensor_tensor(osq[:, :, :], otok[:, :, :], otok[:, :, :], ALU.mult).then_inc(o_step, 1)
                        dve.wait_ge(o_step, 1)
                        dve.tensor_reduce(orms[:, :], osq[:, :, :].rearrange("p t (h d) -> p (t h) d", h=H), AX.X, ALU.add).then_inc(o_step, 1)
                        dve.wait_ge(o_step, 2)
                        dve.tensor_scalar(orms[:, :], orms[:, :], 1.0 / P, EPS, ALU.mult, ALU.add).then_inc(o_step, 1)
                        dve.wait_ge(o_std, 1)
                        dve.reciprocal(orms[:, :], orms[:, :]).then_inc(o_step, 1)
                        dve.wait_ge(o_step, 4)
                        dve.tensor_tensor(oh, oh, orms[:, :].unsqueeze(2).to_broadcast([P, TT * H, P]), ALU.mult).then_inc(o_step, 1)
                        dve.wait_ge(o_step, 5)
                        dve.wait_ge(loaded, 80)
                        dve.tensor_tensor(oh, oh, gn_row[:, :].unsqueeze(1).to_broadcast([P, TT * H, P]), ALU.mult).then_inc(o_step, 1)
                        dve.wait_ge(o_step, 6)
                        dve.wait_ge(moved, 2 * TT)
                        dve.tensor_tensor(otok[:, :, :], otok[:, :, :], zs[:, :, :], ALU.mult)
                        for t in range(TT):
                            dve.wait_ge(moved, 6 * TT)
                            for j in range(2):
                                ins = dve.bn_stats(bn[:, t, j], vv[:, t, j * 512:j * 512 + 512])
                            ins.then_inc(v_step, 1)
                            dve.wait_ge(v_step, 2 * t + 1)
                            dve.bn_aggr(mv[:, t], bn[:, t]).then_inc(v_step, 1)
                        dve.wait_ge(v_std, 1)
                        dve.reciprocal(mv[:, :, 1], mv[:, :, 1]).then_inc(v_out, 1)
                        dve.wait_ge(v_out, 1)
                        for t in range(TT):
                            dve.tensor_scalar(vv[:, t], vv[:, t], mv[:, t, 0:1], mv[:, t, 1:2], ALU.subtract, ALU.mult).then_inc(v_out, 1)
                            dve.wait_ge(v_out, 3 * t + 2)
                            dve.tensor_tensor(vv[:, t], vv[:, t], ln_rows[:, 0], ALU.mult).then_inc(v_out, 1)
                            dve.wait_ge(v_out, 3 * t + 3)
                            dve.tensor_tensor(vv[:, t], vv[:, t], ln_rows[:, 1], ALU.add).then_inc(v_out, 1)

                with ExitStack() as inner:
                    ssem = stage_sems(inner, "sgu_")
                    mixed, gated, turned, moved = (ssem(n) for n in ("mixed", "gated", "turned", "moved"))
                    with nc.Block() as block:
                        @block.tensor
                        def _(pe):
                            for i in range(2 * TT):
                                t, g0 = i // 2, 4 * (i % 2)
                                for m in range(4):
                                    ins = pe.matmul(ps[:, i, m * P:(m + 1) * P], spwT[:, g0 + m], vv[:, t, (g0 + m) * P:(g0 + m + 1) * P],
                                                    start=True, stop=True)
                                ins.then_inc(mixed, 1)
                            for i in range(KT):
                                src = otok if i < KT // 2 else uu
                                if i >= 4:
                                    pe.wait_ge(moved, i - 3)
                                if i == KT // 2:
                                    pe.wait_ge(gated, 2 * TT)
                                kt = 2 * (i % (KT // 2))
                                transpose_in(pe, 4 + i % 4, lambda m: src[:, m % TT, (kt + m // TT) * P:(kt + m // TT + 1) * P], 4).then_inc(turned, 1)

                        @block.vector
                        def _(dve):
                            for i in range(2 * TT):
                                t, g0 = i // 2, 4 * (i % 2)
                                dve.wait_ge(mixed, i + 1)
                                for m in range(4):
                                    g = g0 + m
                                    part = uu[:, t, g * P:(g + 1) * P]
                                    ins = dve.scalar_tensor_tensor(out=part, in0=ps[:, i, m * P:(m + 1) * P], scalar=spb[:, g:g + 1],
                                                                   in1=part, op0=ALU.add, op1=ALU.mult)
                                ins.then_inc(gated, 1)

                        @block.scalar
                        def _(act):
                            for i in range(KT):
                                dst = ygT if i < KT // 2 else ysT
                                kt = 2 * (i % (KT // 2))
                                act.wait_ge(turned, i + 1)
                                act.copy(dst[:, kt:kt + 2], ps[:, 4 + i % 4].rearrange("p (k t) -> p k t", k=2)).then_inc(moved, 1)

            with ExitStack() as scope:
                def loads(sp, loaded):
                    for r in range(4):
                        sp.dma_start(mods[:, r], row_bcast(w["ada_b"][0, (2 + r) * D:(3 + r) * D])).then_inc(loaded, 16)

                ada_block("ada_rest", ADA_REST, 8, cact[:, 0], None, lambda i: mods[:, i // 2, (i % 2) * PANEL:(i % 2 + 1) * PANEL],
                          lambda i: None, loads, 4, MERGE + RING, scope)

            with ExitStack() as scope:
                merged = sb(scope, "merged", [P, TT, D])
                part_b = sb(scope, "part_b", [P, TT, D])
                mT = sb(scope, "mT", [P, KT, L])
                ssem = stage_sems(scope, "merge_")
                proj, gated, summed, turned, moved, outed, scaled, added = (
                    ssem(n) for n in ("proj", "gated", "summed", "turned", "moved", "outed", "scaled", "added"))
                with nc.Block() as block:
                    @block.sync
                    def _(sp):
                        stream.issue(sp, MOE + RING)

                    @block.tensor
                    def _(pe):
                        for i in range(4):
                            n = MERGE + i
                            pe.wait_ge(*stream.arrive(n))
                            for t in range(TT):
                                for kt in range(KT):
                                    ins = pe.matmul(ps[:, TT * i + t], (ygT, ysT)[i // 2][:, kt, t * P:(t + 1) * P], stream.slot(n)[:, kt],
                                                    start=(kt == 0), stop=(kt == KT - 1))
                                ins.then_inc(proj, 1)
                            pe.drain().then_inc(stream.used, 1)
                        pe.wait_ge(summed, 2 * TT)
                        for i in range(4):
                            transpose_in(pe, i, lambda m: merged[:, m % TT, (2 * i + m // TT) * P:(2 * i + m // TT + 1) * P], 4).then_inc(turned, 1)
                        for i in range(2):
                            n = MERGE + 4 + i
                            pe.wait_ge(*stream.arrive(n))
                            pe.wait_ge(moved, 4)
                            for t in range(TT):
                                for kt in range(KT):
                                    ins = pe.matmul(ps[:, 4 + TT * i + t], mT[:, kt, t * P:(t + 1) * P], stream.slot(n)[:, kt],
                                                    start=(kt == 0), stop=(kt == KT - 1))
                                ins.then_inc(outed, 1)
                            pe.drain().then_inc(stream.used, 1)

                    @block.vector
                    def _(dve):
                        for i in range(4 * TT):
                            b, half, t = i // (2 * TT), i // TT % 2, i % TT
                            cols = slice(half * PANEL, half * PANEL + PANEL)
                            dve.wait_ge(proj, i + 1)
                            dve.tensor_tensor((merged, part_b)[b][:, t, cols], ps[:, i], gates[:, b, t, cols], ALU.mult).then_inc(gated, 1)
                        for i in range(2 * TT):
                            t, cols = i % TT, slice(i // TT * PANEL, i // TT * PANEL + PANEL)
                            dve.wait_ge(gated, 2 * TT + i + 1)
                            dve.tensor_tensor(merged[:, t, cols], merged[:, t, cols], part_b[:, t, cols], ALU.add).then_inc(summed, 1)
                        for i in range(2 * TT):
                            t, cols = i % TT, slice(i // TT * PANEL, i // TT * PANEL + PANEL)
                            dve.wait_ge(outed, i + 1)
                            dve.tensor_tensor(part_b[:, t, cols], ps[:, 4 + i], mods[:, 0, cols], ALU.mult).then_inc(scaled, 1)
                            dve.wait_ge(scaled, i + 1)
                            dve.tensor_tensor(xs[:, t, cols], xs[:, t, cols], part_b[:, t, cols], ALU.add).then_inc(added, 1)

                    @block.scalar
                    def _(act):
                        for i in range(4):
                            act.wait_ge(turned, i + 1)
                            act.copy(mT[:, 2 * i:2 * i + 2], ps[:, i].rearrange("p (k t) -> p k t", k=2)).then_inc(moved, 1)

            with ExitStack() as ffn:
                h2T = sb(ffn, "h2T", [P, KT, L])
                acc = sb(ffn, "acc", [P, TT, D])
                gate = sb(ffn, "gate", [P, TT, GROUPS, PER_GROUP])
                with ExitStack() as scope:
                    grow = sb(scope, "grow", [P, D])
                    gm = sb(scope, "gm2", [P, D])
                    h2 = sb(scope, "h2", [P, TT, D])
                    sqr = sb(scope, "sqr", [P, D])
                    wr = sb(scope, "wr", [P, KT, ROUTER])
                    br = sb(scope, "br", [P, ROUTER])
                    logits = sb(scope, "logits", [P, TT, ROUTER])
                    order = sb(scope, "order", [P, PER_GROUP])
                    one = lambda n, k: sb(scope, n, [P, TT, k])
                    gtop, gdiff, gexp, ghot, gprob = one("gtop", 1), one("gdiff", GROUPS), one("gexp", GROUPS), one("ghot", GROUPS), one("gprob", 1)
                    chosen = sb(scope, "chosen", [P, TT, GROUPS, PER_GROUP])
                    lin, top, hot1, hot2, tie = (one("lin", PER_GROUP), one("top", 1), one("hot1", PER_GROUP), one("hot2", PER_GROUP),
                                                 one("tie", PER_GROUP))
                    e2, w_1, w_2 = one("e2", 1), one("w_1", 1), one("w_2", 1)
                    ssem = stage_sems(scope, "route_")
                    loaded, squares, steps, std, turned, moved, routed, ge_done, e2_done, chain, ordered = (
                        ssem(n) for n in ("loaded", "squares", "steps", "std", "turned", "moved", "routed", "ge_done", "e2_done", "chain", "ordered"))
                    with nc.Block() as block:
                        @block.sync
                        def _(sp):
                            sp.dma_start(grow[:, :], row_bcast(w["norm_ffn_g"][0])).then_inc(loaded, 16)
                            sp.dma_start(wr[:, :, 0:GROUPS], ktp(w["router_group_w"][0])).then_inc(loaded, 16)
                            sp.dma_start(wr[:, :, GROUPS:], ktp(w["router_expert_w"][0])).then_inc(loaded, 16)
                            sp.dma_start(br[:, 0:GROUPS], row_bcast(w["router_group_b"][0])).then_inc(loaded, 16)
                            sp.dma_start(br[:, GROUPS:], row_bcast(w["router_expert_b"][0])).then_inc(loaded, 16)

                        @block.gpsimd
                        def _(pool):
                            for i in range(PER_GROUP):
                                ins = pool.memset(order[:, i:i + 1], float(PER_GROUP - i))
                            ins.then_inc(ordered, 1)

                        @block.scalar
                        def _(act):
                            for t in range(TT):
                                if t:
                                    act.wait_ge(squares, t)
                                act.activation(sqr[:, :], xs[:, t], ACT.Square, accum_out=stat[:, t:t + 1]).then_inc(squares, 1)
                            act.wait_ge(steps, 1)
                            act.activation(stat[:, 2:4], stat[:, 2:4], ACT.Sqrt).then_inc(std, 1)
                            for i in range(4):
                                act.wait_ge(turned, i + 1)
                                act.copy(h2T[:, 2 * i:2 * i + 2], ps[:, i].rearrange("p (k t) -> p k t", k=2)).then_inc(moved, 1)
                            act.wait_ge(chain, 3)
                            act.activation(gexp[:, :, :], gdiff[:, :, :], ACT.Exp).then_inc(ge_done, 1)
                            act.wait_ge(chain, 17)
                            act.activation(e2[:, :, :], top[:, :, :], ACT.Exp).then_inc(e2_done, 1)

                        @block.tensor
                        def _(pe):
                            pe.wait_ge(steps, 3 + 2 * TT)
                            for i in range(4):
                                transpose_in(pe, i, lambda m: h2[:, m % TT, (2 * i + m // TT) * P:(2 * i + m // TT + 1) * P], 4).then_inc(turned, 1)
                            pe.wait_ge(moved, 4)
                            pe.wait_ge(loaded, 80)
                            for t in range(TT):
                                for kt in range(KT):
                                    ins = pe.matmul(ps[:, 4, ROUTER * t:ROUTER * (t + 1)], h2T[:, kt, t * P:(t + 1) * P], wr[:, kt],
                                                    start=(kt == 0), stop=(kt == KT - 1))
                            ins.then_inc(routed, 1)

                        @block.vector
                        def _(dve):
                            dve.wait_ge(squares, TT)
                            dve.tensor_scalar(stat[:, 2:4], stat[:, 0:2], 1.0 / D, EPS, ALU.mult, ALU.add).then_inc(steps, 1)
                            dve.wait_ge(loaded, 80)
                            dve.scalar_tensor_tensor(out=gm[:, :], in0=mods[:, 2], scalar=1.0, in1=grow[:, :], op0=ALU.add, op1=ALU.mult).then_inc(steps, 1)
                            dve.wait_ge(std, 1)
                            dve.reciprocal(stat[:, 4:6], stat[:, 2:4]).then_inc(steps, 1)
                            dve.wait_ge(steps, 3)
                            for t in range(TT):
                                norm_modulate(dve, steps, 3 + 2 * t, xs[:, t], stat[:, 4 + t:5 + t], gm[:, :], mods[:, 1],
                                              h2[:, t], h2[:, t]).then_inc(steps, 1)
                            link = chained(dve, chain)
                            wide = lambda a, n: a[:, :, :].to_broadcast([P, TT, n])
                            dve.wait_ge(routed, 1)
                            dve.wait_ge(ordered, 1)
                            link(dve.tensor_tensor(logits[:, :, :], ps[:, 4, 0:TT * ROUTER].rearrange("p (t r) -> p t r", t=TT),
                                                   br[:, :].unsqueeze(1).to_broadcast([P, TT, ROUTER]), ALU.add))
                            group, expert = logits[:, :, 0:GROUPS], logits[:, :, GROUPS:].rearrange("p t (g e) -> p t g e", g=GROUPS)
                            link(dve.tensor_reduce(gtop[:, :, :], group, AX.X, ALU.max))
                            link(dve.tensor_tensor(gdiff[:, :, :], group, wide(gtop, GROUPS), ALU.subtract))

                            def first_top(hot, diff, n):
                                weights = order[:, PER_GROUP - n:].unsqueeze(1).to_broadcast([P, TT, n])
                                link(dve.tensor_scalar(hot, diff, 0.0, None, ALU.is_ge))
                                link(dve.tensor_tensor(hot, hot, weights, ALU.mult))
                                link(dve.tensor_reduce(gtop[:, :, :], hot, AX.X, ALU.max))
                                link(dve.tensor_tensor(hot, hot, wide(gtop, n), ALU.is_equal))

                            first_top(ghot[:, :, :], gdiff[:, :, :], GROUPS)
                            link(dve.tensor_tensor(chosen[:, :, :, :], expert, ghot[:, :, :].unsqueeze(3).to_broadcast([P, TT, GROUPS, PER_GROUP]),
                                                   ALU.mult))
                            link(dve.tensor_reduce(lin[:, :, :], chosen[:, :, :, :].rearrange("p t g e -> p t e g"), AX.X, ALU.add))
                            link(dve.tensor_reduce(top[:, :, :], lin[:, :, :], AX.X, ALU.max))
                            link(dve.tensor_tensor(lin[:, :, :], lin[:, :, :], wide(top, PER_GROUP), ALU.subtract))
                            first_top(hot1[:, :, :], lin[:, :, :], PER_GROUP)
                            link(dve.scalar_tensor_tensor(out=lin[:, :, :], in0=hot1[:, :, :], scalar=MASKED, in1=lin[:, :, :],
                                                          op0=ALU.mult, op1=ALU.add))
                            link(dve.tensor_reduce(top[:, :, :], lin[:, :, :], AX.X, ALU.max))
                            link(dve.tensor_tensor(tie[:, :, :], lin[:, :, :], wide(top, PER_GROUP), ALU.subtract))
                            first_top(hot2[:, :, :], tie[:, :, :], PER_GROUP)
                            dve.wait_ge(ge_done, 1)
                            link(dve.tensor_reduce(gprob[:, :, :], gexp[:, :, :], AX.X, ALU.add))
                            link(dve.reciprocal(gprob[:, :, :], gprob[:, :, :]))
                            dve.wait_ge(e2_done, 1)
                            link(dve.tensor_scalar(w_1[:, :, :], e2[:, :, :], 1.0, None, ALU.add))
                            link(dve.reciprocal(w_1[:, :, :], w_1[:, :, :]))
                            link(dve.tensor_tensor(w_1[:, :, :], w_1[:, :, :], gprob[:, :, :], ALU.mult))
                            link(dve.tensor_tensor(w_2[:, :, :], w_1[:, :, :], e2[:, :, :], ALU.mult))
                            link(dve.tensor_tensor(hot1[:, :, :], hot1[:, :, :], wide(w_1, PER_GROUP), ALU.mult))
                            link(dve.tensor_tensor(hot2[:, :, :], hot2[:, :, :], wide(w_2, PER_GROUP), ALU.mult))
                            link(dve.tensor_tensor(hot1[:, :, :], hot1[:, :, :], hot2[:, :, :], ALU.add))
                            link(dve.tensor_tensor(gate[:, :, :, :], ghot[:, :, :].unsqueeze(3).to_broadcast([P, TT, GROUPS, PER_GROUP]),
                                                   hot1[:, :, :].unsqueeze(2).to_broadcast([P, TT, GROUPS, PER_GROUP]), ALU.mult))

                with ExitStack() as scope:
                    silu1 = sb(scope, "silu1", [P, 2, 2, L])
                    hid = sb(scope, "hid", [P, 2, 2, L])
                    ssem = stage_sems(scope, "moe_")
                    w1_done, w3_done, silu_done, hid_done, down_done, acc_done = (
                        ssem(n) for n in ("w1_done", "w3_done", "silu_done", "hid_done", "down_done", "acc_done"))
                    gates_e = gate[:, :, :, :].rearrange("p t g e -> p t (g e)")
                    ROUNDS = N_EXPERTS // 2
                    base = [stream.arrive(MOE + k)[1] - 32 for k in range(3)]
                    with nc.Block() as block:
                        @block.sync
                        def _(sp):
                            assert stream.issued == MOE + RING == MOE + 3
                            with sp.Fori(0, ROUNDS - 1) as r:
                                for k in range(3):
                                    n = MOE + k
                                    sp.wait_ge(stream.used, 3 * r + (n + 1))
                                    slot, loaded = stream.slot(n), stream.loaded[n % RING]
                                    e = 2 * r + 2
                                    if k < 2:
                                        sp.dma_start(slot[:, :, 0:D_EXPERT], w1[e + k]).then_inc(loaded, 16)
                                        sp.dma_start(slot[:, :, D_EXPERT:], w3[e + k]).then_inc(loaded, 16)
                                    else:
                                        view = slot.rearrange("p (e f c) n -> p e f (c n)", e=2, f=2)
                                        for j in range(2):
                                            sp.dma_start(view[:, j], w2[e + j]).then_inc(loaded, 16)
                            stream.issued = ADA2
                            stream.issue(sp, ADA2 + RING)

                        @block.tensor
                        def _(pe):
                            with pe.Fori(0, ROUNDS) as r:
                                for j in range(2):
                                    n = MOE + j
                                    pe.wait_ge(stream.loaded[n % RING], 32 * r + (base[j] + 32))
                                    pe.wait_ge(hid_done, 2 * r + (j + 1))
                                    for half, done in enumerate((w1_done, w3_done)):
                                        for f in range(2):
                                            col = half * D_EXPERT + f * P
                                            for kt in range(KT):
                                                ins = pe.matmul(ps[:, 2 * j + half, f * L:(f + 1) * L], stream.slot(n)[:, kt, col:col + P],
                                                                h2T[:, kt], start=(kt == 0), stop=(kt == KT - 1))
                                        ins.then_inc(done, 1)
                                    pe.drain().then_inc(stream.used, 1)
                                n = MOE + 2
                                view = stream.slot(n).rearrange("p (e f c) n -> p e f (c n)", e=2, f=2)
                                pe.wait_ge(stream.loaded[n % RING], 32 * r + (base[2] + 32))
                                for j in range(2):
                                    pe.wait_ge(hid_done, 2 * r + (j + 3))
                                    for b in range(4):
                                        t, c = b // 2, b % 2
                                        pe.wait_ge(acc_done, 8 * r + (4 * j + b + 1))
                                        for f in range(2):
                                            ins = pe.matmul(ps[:, 4 + b], hid[:, j, f, t * P:(t + 1) * P], view[:, j, f, c * PANEL:(c + 1) * PANEL],
                                                            start=(f == 0), stop=(f == 1))
                                        ins.then_inc(down_done, 1)
                                pe.drain().then_inc(stream.used, 1)

                        @block.scalar
                        def _(act):
                            with act.Fori(0, ROUNDS) as r:
                                for j in range(2):
                                    act.wait_ge(w1_done, 2 * r + (j + 1))
                                    act.wait_ge(hid_done, 2 * r + (j + 1))
                                    act.activation(silu1[:, j], ps[:, 2 * j].rearrange("p (f t) -> p f t", f=2), ACT.Silu).then_inc(silu_done, 1)

                        @block.vector
                        def _(dve):
                            for j in range(2):
                                dve.memset(hid[:, j], 0.0).then_inc(hid_done, 1)
                            for b in range(4):
                                dve.memset(acc[:, b // 2, b % 2 * PANEL:(b % 2 + 1) * PANEL], 0.0).then_inc(acc_done, 1)
                            dve.wait_ge(hid_done, 2)
                            with dve.Fori(0, ROUNDS) as r:
                                for j in range(2):
                                    dve.wait_ge(w3_done, 2 * r + (j + 1))
                                    dve.wait_ge(silu_done, 2 * r + (j + 1))
                                    dve.tensor_tensor(hid[:, j], silu1[:, j], ps[:, 2 * j + 1].rearrange("p (f t) -> p f t", f=2),
                                                      ALU.mult).then_inc(hid_done, 1)
                                for j in range(2):
                                    for b in range(4):
                                        t, c = b // 2, b % 2
                                        part = acc[:, t, c * PANEL:(c + 1) * PANEL]
                                        dve.wait_ge(acc_done, 8 * r + (4 * j + b + 1))
                                        dve.wait_ge(down_done, 8 * r + (4 * j + b + 1))
                                        dve.scalar_tensor_tensor(out=part, in0=ps[:, 4 + b], scalar=gates_e[:, t, bass.ds(2 * r + j, 1)], in1=part,
                                                                 op0=ALU.mult, op1=ALU.add).then_inc(acc_done, 1)

                with ExitStack() as scope:
                    grow = sb(scope, "grow3", [P, D])
                    sqr = sb(scope, "sqr3", [P, D])
                    ssem = stage_sems(scope, "final_")
                    loaded, steps, squares, std = (ssem(n) for n in ("loaded", "steps", "squares", "std"))
                    with nc.Block() as block:
                        @block.sync
                        def _(sp):
                            sp.dma_start(grow[:, :], row_bcast(w["final_norm_g"])).then_inc(loaded, 16)

                        @block.vector
                        def _(dve):
                            for t in range(TT):
                                dve.tensor_tensor(acc[:, t], acc[:, t], mods[:, 3], ALU.mult).then_inc(steps, 1)
                                dve.wait_ge(steps, 2 * t + 1)
                                dve.tensor_tensor(xs[:, t], xs[:, t], acc[:, t], ALU.add).then_inc(steps, 1)
                            dve.wait_ge(squares, TT)
                            dve.tensor_scalar(stat[:, 2:4], stat[:, 0:2], 1.0 / D, EPS, ALU.mult, ALU.add).then_inc(steps, 1)
                            dve.wait_ge(std, 1)
                            dve.reciprocal(stat[:, 4:6], stat[:, 2:4]).then_inc(steps, 1)
                            dve.wait_ge(steps, 2 * TT + 2)
                            dve.wait_ge(loaded, 16)
                            for t in range(TT):
                                dve.scalar_tensor_tensor(out=xs[:, t], in0=xs[:, t], scalar=stat[:, 4 + t:5 + t], in1=grow[:, :],
                                                         op0=ALU.mult, op1=ALU.mult)

                        @block.scalar
                        def _(act):
                            for t in range(TT):
                                act.wait_ge(steps, 2 * t + 2)
                                if t:
                                    act.wait_ge(squares, t)
                                act.activation(sqr[:, :], xs[:, t], ACT.Square, accum_out=stat[:, t:t + 1]).then_inc(squares, 1)
                            act.wait_ge(steps, 2 * TT + 1)
                            act.activation(stat[:, 2:4], stat[:, 2:4], ACT.Sqrt).then_inc(std, 1)

        with ExitStack() as second:
            hT = sb(second, "hT", [P, KT, 2 * L])
            gate1 = sb(second, "gate1", [P, D])
            rows2 = second.enter_context(ExitStack())
            m2x = sb(rows2, "m2x", [P, 2, 3, D])
            m2c = sb(rows2, "m2c", [P, 2, 3, D])
            with ExitStack() as scope:
                def loads(sp, loaded):
                    for layer in range(2):
                        for m in (m2x, m2c):
                            sp.dma_start(m[:, layer].rearrange("p r d -> p (r d)"), row_bcast(w["b_ada_2"][layer])).then_inc(loaded, 16)

                def row(m, i):
                    return m[:, i // 6, i % 6 // 2, i % 2 * PANEL:(i % 2 + 1) * PANEL]

                ada_block("ada2", ADA2, 12, cact[:, 2], cact[:, 3], lambda i: row(m2x, i), lambda i: row(m2c, i) if i < 10 else None,
                          loads, 4, AB_IN + RING, scope)

            cs = sb(rows2, "cs2", [P, TT, D])

            def modulate_block(name, layer, load_ctx):
                with ExitStack() as scope:
                    hx = sb(scope, f"{name}_hx", [P, TT, D])
                    hc = sb(scope, f"{name}_hc", [P, TT, D])
                    ssem = stage_sems(scope, f"{name}_")
                    loaded, x_step, c_step, turned, moved_a, moved_v = (ssem(n) for n in ("loaded", "x_step", "c_step", "turned", "moved_a", "moved_v"))


                    with nc.Block() as block:
                        @block.sync
                        def _(sp):
                            if load_ctx:
                                sp.dma_start(cs[:, :, :], w["ctx_2"][0].rearrange("(t p) d -> p t d", p=P)).then_inc(loaded, 16)

                        @block.vector
                        def _(dve):
                            for t in range(TT):
                                dve.scalar_tensor_tensor(out=hx[:, t], in0=m2x[:, layer, 1], scalar=1.0, in1=xs[:, t],
                                                         op0=ALU.add, op1=ALU.mult).then_inc(x_step, 1)
                                dve.wait_ge(x_step, 2 * t + 1)
                                dve.tensor_tensor(hx[:, t], hx[:, t], m2x[:, layer, 0], ALU.add).then_inc(x_step, 1)
                            for kt in range(1, KT, 2):
                                dve.wait_ge(turned, kt + 1)
                                dve.tensor_copy(hT[:, kt], ps[:, kt]).then_inc(moved_v, 1)

                        @block.gpsimd
                        def _(pool):
                            link = chained(pool, c_step)
                            link(pool.tensor_scalar(m2c[:, layer, 1], m2c[:, layer, 1], 1.0, None, ALU.add))
                            if load_ctx:
                                pool.wait_ge(loaded, 16)
                            for t in range(TT):
                                link(pool.tensor_tensor(hc[:, t], cs[:, t], m2c[:, layer, 1], ALU.mult))
                                link(pool.tensor_tensor(hc[:, t], hc[:, t], m2c[:, layer, 0], ALU.add))

                        @block.scalar
                        def _(act):
                            for kt in range(0, KT, 2):
                                act.wait_ge(turned, kt + 1)
                                act.copy(hT[:, kt], ps[:, kt]).then_inc(moved_a, 1)

                        @block.tensor
                        def _(pe):
                            pe.wait_ge(x_step, 2 * TT)
                            pe.wait_ge(c_step, 2 * TT + 1)
                            for kt in range(KT):
                                transpose_in(pe, kt, lambda i: (hc, hx)[i // TT][:, i % TT, kt * P:(kt + 1) * P], 2 * TT).then_inc(turned, 1)

            def residual_block(name, layer, panel, lhs, targets, upto, store=None):
                with ExitStack() as scope:
                    n_t = len(targets)
                    gated = sb(scope, f"{name}_gated", [P, 2, PANEL])
                    bn = sb(scope, f"{name}_bn", [P, n_t, 2, 6])
                    mv = sb(scope, f"{name}_mv", [P, n_t, 2])
                    ln_rows = sb(scope, f"{name}_ln", [P, 2, D])
                    ssem = stage_sems(scope, f"{name}_")
                    proj, scaled, added, stats, std, steps, mv_done, loaded, normed, stored = (
                        ssem(n) for n in ("proj", "scaled", "added", "stats", "std", "steps", "mv_done", "loaded", "normed", "stored"))
                    with nc.Block() as block:
                        @block.sync
                        def _(sp):
                            for i, n in enumerate(("ln_g_2", "ln_b_2")):
                                sp.dma_start(ln_rows[:, i], row_bcast(w[n][layer])).then_inc(loaded, 16)
                            stream.issue(sp, upto)
                            if store:
                                for t in range(n_t):
                                    sp.wait_ge(normed, t + 1)
                                    sp.dma_start(store(t), targets[t][0]).then_inc(stored, 16)
                                sp.wait_ge(stored, 16 * n_t)

                        @block.tensor
                        def _(pe):
                            for i in range(2 * n_t):
                                n, t = panel + i // n_t, i % n_t
                                if t == 0:
                                    pe.wait_ge(*stream.arrive(n))
                                if i >= 8:
                                    pe.wait_ge(scaled, i - 7)
                                for kt in range(KT):
                                    ins = pe.matmul(ps[:, i % 8], lhs(t, kt), stream.slot(n)[:, kt], start=(kt == 0), stop=(kt == KT - 1))
                                ins.then_inc(proj, 1)
                                if t == n_t - 1:
                                    pe.drain().then_inc(stream.used, 1)

                        @block.vector
                        def _(dve):
                            for i in range(2 * n_t):
                                half, t = i // n_t, i % n_t
                                cols = slice(half * PANEL, half * PANEL + PANEL)
                                x, g = targets[t]
                                dve.wait_ge(proj, i + 1)
                                dve.tensor_tensor(gated[:, i % 2], ps[:, i % 8], g[:, cols], ALU.mult).then_inc(scaled, 1)
                                dve.wait_ge(scaled, i + 1)
                                dve.scalar_tensor_tensor(out=x[:, cols], in0=x[:, cols], scalar=DEEPNORM_ALPHA, in1=gated[:, i % 2],
                                                         op0=ALU.mult, op1=ALU.add).then_inc(added, 1)
                                dve.wait_ge(added, i + 1)
                                dve.bn_stats(bn[:, t, half], x[:, cols]).then_inc(stats, 1)
                            dve.wait_ge(stats, 2 * n_t)
                            for t in range(n_t):
                                dve.bn_aggr(mv[:, t], bn[:, t]).then_inc(mv_done, 1)
                            dve.wait_ge(std, 1)
                            dve.reciprocal(mv[:, :, 1], mv[:, :, 1]).then_inc(mv_done, 1)
                            dve.wait_ge(mv_done, n_t + 1)
                            dve.wait_ge(loaded, 32)
                            for t in range(n_t):
                                x = targets[t][0]
                                dve.tensor_scalar(x, x, mv[:, t, 0:1], mv[:, t, 1:2], ALU.subtract, ALU.mult).then_inc(steps, 1)
                                dve.wait_ge(steps, 2 * t + 1)
                                dve.tensor_tensor(x, x, ln_rows[:, 0], ALU.mult).then_inc(steps, 1)
                                dve.wait_ge(steps, 2 * t + 2)
                                dve.tensor_tensor(x, x, ln_rows[:, 1], ALU.add).then_inc(normed, 1)

                        @block.scalar
                        def _(act):
                            act.wait_ge(mv_done, n_t)
                            act.activation(mv[:, :, 1], mv[:, :, 1], ACT.Sqrt, bias=eps[:, 1:2]).then_inc(std, 1)

            modulate_block("mod0", 0, True)
            with ExitStack() as ab:
                big = sb(ab, "big", [P, const_dram.shape[1] - small])

                def bigc(name):
                    at, n = parts[name]
                    return big[:, at - small:at - small + n]

                AT = 4
                qa = sb(ab, "qa", [P, AT, 2 * L])
                ka = sb(ab, "ka", [P, KV_HEADS, 2 * L])
                kraw = sb(ab, "kraw", [P, 1, 2 * L])
                va = sb(ab, "va", [P, 2 * TT, KV_HEADS, 2, A_DIM])
                sga = sb(ab, "sga", [P, AT, 2 * L])
                sgb = sb(ab, "sgb", [P, AT, 2 * L])
                bg = sb(ab, "bg", [P, AT, 2 * L])
                up = sb(ab, "up", [P, AT, 2, L + 2])
                taps_row = sb(ab, "taps_row2", [3, AT * P])
                taps = sb(ab, "taps2", [P, AT, 3])
                sink = sb(ab, "sink", [P, A_HEADS])
                catT = hT
                seqs = lambda a: a.rearrange("p (s t) -> p s t", s=2)
                pieces = [("q", j) for j in range(AT)] + [("k", 0), ("v", 0)]
                pieces += [(n, j) for n in ("ga", "xb", "bg", "cg", "gb") for j in range(AT)]
                first_tile = {"q": 0, "k": 4, "v": 5, "ga": 6, "xb": 10, "bg": 14, "cg": 18, "gb": 22}
                with ExitStack() as scope:
                    ssem = stage_sems(scope, "ab_")
                    loaded, turned, taps_done, zeroed, proj, moved_a, moved_v = (
                        ssem(n) for n in ("loaded", "turned", "taps_done", "zeroed", "proj", "moved_a", "moved_v"))
                    on_dve = [n == "cg" for n, _ in pieces]
                    count = lambda i: sum(1 for m in range(i + 1) if on_dve[m] == on_dve[i])
                    BANKS = 7
                    with nc.Block() as block:
                        @block.sync
                        def _(sp):
                            sp.dma_start(big[:, :], const_dram[:, small:]).then_inc(loaded, 16)
                            sp.dma_start(taps_row[:, :], w["conv_ab_2"][0]).then_inc(loaded, 16)
                            sp.dma_start(sink[:, :], row_bcast(w["sink_ab_2"][0])).then_inc(loaded, 16)
                            stream.issue(sp, AB_OUT + RING)

                        @block.gpsimd
                        def _(pool):
                            pool.memset(up[:, :, :, :], 0.0).then_inc(zeroed, 1)

                        @block.tensor
                        def _(pe):
                            pe.wait_ge(loaded, 48)
                            for j in range(AT):
                                ins = pe.transpose(ps[:, 7, 3 * j:3 * j + 3], taps_row[:, j * P:(j + 1) * P], ident[0:3, 0:3])
                            ins.then_inc(turned, 1)
                            last_panel = -1
                            for i, (name, j) in enumerate(pieces):
                                tile = first_tile[name] + j
                                n, c0 = AB_IN + tile // 4, tile % 4 * P
                                if tile // 4 != last_panel:
                                    if last_panel >= 0:
                                        pe.drain().then_inc(stream.used, 1)
                                    pe.wait_ge(*stream.arrive(n))
                                    last_panel = tile // 4
                                if i >= BANKS:
                                    pe.wait_ge(moved_v if on_dve[i - BANKS] else moved_a, count(i - BANKS))
                                bank, slot = ps[:, i % BANKS], stream.slot(n)
                                if name == "v":
                                    for t in range(2 * TT):
                                        for kt in range(KT):
                                            ins = pe.matmul(bank[:, t * P:(t + 1) * P], hT[:, kt, t * P:(t + 1) * P], slot[:, kt, c0:c0 + P],
                                                            start=(kt == 0), stop=(kt == KT - 1))
                                else:
                                    for kt in range(KT):
                                        ins = pe.matmul(bank, slot[:, kt, c0:c0 + P], hT[:, kt], start=(kt == 0), stop=(kt == KT - 1))
                                ins.then_inc(proj, 1)
                            pe.drain().then_inc(stream.used, 1)

                        @block.scalar
                        def _(act):
                            act.wait_ge(zeroed, 1)
                            for i, (name, j) in enumerate(pieces):
                                if on_dve[i]:
                                    continue
                                bank = ps[:, i % BANKS]
                                act.wait_ge(proj, i + 1)
                                if name == "v":
                                    heads = bank.rearrange("p (t g d) -> p (t g) d", t=2 * TT, g=KV_HEADS)
                                    ins = act.copy(va[:, :, :, :, :].rearrange("p t g c d -> p (t g) c d"),
                                                   heads.unsqueeze(2).to_broadcast([P, 2 * TT * KV_HEADS, 2, A_DIM]))
                                elif name == "xb":
                                    ins = act.copy(up[:, j, :, 1:1 + L], seqs(bank))
                                elif name in ("ga", "gb"):
                                    ins = act.activation((sga if name == "ga" else sgb)[:, j], bank, ACT.Silu)
                                else:
                                    ins = act.copy({"q": qa, "k": kraw, "bg": bg}[name][:, j], bank)
                                ins.then_inc(moved_a, 1)

                        @block.vector
                        def _(dve):
                            dve.wait_ge(turned, 1)
                            dve.tensor_copy(taps[:, :, :], ps[:, 7, 0:3 * AT].rearrange("p (j c) -> p j c", c=3)).then_inc(taps_done, 1)
                            for i, (name, j) in enumerate(pieces):
                                if on_dve[i]:
                                    part = up[:, j, :, 1:1 + L]
                                    dve.wait_ge(proj, i + 1)
                                    dve.wait_ge(moved_a, count(pieces.index(("xb", j))))
                                    dve.tensor_tensor(part, seqs(ps[:, i % BANKS]), part, ALU.mult).then_inc(moved_v, 1)

                with ExitStack() as scope:
                    rot_sin = sb(scope, "rot_sin", [P, 2, L])
                    conv = lambda j: seqs(catT[:, AT + j])
                    ssem = stage_sems(scope, "rope_")
                    rotated, sin_done, cos_done, rope_done, conv_step, gate_done, doubled, k_moved = (
                        ssem(n) for n in ("rotated", "sin_done", "cos_done", "rope_done", "conv_step", "gate_done", "doubled", "k_moved"))
                    items = [qa[:, j, L:] for j in range(AT)] + [ka[:, g, L:] for g in range(KV_HEADS)]
                    with nc.Block() as block:
                        @block.scalar
                        def _(act):
                            for g in range(KV_HEADS):
                                act.wait_ge(doubled, g + 1)
                                act.copy(ka[:, g], ps[:, 6 + g]).then_inc(k_moved, 1)

                        @block.tensor
                        def _(pe):
                            for g in range(KV_HEADS):
                                pe.matmul(ps[:, 6 + g], bigc("kdup").rearrange("p (g m) -> p g m", g=KV_HEADS)[:, g], kraw[:, 0],
                                          start=True, stop=True).then_inc(doubled, 1)
                            for i, a in enumerate(items):
                                if i == AT:
                                    pe.wait_ge(k_moved, KV_HEADS)
                                pe.matmul(ps[:, i, 0:L], bigc("rot"), a, start=True, stop=True).then_inc(rotated, 1)

                        @block.vector
                        def _(dve):
                            for i, a in enumerate(items):
                                dve.wait_ge(rotated, i + 1)
                                if i >= 2:
                                    dve.wait_ge(rope_done, i - 1)
                                dve.tensor_tensor(rot_sin[:, i % 2], ps[:, i, 0:L], bigc("sin"), ALU.mult).then_inc(sin_done, 1)
                                dve.tensor_tensor(a, a, bigc("cos"), ALU.mult).then_inc(cos_done, 1)
                                dve.wait_ge(sin_done, i + 1)
                                dve.wait_ge(cos_done, i + 1)
                                dve.tensor_tensor(a, a, rot_sin[:, i % 2], ALU.add).then_inc(rope_done, 1)
                            link = chained(dve, conv_step)
                            for j in range(AT):
                                for c in range(3):
                                    src = up[:, j, :, c:c + L]
                                    if c == 0:
                                        link(dve.tensor_scalar(conv(j), src, taps[:, j, 0:1], None, ALU.mult))
                                    else:
                                        link(dve.scalar_tensor_tensor(out=conv(j), in0=src, scalar=taps[:, j, c:c + 1], in1=conv(j),
                                                                      op0=ALU.mult, op1=ALU.add))

                        @block.gpsimd
                        def _(pool):
                            for j in range(AT):
                                pool.tensor_tensor(bg[:, j], bg[:, j], sgb[:, j], ALU.mult).then_inc(gate_done, 1)
                            for j in range(AT):
                                pool.wait_ge(gate_done, j + 1)
                                pool.wait_ge(conv_step, 3 * j + 3)
                                pool.tensor_tensor(catT[:, AT + j], catT[:, AT + j], bg[:, j], ALU.mult)

                with ExitStack() as scope:
                    BUF = 3
                    s_buf = up[:, :, :, :].rearrange("p j s t -> p (j s t)")[:, 0:BUF * 2 * L].rearrange("p (b k) -> p b k", b=BUF)
                    pT = bg[:, 0:BUF]
                    small_t = sb(scope, "softmax_rows", [P, 2 * TT * A_HEADS, 6])
                    ssem = stage_sems(scope, "att_")
                    scored, biased, maxed, summed, sunk, inverted, scaled, turned, moved, outed, gated, row_step = (
                        ssem(n) for n in ("scored", "biased", "maxed", "summed", "sunk", "inverted", "scaled", "turned", "moved", "outed", "gated",
                                          "row_step"))
                    work = [(t, h) for t in range(2 * TT) for h in range(A_HEADS)]
                    n_keys = lambda t: 2 * L if t >= TT else L
                    with nc.Block() as block:
                        @block.tensor
                        def _(pe):
                            def scores(i):
                                t, h = work[i]
                                at = slice(h % 2 * A_DIM, h % 2 * A_DIM + A_DIM)
                                if i >= 2:
                                    pe.wait_ge(biased, i - 1)
                                pe.matmul(ps[:, i % 2, 0:n_keys(t)], qa[at, h // 2, t * P:(t + 1) * P], ka[at, h // 4, 0:n_keys(t)],
                                          start=True, stop=True).then_inc(scored, 1)

                            def turn(i):
                                t, h = work[i]
                                pe.wait_ge(scaled, i + 1)
                                if i >= 2:
                                    pe.wait_ge(moved, i - 1)
                                transpose_in(pe, 2 + i % 2, lambda m: s_buf[:, i % BUF, m * P:(m + 1) * P], n_keys(t) // P).then_inc(turned, 1)

                            def outputs(i):
                                t, h = work[i]
                                pe.wait_ge(moved, i + 1)
                                if i >= 2:
                                    pe.wait_ge(gated, i - 1)
                                n = n_keys(t) // P
                                for m in range(n):
                                    ins = pe.matmul(ps[:, 4 + i % 2, 0:P], va[:, m, h // 4].rearrange("p c d -> p (c d)"), pT[:, i % BUF, m * P:(m + 1) * P],
                                                    start=(m == 0), stop=(m == n - 1))
                                ins.then_inc(outed, 1)

                            N = len(work)
                            for i in range(N + 3):
                                if i < N:
                                    scores(i)
                                if 2 <= i < N + 2:
                                    turn(i - 2)
                                if i >= 3:
                                    outputs(i - 3)

                        @block.vector
                        def _(dve):
                            def soft(i):
                                t, h = work[i]
                                keys, row = n_keys(t), small_t[:, i]
                                dve.wait_ge(scored, i + 1)
                                if i >= BUF:
                                    dve.wait_ge(turned, i - BUF + 1)
                                s = s_buf[:, i % BUF, 0:keys]
                                if t >= TT:
                                    win = bigc("win").rearrange("p (t k) -> p t k", t=TT)[:, t - TT]
                                    dve.scalar_tensor_tensor(out=s, in0=ps[:, i % 2, 0:keys], scalar=A_DIM ** -0.5, in1=win,
                                                             op0=ALU.mult, op1=ALU.add).then_inc(biased, 1)
                                else:
                                    dve.tensor_scalar(s, ps[:, i % 2, 0:keys], A_DIM ** -0.5, None, ALU.mult).then_inc(biased, 1)
                                dve.wait_ge(biased, i + 1)
                                dve.tensor_reduce(row[:, 0:1], s, AX.X, ALU.max).then_inc(row_step, 1)
                                dve.wait_ge(row_step, 2 * i + 1)
                                dve.tensor_tensor(row[:, 0:1], row[:, 0:1], sink[:, h:h + 1], ALU.max).then_inc(row_step, 1)
                                dve.wait_ge(row_step, 2 * i + 2)
                                dve.tensor_scalar(row[:, 1:2], row[:, 0:1], -1.0, None, ALU.mult).then_inc(maxed, 1)

                            def invert(i):
                                row = small_t[:, i]
                                dve.wait_ge(summed, i + 1)
                                dve.wait_ge(sunk, i + 1)
                                dve.tensor_tensor(row[:, 4:5], row[:, 2:3], row[:, 3:4], ALU.add).then_inc(inverted, 1)
                                dve.wait_ge(inverted, 2 * i + 1)
                                dve.reciprocal(row[:, 4:5], row[:, 4:5]).then_inc(inverted, 1)

                            def gate(i):
                                t, h = work[i]
                                at = slice(h % 2 * A_DIM, h % 2 * A_DIM + A_DIM)
                                dve.wait_ge(outed, i + 1)
                                dve.tensor_tensor(catT[at, h // 2, t * P:(t + 1) * P], ps[at, 4 + i % 2, 0:P], sga[at, h // 2, t * P:(t + 1) * P],
                                                  ALU.mult).then_inc(gated, 1)

                            N = len(work)
                            for i in range(N + 3):
                                if i < N:
                                    soft(i)
                                if 1 <= i < N + 1:
                                    invert(i - 1)
                                if i >= 3:
                                    gate(i - 3)

                        @block.scalar
                        def _(act):
                            def exps(i):
                                t, h = work[i]
                                s, row = s_buf[:, i % BUF, 0:n_keys(t)], small_t[:, i]
                                act.wait_ge(maxed, i + 1)
                                act.activation(s, s, ACT.Exp, bias=row[:, 1:2], accum_out=row[:, 2:3]).then_inc(summed, 1)
                                act.activation(row[:, 3:4], sink[:, h:h + 1], ACT.Exp, bias=row[:, 1:2]).then_inc(sunk, 1)

                            def move(i):
                                t, h = work[i]
                                act.wait_ge(turned, i + 1)
                                if i >= BUF:
                                    act.wait_ge(outed, i - BUF + 1)
                                act.copy(pT[:, i % BUF, 0:n_keys(t)], ps[:, 2 + i % 2, 0:n_keys(t)]).then_inc(moved, 1)

                            N = len(work)
                            for i in range(N + 2):
                                if i < N:
                                    exps(i)
                                if i >= 2:
                                    move(i - 2)

                        @block.gpsimd
                        def _(pool):
                            for i, (t, h) in enumerate(work):
                                s = s_buf[:, i % BUF, 0:n_keys(t)]
                                pool.wait_ge(inverted, 2 * i + 2)
                                pool.wait_ge(summed, i + 1)
                                pool.tensor_scalar(s, s, small_t[:, i, 4:5], None, ALU.mult).then_inc(scaled, 1)
            targets = [(cs[:, t], m2c[:, 0, 2]) for t in range(TT)] + [(xs[:, t], m2x[:, 0, 2]) for t in range(TT)]
            residual_block("res0", 0, AB_OUT, lambda i, kt: hT[:, kt, i * P:(i + 1) * P], targets, C_IN + RING)

            modulate_block("mod1", 1, False)
            with nc.Block() as block:
                @block.vector
                def _(dve):
                    dve.tensor_copy(gate1[:, :], m2x[:, 1, 2])
            rows2.close()
            with ExitStack() as rec:
                qT = sb(rec, "cqT", [P, H, L])
                kT = [sb(rec, f"ckT{d}", [P, H, 2 * L]) for d in range(2)]
                bT = [sb(rec, f"cbT{d}", [P, H, 2 * L]) for d in range(2)]
                vtok = sb(rec, "cvtok", [P, 2 * TT, D])
                state = sb(rec, "cstate", [P, 2 * H, P])
                sg = sb(rec, "csg", [P, TT, D])
                otok = hT[:, 0:KT // 2].rearrange("p k (t c) -> p (k t c)", t=2).rearrange("p (t d) -> p t d", t=TT)
                with ExitStack() as scope:
                    soft = sb(scope, "soft", [P, 2, 2 * L])
                    ssem = stage_sems(scope, "cproj_")
                    proj, moved_a, moved_v, sig = (ssem(n) for n in ("proj", "moved_a", "moved_v", "sig"))
                    abs_done, exp_done, ln_done, logf_done, scan_done = (ssem(n) for n in ("abs_done", "exp_done", "ln_done", "logf_done", "scan_done"))
                    pieces = [("q", j) for j in range(H)] + [("zf", j) for j in range(H)] + [("zb", j) for j in range(H)]
                    pieces += [("i", j) for j in range(2 * 2 * TT)] + [("g", j) for j in range(2 * TT)]
                    on_dve = [n in ("zf", "zb") or (n == "i" and j % 2 == 1) for n, j in pieces]
                    count = lambda i: sum(1 for m in range(i + 1) if on_dve[m] == on_dve[i])
                    n_sig = lambda i: sum(1 for n, _ in pieces[:i + 1] if n in ("zf", "zb"))
                    with nc.Block() as block:
                        @block.sync
                        def _(sp):
                            stream.issue(sp, END)

                        @block.tensor
                        def _(pe):
                            for i, (name, j) in enumerate(pieces):
                                of = TT if name == "g" else 4
                                first_of, last_of = j % of == 0, j % of == of - 1
                                n = C_IN + {"q": 0, "zf": 2, "zb": 4, "i": 6, "g": 8}[name] + j // of
                                if first_of:
                                    pe.wait_ge(*stream.arrive(n))
                                if i >= 8:
                                    pe.wait_ge(moved_v if on_dve[i - 8] else moved_a, count(i - 8))
                                bank, slot = ps[:, i % 8], stream.slot(n)
                                for kt in range(KT):
                                    edge = dict(start=(kt == 0), stop=(kt == KT - 1))
                                    if name == "i":
                                        ins = pe.matmul(bank, hT[:, kt, j % 4 * P:(j % 4 + 1) * P], slot[:, kt], **edge)
                                    elif name == "g":
                                        ins = pe.matmul(bank, hT[:, kt, L + j % TT * P:L + (j % TT + 1) * P], slot[:, kt], **edge)
                                    elif name == "q":
                                        ins = pe.matmul(bank[:, 0:L], slot[:, kt, j % 4 * P:(j % 4 + 1) * P], hT[:, kt, L:], **edge)
                                    else:
                                        ins = pe.matmul(bank, slot[:, kt, j % 4 * P:(j % 4 + 1) * P], hT[:, kt], **edge)
                                ins.then_inc(proj, 1)
                                if last_of:
                                    pe.drain().then_inc(stream.used, 1)

                        @block.scalar
                        def _(act):
                            for i, (name, j) in enumerate(pieces):
                                if name == "i" and on_dve[i]:
                                    continue
                                bank = ps[:, i % 8]
                                act.wait_ge(proj, i + 1)
                                if name == "q":
                                    act.activation(qT[:, j], bank[:, 0:L], ACT.Silu).then_inc(moved_a, 1)
                                elif name == "i":
                                    act.copy(vtok[:, j % 4, j // 4 * PANEL:(j // 4 + 1) * PANEL], bank).then_inc(moved_a, 1)
                                elif name == "g":
                                    act.activation(sg[:, j % TT, j // TT * PANEL:(j // TT + 1) * PANEL], bank, ACT.Silu).then_inc(moved_a, 1)
                                else:
                                    act.activation(kT[name == "zb"][:, j], bank, ACT.Sigmoid, scale=-1.0).then_inc(sig, 1)
                            for m in range(2 * H):
                                z, part = bT[m // H][:, m % H], soft[:, m % 2]
                                act.wait_ge(moved_v, m + 1)
                                if m >= 2:
                                    act.wait_ge(logf_done, m - 1)
                                act.activation(part, z, ACT.Abs).then_inc(abs_done, 1)
                                act.wait_ge(abs_done, m + 1)
                                act.activation(part, part, ACT.Exp, scale=-1.0).then_inc(exp_done, 1)
                                act.wait_ge(exp_done, m + 1)
                                act.activation(part, part, ACT.Ln, bias=1.0).then_inc(ln_done, 1)

                        @block.vector
                        def _(dve):
                            for i, (name, j) in enumerate(pieces):
                                if not on_dve[i]:
                                    continue
                                dve.wait_ge(proj, i + 1)
                                if name == "i":
                                    dve.tensor_copy(vtok[:, j % 4, j // 4 * PANEL:(j // 4 + 1) * PANEL], ps[:, i % 8]).then_inc(moved_v, 1)
                                else:
                                    dve.wait_ge(sig, n_sig(i))
                                    dve.tensor_copy(bT[name == "zb"][:, j], ps[:, i % 8]).then_inc(moved_v, 1)
                            dve.wait_ge(moved_a, H)
                            dve.tensor_scalar(qT[:, :, :], qT[:, :, :], P ** -0.5, None, ALU.mult)
                            for m in range(2 * H):
                                d, h = m // H, m % H
                                dve.wait_ge(ln_done, m + 1)
                                dve.scalar_tensor_tensor(out=bT[d][:, h], in0=bT[d][:, h], scalar=0.0, in1=soft[:, m % 2],
                                                         op0=ALU.min, op1=ALU.subtract).then_inc(logf_done, 1)
                                dve.wait_ge(logf_done, m + 1)
                                for t in range(2 * TT):
                                    chunk = bT[d][:, h, t * P:(t + 1) * P]
                                    if d:
                                        chunk = chunk[:, ::-1]
                                    dve.tensor_tensor_scan(chunk, ones, chunk, 0.0, ALU.mult, ALU.add)

                with ExitStack() as scope:
                    ksf = sb(scope, "ksf", [P, H, P])
                    kst = sb(scope, "kst", [P, H, P])
                    scT = sb(scope, "scT", [P, H, P])
                    lb = sb(scope, "lb", [P, 2, H, P])
                    dn = sb(scope, "dn", [P, H])
                    for step in range(2 * TT):
                        on_x, more = step >= TT, step < 2 * TT - 1
                        for d in range(2):
                            t = step ^ d
                            chunk = lambda a: a[:, :, t * P:(t + 1) * P]
                            b, k = chunk(bT[d]), chunk(kT[d])
                            q = qT[:, :, (t - TT) * P:(t - TT + 1) * P] if on_x else None
                            S = state[:, d * H:(d + 1) * H]
                            last = 0 if d else P - 1
                            k_side, q_side = d, 1 - d
                            v = lambda h: vtok[:, t, h * P:(h + 1) * P]
                            two = lambda bank: ps[:, bank:bank + 2].rearrange("p b (h c) -> p (b h) c", h=4)

                            def border(lv):
                                return half_cols(b, lv, k_side)[:, :, :, (0 if d else (1 << lv) - 1)]

                            with ExitStack() as inner:
                                ssem = stage_sems(inner, f"rec{step}{d}_")
                                (ks_arg, ks_exp, ks_done, kst_turned, kst_moved, q_exp, q_done, diag, diag_done, arg, lexp, lk, lq, level, put_done,
                                 o_done, s_done, dn_done) = (ssem(n) for n in (
                                     "ks_arg", "ks_exp", "ks_done", "kst_turned", "kst_moved", "q_exp", "q_done", "diag", "diag_done", "arg", "lexp",
                                     "lk", "lq", "level", "put_done", "o_done", "s_done", "dn_done"))
                                with nc.Block() as block:
                                    @block.vector
                                    def _(dve):
                                        if more:
                                            dve.tensor_tensor(ksf[:, :, :], b[:, :, last:last + 1].to_broadcast([P, H, P]), b, ALU.subtract).then_inc(ks_arg, 1)
                                        if on_x:
                                            dve.wait_ge(diag, 1)
                                            dve.tensor_tensor(scT[:, :, :], two(0), ident.unsqueeze(1).to_broadcast([P, H, P]), ALU.mult).then_inc(diag_done, 1)

                                            def args(lv):
                                                if lv >= 2:
                                                    dve.wait_ge(level, lv - 1)
                                                n, j = P >> (lv + 1), 1 << lv
                                                at = border(lv).unsqueeze(3).to_broadcast([P, H, n, j])
                                                dve.tensor_tensor(half_cols(lb[:, lv % 2], lv, k_side), at, half_cols(b, lv, k_side), ALU.subtract)
                                                dve.tensor_tensor(half_cols(lb[:, lv % 2], lv, q_side), half_cols(b, lv, q_side), at,
                                                                  ALU.subtract).then_inc(arg, 1)

                                            def times_q(lv):
                                                part = half_cols(lb[:, lv % 2], lv, q_side)
                                                dve.wait_ge(lexp, lv + 1)
                                                dve.tensor_tensor(part, part, half_cols(q, lv, q_side), ALU.mult).then_inc(lq, 1)

                                            def put(lv):
                                                n, j = P >> (lv + 1), 1 << lv
                                                mask = lev[:, 1 - d, lv].unsqueeze(1).to_broadcast([P, H, P // 2]).bitcast(I32)
                                                dve.wait_ge(level, lv + 1)
                                                if lv == 0:
                                                    dve.wait_ge(diag_done, 1)
                                                else:
                                                    dve.wait_ge(put_done, lv)
                                                dve.copy_predicated(half_cols(scT[:, :, :], lv, q_side), packed_cols(mask, lv),
                                                                    packed_cols(ps[:, 2 + lv % 2].rearrange("p (h c) -> p h c", h=H), lv)).then_inc(put_done, 1)

                                            args(0)
                                            args(1)
                                            for lv in range(LEVELS):
                                                times_q(lv)
                                                if lv >= 1:
                                                    put(lv - 1)
                                                if lv + 2 < LEVELS:
                                                    args(lv + 2)
                                            put(LEVELS - 1)
                                            o = otok[:, t - TT].rearrange("p (h c) -> p h c", h=H)
                                            dve.wait_ge(o_done, 1)
                                            if step == TT:
                                                dve.tensor_copy(o, two(6))
                                            else:
                                                dve.tensor_tensor(o, two(6), o, ALU.add)
                                        if more:
                                            dve.wait_ge(s_done, 1)
                                            dve.wait_ge(dn_done, 1)
                                            for h in range(H):
                                                part = ps[:, 4 + h // 4, h % 4 * P:(h % 4 + 1) * P]
                                                if step:
                                                    dve.scalar_tensor_tensor(out=S[:, h], in0=S[:, h], scalar=dn[:, h:h + 1], in1=part, op0=ALU.mult, op1=ALU.add)
                                                else:
                                                    dve.tensor_copy(S[:, h], part)

                                    @block.scalar
                                    def _(act):
                                        act.activation(dn[:, :], b[:, :, last], ACT.Exp).then_inc(dn_done, 1)
                                        if more:
                                            act.wait_ge(ks_arg, 1)
                                            act.activation(ksf[:, :, :], ksf[:, :, :], ACT.Exp).then_inc(ks_exp, 1)
                                        if on_x:
                                            for lv in range(LEVELS):
                                                act.wait_ge(arg, lv + 1)
                                                act.activation(lb[:, lv % 2], lb[:, lv % 2], ACT.Exp).then_inc(lexp, 1)
                                        if more:
                                            act.wait_ge(kst_turned, 1)
                                            act.copy(kst[:, :, :], two(4)).then_inc(kst_moved, 1)
                                        if on_x:
                                            act.activation(ksf[:, :, :], b, ACT.Exp).then_inc(q_exp, 1)

                                    @block.gpsimd
                                    def _(pool):
                                        if more:
                                            pool.wait_ge(ks_exp, 1)
                                            pool.tensor_tensor(ksf[:, :, :], ksf[:, :, :], k, ALU.mult).then_inc(ks_done, 1)
                                        if on_x:
                                            for lv in range(LEVELS):
                                                part = half_cols(lb[:, lv % 2], lv, k_side)
                                                pool.wait_ge(lexp, lv + 1)
                                                pool.tensor_tensor(part, part, half_cols(k, lv, k_side), ALU.mult).then_inc(lk, 1)
                                            pool.wait_ge(q_exp, 1)
                                            pool.tensor_tensor(ksf[:, :, :], ksf[:, :, :], q, ALU.mult).then_inc(q_done, 1)

                                    @block.tensor
                                    def _(pe):
                                        if on_x:
                                            for h in range(H):
                                                ins = pe.matmul(ps[:, h // 4, h % 4 * P:(h % 4 + 1) * P], k[:, h], q[:, h], start=True, stop=True)
                                            ins.then_inc(diag, 1)
                                        if more:
                                            pe.wait_ge(ks_done, 1)
                                            transpose_in(pe, 4, lambda i: ksf[:, i], 4)
                                            transpose_in(pe, 5, lambda i: ksf[:, 4 + i], 4).then_inc(kst_turned, 1)
                                        if on_x:
                                            for lv in range(LEVELS):
                                                pe.wait_ge(lk, lv + 1)
                                                pe.wait_ge(lq, lv + 1)
                                                if lv >= 2:
                                                    pe.wait_ge(put_done, lv - 1)
                                                for h in range(H):
                                                    ins = pe.matmul(ps[:, 2 + lv % 2, 64 * h:64 * h + 64], lb[:, lv % 2, h],
                                                                    half_cols(lb[:, lv % 2, h], lv, q_side), start=True, stop=True)
                                                ins.then_inc(level, 1)
                                            pe.wait_ge(put_done, LEVELS)
                                            pe.wait_ge(q_done, 1)
                                            for h in range(H):
                                                bank = ps[:, 6 + h // 4, h % 4 * P:(h % 4 + 1) * P]
                                                pe.matmul(bank, ksf[:, h], S[:, h], start=True, stop=False)
                                                ins = pe.matmul(bank, scT[:, h], v(h), start=False, stop=True)
                                            ins.then_inc(o_done, 1)
                                        if more:
                                            pe.wait_ge(kst_moved, 1)
                                            for h in range(H):
                                                ins = pe.matmul(ps[:, 4 + h // 4, h % 4 * P:(h % 4 + 1) * P], kst[:, h], v(h), start=True, stop=True)
                                            ins.then_inc(s_done, 1)

                yT = hT[:, KT // 2:].rearrange("p k t -> p (k t)").rearrange("p (k t) -> p k t", k=KT)
                with ExitStack() as scope:
                    sq = sb(scope, "csq", [P, TT, D])
                    rms = sb(scope, "crms", [P, TT * H])
                    gn = sb(scope, "cgn", [P, P])
                    ssem = stage_sems(scope, "cout_")
                    loaded, squared, steps, std, scaled, gained, gated, turned, moved = (
                        ssem(n) for n in ("loaded", "squared", "steps", "std", "scaled", "gained", "gated", "turned", "moved"))
                    per_head = lambda a: a.rearrange("p t (h c) -> p (t h) c", h=H)
                    with nc.Block() as block:
                        @block.sync
                        def _(sp):
                            sp.dma_start(gn[:, :], row_bcast(w["gnorm_c_2"][0])).then_inc(loaded, 16)

                        @block.scalar
                        def _(act):
                            act.activation(sq[:, :, :], otok, ACT.Square).then_inc(squared, 1)
                            act.wait_ge(steps, 1)
                            act.activation(rms[:, :], rms[:, :], ACT.Sqrt, bias=eps[:, 0:1], scale=1.0 / P).then_inc(std, 1)
                            for b in range(4):
                                act.wait_ge(turned, b + 1)
                                act.copy(yT[:, 2 * b:2 * b + 2], ps[:, b].rearrange("p (k t) -> p k t", k=2)).then_inc(moved, 1)

                        @block.vector
                        def _(dve):
                            dve.wait_ge(squared, 1)
                            dve.tensor_reduce(rms[:, :], per_head(sq[:, :, :]), AX.X, ALU.add).then_inc(steps, 1)
                            dve.wait_ge(std, 1)
                            dve.reciprocal(rms[:, :], rms[:, :]).then_inc(steps, 1)
                            dve.wait_ge(steps, 2)
                            for t in range(TT):
                                o, r = otok[:, t].rearrange("p (h c) -> p h c", h=H), rms[:, t * H:(t + 1) * H]
                                dve.tensor_tensor(o, o, r.unsqueeze(2).to_broadcast([P, H, P]), ALU.mult).then_inc(scaled, 1)

                        @block.gpsimd
                        def _(pool):
                            pool.wait_ge(loaded, 16)
                            for t in range(TT):
                                g = sg[:, t].rearrange("p (h c) -> p h c", h=H)
                                pool.tensor_tensor(g, g, gn[:, :].unsqueeze(1).to_broadcast([P, H, P]), ALU.mult).then_inc(gained, 1)
                            for t in range(TT):
                                pool.wait_ge(gained, t + 1)
                                pool.wait_ge(scaled, t + 1)
                                pool.tensor_tensor(otok[:, t], otok[:, t], sg[:, t], ALU.mult).then_inc(gated, 1)

                        @block.tensor
                        def _(pe):
                            pe.wait_ge(gated, TT)
                            for b in range(4):
                                transpose_in(pe, b, lambda i: otok[:, i % TT, (2 * b + i // TT) * P:(2 * b + i // TT + 1) * P], 2 * TT).then_inc(turned, 1)

                residual_block("res1", 1, C_OUT, lambda i, kt: yT[:, kt, i * P:(i + 1) * P], [(xs[:, t], gate1[:, :]) for t in range(TT)], END,
                               store=lambda t: out[0, t * P:(t + 1) * P, :])


_INS = ["x", "c", "ctx", "c_ctx", "ada_w", "ada_b", "norm_mix_g", "w_in", "conv_w", "a_log", "dt_bias",
        "gdn_norm_g", "sgu_ln_g", "sgu_ln_b", "sgu_w", "sgu_b", "w_branch_a", "w_branch_b", "w_out",
        "norm_ffn_g", "router_group_w", "router_group_b", "router_expert_w", "router_expert_b",
        "expert_w1", "expert_w3", "expert_w2", "final_norm_g", "c_2", "ctx_2", "c_ctx_2", "w_ada_2",
        "b_ada_2", "ln_g_2", "ln_b_2", "w_in_ab_2", "w_out_ab_2", "sink_ab_2", "conv_ab_2", "w_in_c_2",
        "w_out_c_2", "lb_c_2", "gnorm_c_2"]


def kernel(**inputs):
    import concourse.bacc as bacc
    from concourse.bass_utils import run_bass_kernel_spmd

    nc = bacc.Bacc("TRN2", target_bir_lowering=False, num_devices=1)
    arrays, w = {}, {}
    for name in _INS:
        a = np.ascontiguousarray(inputs[name])
        arrays["in_" + name] = a
        w[name] = nc.dram_tensor("in_" + name, a.shape, mybir.dt.from_np(a.dtype), kind="ExternalInput").ap()
    table = shape_constants()[0]
    arrays["shape_constants"] = table
    consts = nc.dram_tensor("shape_constants", table.shape, F32, kind="ExternalInput").ap()
    out = nc.dram_tensor("out", (1, L, D), F32, kind="ExternalOutput").ap()
    build(nc, w, out, consts)
    r = run_bass_kernel_spmd(nc, [arrays], core_ids=[0])
    return r.results[0]["out"]
```

```python
import math
from contextlib import ExitStack

import numpy as np
import concourse.bass as bass
import concourse.mybir as mybir

F32 = mybir.dt.float32
I32 = mybir.dt.int32
ALU = mybir.AluOpType
ACT = mybir.ActivationFunctionType
AX = mybir.AxisListType

P = 128
D = 1024
KT = D // P
L = 256
TT = L // P
H = 8
PANEL = 512
HALF = PANEL // 2
RING = 3
CONV_K = 5
N_QKV = 3 * D
COL_BA = N_QKV
COL_Z = COL_BA + 4 * H
EPS = 1e-6
LN_EPS = 1e-5
LEVELS = 7
GROUPS = 4
PER_GROUP = 8
N_EXPERTS = GROUPS * PER_GROUP
D_EXPERT = 256
TOP_K = 2
MAIN = L * TOP_K
OVERFLOW = 3
SLOTS = MAIN + OVERFLOW * P
SB = SLOTS // P
ROUTER = GROUPS + N_EXPERTS
A_HEADS, A_DIM = 8, 64
KV_HEADS = 2
WINDOW = 128
GRID_W = 64
ROPE_BASE = 10000.0
DEEPNORM_ALPHA = 4.0 ** 0.25
MASKED = -1e30


def shape_constants():
    parts, at = {}, 0
    cols = []

    def put(name, a):
        nonlocal at
        a = np.asarray(a, np.float32).reshape(P, -1)
        parts[name] = (at, a.shape[1])
        cols.append(a)
        at += a.shape[1]

    i = np.arange(P)
    put("ident", np.eye(P))
    put("ones", np.ones((P, P)))
    put("tri", np.stack([i[:, None] <= i[None, :], i[:, None] >= i[None, :]], 1))
    lev = np.zeros((P, 2, LEVELS, P // 2))
    for lv in range(LEVELS):
        b = 1 << lv
        blk = np.arange(P // 2) // b
        low, high = blk * 2 * b, blk * 2 * b + b
        lev[:, 0, lv] = (i[:, None] >= high) & (i[:, None] < high + b)
        lev[:, 1, lv] = (i[:, None] >= low) & (i[:, None] < high)
    put("lev", lev)
    small = at
    put("slots", np.tile(np.arange(SLOTS), (P, 1)))
    ffn_end = at
    tok = np.arange(L)
    half = A_DIM // 4
    freq = np.power(np.float32(ROPE_BASE), -np.arange(half, dtype=np.float32) / np.float32(half)).astype(np.float32)
    d = i % A_DIM
    pos = np.where((d < A_DIM // 2)[:, None], (tok // GRID_W)[None], (tok % GRID_W)[None]).astype(np.float32)
    ang = pos * freq[d % half][:, None]
    put("cos", np.cos(ang))
    put("sin", np.sin(ang))
    rot = np.zeros((P, P))
    first = (d % (2 * half)) < half
    rot[(i + half)[first], i[first]] = -1
    rot[(i - half)[~first], i[~first]] = 1
    put("rot", rot)
    q, k = tok[:, None], tok[None, :]
    win = np.where(np.abs(q - k) <= WINDOW, 0.0, MASKED)
    put("kdup", np.stack([i[:, None] == g * A_DIM + i[None, :] % A_DIM for g in range(KV_HEADS)], 1))
    put("win", np.concatenate([np.zeros((L, L)), win], 1).reshape(TT, P, 2 * L).transpose(1, 0, 2))
    return np.concatenate(cols, 1), parts, (small, ffn_end)


def row_bcast(ap, n=P):
    return ap.unsqueeze(0).to_broadcast([n, ap.shape[0]])


def half_cols(ap, lv, side):
    b = 1 << lv
    if len(ap.shape) == 2:
        return ap.rearrange("p (n s j) -> p n s j", s=2, j=b)[:, :, side, :]
    return ap.rearrange("p u (n s j) -> p u n s j", s=2, j=b)[:, :, :, side, :]


def packed_cols(ap, lv):
    b = 1 << lv
    if len(ap.shape) == 2:
        return ap.rearrange("p (n j) -> p n j", j=b)
    return ap.rearrange("p u (n j) -> p u n j", j=b)


class Stream:

    def __init__(self, ring, loaded, used):
        self.ring, self.loaded, self.used = ring, loaded, used
        self.panels = []
        self.issued = 0
        self.taken = 0

    def slot(self, n):
        return self.ring[:, n % RING]

    def issue(self, sp, upto):
        while self.issued < min(upto, len(self.panels)):
            n = self.issued
            if n >= RING:
                sp.wait_ge(self.used, n - RING + 1)
            self.load(sp, n)
            self.issued += 1

    def load(self, sp, n):
        for src, dst in self.panels[n](self.slot(n)):
            sp.dma_start(dst, src).then_inc(self.loaded[n % RING], 16)

    def arrive(self, n):
        parts = sum(len(self.panels[m](self.slot(m))) for m in range(n % RING, n + 1, RING))
        return self.loaded[n % RING], 16 * parts


def build(nc, w, out, const_dram):
    _, parts, (small, ffn_end) = shape_constants()
    with ExitStack() as whole:
        def sem(name):
            return whole.enter_context(nc.semaphore(name))

        def sb(scope, name, shape, dt=F32):
            return scope.enter_context(nc.sbuf_tensor(name, shape, dt))

        def stage_sems(scope, prefix):
            held = []

            def clear():
                nc.clear_and_free_semaphores(held)
                nc.all_engine_barrier(sem_only=True)

            scope.callback(clear)

            def make(what):
                held.append(nc.alloc_semaphore(prefix + what))
                return held[-1]

            return make

        ps = whole.enter_context(nc.psum_tensor("ps", [P, 8, 512], F32))
        ring = sb(whole, "ring", [P, RING, KT, PANEL])
        consts = sb(whole, "consts", [P, small])

        def const(name):
            at, n = parts[name]
            return consts[:, at:at + n]

        ident, ones = const("ident"), const("ones")
        tri = const("tri").rearrange("p (d t) -> p d t", d=2)
        lev = const("lev").rearrange("p (d l c) -> p d l c", d=2, l=LEVELS)
        xs = sb(whole, "xs", [P, TT, D])
        high = whole.enter_context(ExitStack())
        stat = sb(whole, "stat", [P, 16])

        stream = Stream(ring, [sem(f"panel_loaded{i}") for i in range(RING)], sem("panel_used"))
        add = stream.panels.append

        def add_cols(src, cols, width=PANEL):
            add(lambda slot: [(src[:, :, cols:cols + width], slot[:, :, 0:width])])

        ktp = lambda a: a.rearrange("(kt p) n -> p kt n", p=P)
        pkt = lambda a: a.rearrange("(p kt) n -> p kt n", kt=KT)
        w_in, ada = ktp(w["w_in"][0]), pkt(w["ada_w"][0])
        ADA_MIX = 0
        for i in range(4):
            add_cols(ada, i * PANEL)
        QKV = len(stream.panels)
        for i in range(N_QKV // PANEL):
            add_cols(w_in, i * PANEL)
        zuvg, rest = [], []
        for i in range(10):
            zuvg.append(len(stream.panels))
            add_cols(w_in, COL_Z + i * PANEL)
            if i < 8:
                rest.append(len(stream.panels))
                add_cols(ada, (4 + i) * PANEL)
        merge, ada2 = [], ([], [])
        for i in range(6):
            merge.append(len(stream.panels))
            add_cols(ktp(w[("w_branch_a", "w_branch_b", "w_out")[i // 2]][0]), i % 2 * PANEL)
            ada2[0].append(len(stream.panels))
            add_cols(pkt(w["w_ada_2"][0]), i * PANEL)
        MOE = len(stream.panels)
        w1 = w["expert_w1"][0].rearrange("e (kt p) f -> e p kt f", p=P)
        w3 = w["expert_w3"][0].rearrange("e (kt p) f -> e p kt f", p=P)
        w2 = w["expert_w2"][0].rearrange("e (ft p) n -> e p ft n", p=P)

        def add_up(e):
            add(lambda slot: [(w1[e], slot[:, :, 0:D_EXPERT]), (w3[e], slot[:, :, D_EXPERT:])])

        def add_down(e):
            view = lambda slot: slot.rearrange("p (e f c) n -> p e f (c n)", e=2, f=2)
            add(lambda slot: [(w2[e + j], view(slot)[:, j]) for j in range(2)])

        for e in range(0, N_EXPERTS, 2):
            add_up(e)
            add_up(e + 1)
            add_down(e)
        EXTRA = len(stream.panels)
        extra = {}
        add(lambda slot: [(w1[extra.get(0, 0)], slot[:, :, 0:D_EXPERT]), (w3[extra.get(0, 0)], slot[:, :, D_EXPERT:])])
        add(lambda slot: [(w1[extra.get(1, 0)], slot[:, :, 0:D_EXPERT]), (w3[extra.get(1, 0)], slot[:, :, D_EXPERT:])])
        add(lambda slot: [(w2[extra.get(j, 0)], slot.rearrange("p (e f c) n -> p e f (c n)", e=2, f=2)[:, j]) for j in range(2)])
        add(lambda slot: [(w1[extra.get(2, 0)], slot[:, :, 0:D_EXPERT]), (w3[extra.get(2, 0)], slot[:, :, D_EXPERT:])])
        add(lambda slot: [(w2[extra.get(2, 0)], slot.rearrange("p (e f c) n -> p e f (c n)", e=2, f=2)[:, 0])])
        ab_in = []
        for i in range(7):
            ab_in.append(len(stream.panels))
            add_cols(ktp(w["w_in_ab_2"][0]), i * PANEL, PANEL if i < 6 else HALF)
            if i < 6:
                ada2[1].append(len(stream.panels))
                add_cols(pkt(w["w_ada_2"][1]), i * PANEL)
        AB_OUT = len(stream.panels)
        for i in range(2):
            add_cols(ktp(w["w_out_ab_2"][0]), i * PANEL)
        C_IN = len(stream.panels)
        for i in (2, 3, 4, 5, 0, 1, 6, 7, 8, 9):
            add_cols(ktp(w["w_in_c_2"][0]), i * PANEL)
        C_OUT = len(stream.panels)
        for i in range(2):
            add_cols(ktp(w["w_out_c_2"][0]), i * PANEL)
        END = len(stream.panels)


        def chained(eng, done):
            count = [0]

            def link(ins):
                count[0] += 1
                ins.then_inc(done, 1)
                eng.wait_ge(done, count[0])

            return link

        def ada_dot(eng, n, acc, cvec, done, count):
            slot = stream.slot(n)
            for kt in range(KT):
                if kt == 0:
                    ins = eng.tensor_scalar(acc, slot[:, 0], cvec[:, 0:1], None, ALU.mult)
                else:
                    eng.wait_ge(done, count + kt)
                    ins = eng.scalar_tensor_tensor(out=acc, in0=slot[:, kt], scalar=cvec[:, kt:kt + 1],
                                                   in1=acc, op0=ALU.mult, op1=ALU.add)
                ins.then_inc(done, 1)

        def ada_side(scope, prefix, items, banks):
            acc = sb(scope, f"{prefix}_acc", [P, 2, max(len(rows) for _, rows in items), PANEL])
            sem = stage_sems(scope, prefix + "_")
            dotted, summed, added = sem("dotted"), sem("summed"), sem("added")
            rows_before = lambda k: sum(len(rows) for _, rows in items[:k])

            def dot(dve, k):
                panel, rows = items[k]
                dve.wait_ge(*stream.arrive(panel))
                if k >= 2:
                    dve.wait_ge(summed, rows_before(k - 1))
                for j, (c, _) in enumerate(rows):
                    ada_dot(dve, panel, acc[:, k % 2, j], c, dotted, KT * (rows_before(k) + j))

            def total(pe, k):
                panel, rows = items[k]
                if k >= 1:
                    pe.wait_ge(added, rows_before(k))
                for j in range(len(rows)):
                    pe.wait_ge(dotted, KT * (rows_before(k) + j + 1))
                    pe.matmul(ps[:, banks[j]], ones, acc[:, k % 2, j], start=True, stop=True).then_inc(summed, 1)
                pe.drain().then_inc(stream.used, 1)

            def put(dve, k):
                for j, (_, row) in enumerate(items[k][1]):
                    dve.wait_ge(summed, rows_before(k) + j + 1)
                    dve.tensor_tensor(row, ps[:, banks[j]], row, ALU.add).then_inc(added, 1)

            return dot, total, put

        def ada_block(name, first, n_panels, cx, cc, dest_x, dest_c, loads, n_loads, upto, scope, prepare=None):
            acc = sb(scope, f"{name}_acc", [P, 2, PANEL])
            sem = stage_sems(scope, name + "_")
            dot_x, mod_done, summed = sem("dot_x"), sem("mod_done"), sem("summed")
            loaded, c_ready = sem("loaded"), sem("c_ready")
            has_c = [i for i in range(n_panels) if dest_c(i) is not None]
            dests = [[d for d in (dest_x(i), dest_c(i)) if d is not None] for i in range(n_panels)]
            evacs = [sum(len(d) for d in dests[:i + 1]) for i in range(n_panels)]
            with nc.Block() as block:
                @block.sync
                def _(sp):
                    loads(sp, loaded)
                    stream.issue(sp, upto)

                @block.scalar
                def _(act):
                    if prepare:
                        act.wait_ge(loaded, 16 * n_loads)
                        prepare(act).then_inc(c_ready, 1)

                @block.vector
                def _(dve):
                    if prepare:
                        dve.wait_ge(c_ready, 1)
                    dve.wait_ge(loaded, 16 * n_loads)

                    def finish(i):
                        dve.wait_ge(summed, evacs[i])
                        for j, d in enumerate(dests[i]):
                            dve.tensor_tensor(d, ps[:, 2 * j + i % 2], d, ALU.add).then_inc(mod_done, 1)

                    for i in range(n_panels):
                        dve.wait_ge(*stream.arrive(first + i))
                        if i >= 2:
                            dve.wait_ge(summed, evacs[i - 2])
                        ada_dot(dve, first + i, acc[:, i % 2], cx, dot_x, KT * i)
                        if i >= 1:
                            finish(i - 1)
                    finish(n_panels - 1)

                @block.tensor
                def _(pe):
                    if prepare:
                        pe.wait_ge(c_ready, 1)
                    for i in range(n_panels):
                        if i >= 2:
                            pe.wait_ge(mod_done, evacs[i - 2])
                        if i in has_c:
                            pe.wait_ge(*stream.arrive(first + i))
                            for kt in range(KT):
                                ins = pe.matmul(ps[:, 2 + i % 2], cc[:, kt:kt + 1].to_broadcast([P, P]), stream.slot(first + i)[:, kt],
                                                start=(kt == 0), stop=(kt == KT - 1))
                            ins.then_inc(summed, 1)
                        pe.wait_ge(dot_x, KT * (i + 1))
                        pe.matmul(ps[:, i % 2], ones, acc[:, i % 2], start=True, stop=True).then_inc(summed, 1)
                        pe.drain().then_inc(stream.used, 1)

        def transpose_in(pe, bank, src, n, name=None):
            for i in range(n):
                ins = pe.transpose(ps[:, bank, i * P:(i + 1) * P], src(i), ident)
            return ins

        def norm_modulate(eng, done, base, x, rstd, gm, shift, tmp, out_t):
            eng.scalar_tensor_tensor(out=tmp, in0=x, scalar=rstd, in1=gm, op0=ALU.mult, op1=ALU.mult).then_inc(done, 1)
            eng.wait_ge(done, base + 1)
            return eng.tensor_tensor(out_t, tmp, shift, ALU.add)

        eps = sb(whole, "eps", [P, 2])
        cact = sb(whole, "cact", [P, 4, KT])
        with ExitStack() as first:
            hTx = sb(first, "hTx", [P, KT, L])
            otok = sb(first, "otok", [P, TT, D])

            qkv = first.enter_context(ExitStack())
            kT = sb(qkv, "kT", [P, H, 2 * L])
            qT = sb(qkv, "qT", [P, H, L])
            beta = sb(qkv, "beta", [P, 2 * TT, 2 * H])
            glog = sb(qkv, "glog", [P, 2 * TT, 2 * H])
            ktok = sb(qkv, "ktok", [P, 2 * TT, D])
            vtok = sb(qkv, "vtok", [P, 2 * TT, D])
            proj_in = qkv.enter_context(ExitStack())
            hTc = sb(proj_in, "hTc", [P, KT, L])

            with ExitStack() as scope:
                mix = sb(scope, "mix", [P, 2, 2, D])
                cs = sb(scope, "cs", [P, TT, D])
                gmix = sb(scope, "gmix", [P, D])
                craw = sb(scope, "craw", [P, 4, KT])

                def loads(sp, loaded):
                    for i, n in enumerate(("c", "c_ctx", "c_2", "c_ctx_2")):
                        src = w[n] if len(w[n].shape) == 1 else w[n][0]
                        sp.dma_start(craw[:, i], src.rearrange("(p kt) -> p kt", kt=KT)).then_inc(loaded, 16)
                    for j in range(2):
                        for r in range(2):
                            sp.dma_start(mix[:, j, r], row_bcast(w["ada_b"][0, r * D:(r + 1) * D])).then_inc(loaded, 16)
                    sp.dma_start(consts[:, :], const_dram[:, 0:small]).then_inc(loaded, 16)
                    sp.dma_start(xs[:, :, :], w["x"][0].rearrange("(t p) d -> p t d", p=P)).then_inc(loaded, 16)
                    sp.dma_start(cs[:, :, :], w["ctx"][0].rearrange("(t p) d -> p t d", p=P)).then_inc(loaded, 16)
                    sp.dma_start(gmix[:, :], row_bcast(w["norm_mix_g"][0])).then_inc(loaded, 16)

                with ExitStack() as inner:
                    ada_block("ada_mix", ADA_MIX, 4, cact[:, 0], cact[:, 1],
                              lambda i: mix[:, 0, i // 2, (i % 2) * PANEL:(i % 2 + 1) * PANEL],
                              lambda i: mix[:, 1, i // 2, (i % 2) * PANEL:(i % 2 + 1) * PANEL],
                              loads, 12, 4 + RING, inner,
                              lambda act: act.activation(cact[:, :, :], craw[:, :, :], ACT.Silu))

                gm = sb(scope, "gm", [P, 2, D])
                tmp = sb(scope, "tmp", [P, 2, D])
                ssem = stage_sems(scope, "norm_")
                squares, std, rstd_done = ssem("squares"), ssem("std"), ssem("rstd")
                gm_done, x_steps, c_steps = ssem("gm"), ssem("x_steps"), ssem("c_steps")
                turned, moved_a, moved_v = ssem("turned"), ssem("moved_a"), ssem("moved_v")
                seqs = (xs, cs)
                with nc.Block() as block:
                    @block.scalar
                    def _(act):
                        for j in range(2):
                            for t in range(TT):
                                act.activation(hTx[:, 4 * (t % 2):4 * (t % 2) + 4].rearrange("p a b -> p (a b)"), seqs[j][:, t],
                                               ACT.Square, accum_out=stat[:, 2 * j + t:2 * j + t + 1]).then_inc(squares, 1)
                                act.wait_ge(squares, 2 * j + t + 1)
                        act.wait_ge(rstd_done, 1)
                        act.activation(stat[:, 4:8], stat[:, 4:8], ACT.Sqrt).then_inc(std, 1)
                        for kt in range(0, KT, 2):
                            act.wait_ge(turned, kt + 1)
                            act.copy(hTx[:, kt], ps[:, kt, L:2 * L])
                            act.copy(hTc[:, kt], ps[:, kt, 0:L]).then_inc(moved_a, 1)

                    @block.vector
                    def _(dve):
                        dve.wait_ge(squares, 4)
                        dve.tensor_scalar(stat[:, 4:8], stat[:, 0:4], 1.0 / D, EPS, ALU.mult, ALU.add).then_inc(rstd_done, 1)
                        for j in range(2):
                            dve.scalar_tensor_tensor(out=gm[:, j], in0=mix[:, j, 1], scalar=1.0, in1=gmix[:, :],
                                                     op0=ALU.add, op1=ALU.mult).then_inc(gm_done, 1)
                        dve.wait_ge(std, 1)
                        dve.reciprocal(stat[:, 8:12], stat[:, 4:8]).then_inc(rstd_done, 1)
                        dve.wait_ge(rstd_done, 2)
                        dve.wait_ge(gm_done, 2)
                        for t in range(TT):
                            norm_modulate(dve, x_steps, 2 * t, xs[:, t], stat[:, 8 + t:9 + t], gm[:, 0], mix[:, 0, 0],
                                          tmp[:, t], tmp[:, t]).then_inc(x_steps, 1)
                        for kt in range(1, KT, 2):
                            dve.wait_ge(turned, kt + 1)
                            dve.tensor_copy(hTx[:, kt], ps[:, kt, L:2 * L])
                            dve.tensor_copy(hTc[:, kt], ps[:, kt, 0:L]).then_inc(moved_v, 1)

                    @block.gpsimd
                    def _(pool):
                        pool.memset(eps[:, 0:1], EPS)
                        pool.memset(eps[:, 1:2], LN_EPS)
                        pool.wait_ge(rstd_done, 2)
                        pool.wait_ge(gm_done, 2)
                        link = chained(pool, c_steps)
                        for t in range(TT):
                            link(pool.tensor_scalar(cs[:, t], cs[:, t], stat[:, 10 + t:11 + t], None, ALU.mult))
                            link(pool.tensor_tensor(cs[:, t], cs[:, t], gm[:, 1], ALU.mult))
                            link(pool.tensor_tensor(cs[:, t], cs[:, t], mix[:, 1, 0], ALU.add))

                    @block.tensor
                    def _(pe):
                        pe.wait_ge(x_steps, 2 * TT)
                        pe.wait_ge(c_steps, 3 * TT)
                        for kt in range(KT):
                            cols = slice(kt * P, kt * P + P)
                            transpose_in(pe, kt, lambda i: (cs, tmp)[i // TT][:, i % TT, cols], 2 * TT).then_inc(turned, 1)

            with ExitStack() as scope:
                vT = sb(scope, "vT", [P, H, 2 * L])
                wba = sb(scope, "wba", [P, KT, 4 * H])
                taps_row = sb(scope, "taps_row", [CONV_K, N_QKV])
                taps = sb(scope, "taps", [P, 24, CONV_K])
                xpad = sb(scope, "xpad", [P, 3, 2, L + CONV_K - 1])
                conv = sb(scope, "conv", [P, 3, 2, L])
                rows = sb(scope, "rows", [P, 2, 2 * H])
                sp1 = sb(scope, "sp1", [P, 3, 2 * TT, 2 * H])
                norm = sb(scope, "norm", [P, 1, 2 * L])
                sq = sb(scope, "sq", [P, 2, 2 * L])
                pick_row = sb(scope, "pick_row", [P, 4 * H])
                ssem = stage_sems(scope, "qkv_")
                loaded, proj, padded, conved, silued = ssem("loaded"), ssem("proj"), ssem("padded"), ssem("conved"), ssem("silued")
                pad_zero, taps_t, taps_done = ssem("pad_zero"), ssem("taps_t"), ssem("taps_done")
                ba_done, ba_chain, ba_act, ba_pool = ssem("ba_done"), ssem("ba_chain"), ssem("ba_act"), ssem("ba_pool")
                squared, sums, rooted, inverted, normed = ssem("squared"), ssem("sums"), ssem("rooted"), ssem("inverted"), ssem("normed")
                turned, moved_a, moved_v = ssem("turned"), ssem("moved_a"), ssem("moved_v")
                conv_step, row_set, spread = ssem("conv_step"), ssem("row_set"), ssem("spread")
                N_TILES = 24
                BANKS = 4

                def dest(j):
                    return qT[:, j, :] if j < H else (kT[:, j - H, :] if j < 2 * H else vT[:, j - 2 * H, :])

                def seq(j):
                    return slice(1, 2) if j < H else slice(0, 2)

                with nc.Block() as block:
                    @block.sync
                    def _(sp):
                        sp.dma_start(taps_row[:, :], w["conv_w"][0]).then_inc(loaded, 16)
                        sp.dma_start(wba[:, :, :], w_in[:, :, COL_BA:COL_Z]).then_inc(loaded, 16)
                        sp.dma_start(rows[:, 0], row_bcast(w["a_log"][0].rearrange("a b -> (a b)"))).then_inc(loaded, 16)
                        sp.dma_start(rows[:, 1], row_bcast(w["dt_bias"][0].rearrange("a b -> (a b)"))).then_inc(loaded, 16)
                        stream.issue(sp, zuvg[0] + RING)

                    @block.gpsimd
                    def _(pool):
                        pool.memset(xpad[:, :, :, :], 0.0).then_inc(pad_zero, 1)

                    @block.tensor
                    def _(pe):
                        pe.wait_ge(loaded, 64)
                        for j in range(N_TILES):
                            ins = pe.transpose(ps[:, 7, CONV_K * j:CONV_K * (j + 1)], taps_row[:, j * P:(j + 1) * P],
                                               ident[0:CONV_K, 0:CONV_K])
                        ins.then_inc(taps_t, 1)
                        for t in range(2 * TT):
                            lhs = (hTc, hTx)[t // TT]
                            for kt in range(KT):
                                ins = pe.matmul(ps[:, 6, 4 * H * t:4 * H * (t + 1)], lhs[:, kt, (t % TT) * P:(t % TT + 1) * P],
                                                wba[:, kt], start=(kt == 0), stop=(kt == KT - 1))
                        ins.then_inc(ba_done, 1)
                        for j in range(N_TILES):
                            n = QKV + j // 4
                            if j % 4 == 0:
                                pe.wait_ge(*stream.arrive(n))
                            if j >= BANKS:
                                pe.wait_ge(padded, j - BANKS + 1)
                            slot = stream.slot(n)
                            for s in range(2)[seq(j)]:
                                for kt in range(KT):
                                    ins = pe.matmul(ps[:, j % BANKS, s * L:(s + 1) * L], slot[:, kt, (j % 4) * P:(j % 4 + 1) * P],
                                                    (hTc, hTx)[s][:, kt], start=(kt == 0), stop=(kt == KT - 1))
                            ins.then_inc(proj, 1)
                            if j % 4 == 3:
                                pe.drain().then_inc(stream.used, 1)

                    @block.scalar
                    def _(act):
                        act.wait_ge(loaded, 64)
                        act.wait_ge(ba_chain, 1)
                        ba = ps[:, 6, 0:2 * TT * 4 * H].rearrange("p (t c) -> p t c", t=2 * TT)
                        act.activation(beta[:, :, :], ba[:, :, 0:2 * H], ACT.Sigmoid)
                        act.wait_ge(pad_zero, 1)

                        def pad(j):
                            act.wait_ge(proj, j + 1)
                            if j >= 3:
                                act.wait_ge(conved, j - 2)
                            act.copy(xpad[:, j % 3, seq(j), 2:2 + L],
                                     ps[:, j % BANKS].rearrange("p (s t) -> p s t", s=2)[:, seq(j)]).then_inc(padded, 1)

                        def silu(j):
                            act.wait_ge(conved, j + 1)
                            out_t = dest(j) if j < H else dest(j).rearrange("p (s t) -> p s t", s=2)
                            act.activation(out_t, conv[:, j % 3, 1] if j < H else conv[:, j % 3], ACT.Silu).then_inc(silued, 1)

                        for j in range(N_TILES + 1):
                            if j < N_TILES:
                                pad(j)
                            if j >= 1:
                                silu(j - 1)
                        act.wait_ge(ba_chain, 2)
                        act.activation(sp1[:, 1], sp1[:, 0], ACT.Abs).then_inc(ba_act, 1)
                        act.wait_ge(ba_act, 1)
                        act.activation(sp1[:, 1], sp1[:, 1], ACT.Exp, scale=-1.0)
                        act.activation(rows[:, 0], rows[:, 0], ACT.Exp).then_inc(ba_act, 1)
                        act.wait_ge(ba_act, 2)
                        act.activation(sp1[:, 1], sp1[:, 1], ACT.Ln, bias=1.0).then_inc(ba_act, 1)

                    @block.vector
                    def _(dve):
                        dve.wait_ge(loaded, 64)
                        dve.wait_ge(taps_t, 1)
                        dve.tensor_copy(taps[:, :, :], ps[:, 7, 0:N_TILES * CONV_K].rearrange("p (j c) -> p j c", c=CONV_K)).then_inc(taps_done, 1)
                        dve.wait_ge(ba_done, 1)
                        ba = ps[:, 6, 0:2 * TT * 4 * H].rearrange("p (t c) -> p t c", t=2 * TT)
                        dve.tensor_tensor(sp1[:, 0], ba[:, :, 2 * H:], rows[:, 1].unsqueeze(1).to_broadcast([P, 2 * TT, 2 * H]),
                                          ALU.add).then_inc(ba_chain, 1)
                        dve.wait_ge(ba_chain, 1)
                        dve.tensor_scalar(sp1[:, 2], sp1[:, 0], 0.0, None, ALU.max).then_inc(ba_chain, 1)
                        dve.wait_ge(taps_done, 1)
                        step = [0]
                        for j in range(N_TILES):
                            dve.wait_ge(padded, j + 1)
                            if j >= 3:
                                dve.wait_ge(silued, j - 2)
                            src, acc = xpad[:, j % 3, seq(j)], conv[:, j % 3, seq(j)]
                            for c in range(CONV_K):
                                if c == 0:
                                    ins = dve.tensor_scalar(acc, src[:, :, 0:L], taps[:, j, 0:1], None, ALU.mult)
                                else:
                                    dve.wait_ge(conv_step, step[0])
                                    ins = dve.scalar_tensor_tensor(out=acc, in0=src[:, :, c:c + L], scalar=taps[:, j, c:c + 1],
                                                                   in1=acc, op0=ALU.mult, op1=ALU.add)
                                if c < CONV_K - 1:
                                    step[0] += 1
                                    ins.then_inc(conv_step, 1)
                            ins.then_inc(conved, 1)
                        dve.wait_ge(ba_act, 3)
                        dve.tensor_tensor(sp1[:, 2], sp1[:, 2], sp1[:, 1], ALU.add).then_inc(ba_chain, 1)
                        dve.wait_ge(ba_chain, 3)
                        dve.scalar_tensor_tensor(out=glog[:, :, :], in0=sp1[:, 2], scalar=-1.0,
                                                 in1=rows[:, 0].unsqueeze(1).to_broadcast([P, 2 * TT, 2 * H]),
                                                 op0=ALU.mult, op1=ALU.mult).then_inc(ba_chain, 1)

                def span(j):
                    return (L, 2 * L) if j < H else (0, 2 * L)

                order = list(range(H, 2 * H)) + list(range(H))
                inv = norm[0:2 * H, 0]
                SPREAD = 4
                with nc.Block() as block:
                    @block.gpsimd
                    def _(pool):
                        pool.memset(pick_row[:, :], 0.0).then_inc(row_set, 1)
                        pool.wait_ge(row_set, 1)
                        pool.memset(pick_row[:, 2 * H - 1:2 * H], 1.0).then_inc(row_set, 1)

                    @block.scalar
                    def _(act):
                        for n, j in enumerate(order):
                            a, b = span(j)
                            if n >= 2:
                                act.wait_ge(sums, n - 1)
                            act.activation(sq[:, n % 2, a:b], dest(j), ACT.Square).then_inc(squared, 1)
                        act.wait_ge(sums, 2 * H)
                        act.activation(inv, ps[0:2 * H, 0], ACT.Sqrt, bias=eps[0:2 * H, 0:1]).then_inc(rooted, 1)

                    @block.tensor
                    def _(pe):
                        pe.wait_ge(row_set, 2)
                        for n, j in enumerate(order):
                            a, b = span(j)
                            pe.wait_ge(squared, n + 1)
                            pe.matmul(ps[0:2 * H, 0, a:b], pick_row[:, 2 * H - 1 - j:4 * H - 1 - j], sq[:, n % 2, a:b],
                                      start=(n == 0), stop=(n == 2 * H - 1)).then_inc(sums, 1)
                        pe.wait_ge(inverted, 1)
                        for n, j in enumerate(order):
                            a, b = span(j)
                            if n >= SPREAD:
                                pe.wait_ge(normed, n - SPREAD + 1)
                            pe.matmul(ps[:, 1 + n % SPREAD, a:b], ident[0:2 * H, j:j + 1].to_broadcast([2 * H, P]), inv[:, a:b],
                                      start=True, stop=True).then_inc(spread, 1)

                    @block.vector
                    def _(dve):
                        dve.wait_ge(rooted, 1)
                        dve.reciprocal(inv, inv).then_inc(inverted, 1)
                        for n, j in enumerate(order):
                            a, b = span(j)
                            dve.wait_ge(spread, n + 1)
                            dve.scalar_tensor_tensor(out=dest(j), in0=dest(j), scalar=P ** -0.5 if j < H else 1.0,
                                                     in1=ps[:, 1 + n % SPREAD, a:b], op0=ALU.mult, op1=ALU.mult).then_inc(normed, 1)

                with nc.Block() as block:
                    @block.tensor
                    def _(pe):
                        for i in range(16):
                            src, t, half = (vT, kT)[i // 8], i % 8 // 2, i % 2
                            if i >= 4:
                                pe.wait_ge(moved_v if i % 2 else moved_a, (i - 4) // 2 + 1)
                            transpose_in(pe, i % 4, lambda m: src[:, 4 * half + m, t * P:(t + 1) * P], 4).then_inc(turned, 1)

                    def move(copy, i):
                        dst, t, half = (vtok, ktok)[i // 8], i % 8 // 2, i % 2
                        return copy(dst[:, t, half * 512:half * 512 + 512], ps[:, i % 4])

                    @block.scalar
                    def _(act):
                        for i in range(0, 16, 2):
                            act.wait_ge(turned, i + 1)
                            move(act.copy, i).then_inc(moved_a, 1)

                    @block.vector
                    def _(dve):
                        for i in range(1, 16, 2):
                            dve.wait_ge(turned, i + 1)
                            move(dve.tensor_copy, i).then_inc(moved_v, 1)
            proj_in.close()

            with ExitStack() as scope:
                dm = sb(scope, "dm", [P, 2 * H, P])
                nt = sb(scope, "nt", [P, 2 * H, P])
                tm = sb(scope, "tm", [P, 2 * H, P])
                tt = sb(scope, "tt", [P, 2 * H, P])
                qd = sb(scope, "qd", [P, 2 * H, P])
                sc = sb(scope, "sc", [P, 2 * H, P])
                state = sb(scope, "state", [P, 2 * H, P])
                xk = sb(scope, "xk", [P, 2 * H, P // 2])
                vn = sb(scope, "vn", [P, 2, 4, P])
                vdec = sb(scope, "vdec", [P, 2, 4, P])
                gsum = sb(scope, "gsum", [P, 2 * TT, 2 * H])
                nbeg = sb(scope, "nbeg", [P, 2 * TT, 2 * H])
                kdec = sb(scope, "kdec", [P, 2 * H])
                glast = sb(scope, "glast", [P, 2 * H])
                GRP = 4

                with ExitStack() as inner:
                    ssem = stage_sems(inner, "gsum_")
                    summed, copied, exped = ssem("summed"), ssem("copied"), ssem("exped")
                    with nc.Block() as block:
                        @block.tensor
                        def _(pe):
                            for t in range(2 * TT):
                                for d in range(2):
                                    ins = pe.matmul(ps[:, 0, (2 * t + d) * H:(2 * t + d + 1) * H], tri[:, d], glog[:, t, d * H:(d + 1) * H],
                                                    start=True, stop=True)
                            ins.then_inc(summed, 1)

                        @block.vector
                        def _(dve):
                            dve.wait_ge(summed, 1)
                            dve.tensor_copy(gsum[:, :, :], ps[:, 0, 0:4 * TT * H].rearrange("p (t u) -> p t u", t=2 * TT)).then_inc(copied, 1)
                            dve.wait_ge(exped, 1)
                            dve.scalar_tensor_tensor(out=nbeg[:, :, :], in0=nbeg[:, :, :], scalar=-1.0, in1=beta[:, :, :],
                                                     op0=ALU.mult, op1=ALU.mult)

                        @block.scalar
                        def _(act):
                            act.wait_ge(copied, 1)
                            act.activation(nbeg[:, :, :], gsum[:, :, :], ACT.Exp).then_inc(exped, 1)

                def unit(gi, m):
                    return 4 * gi + m

                def units(gi):
                    return slice(4 * gi, 4 * gi + 4)

                for step in range(2 * TT):
                    tiles = (step, step ^ 1)
                    on_x = step >= TT
                    tok = lambda gi: tiles[gi // 2]
                    head = lambda gi, m: 4 * (gi % 2) + m
                    cols = lambda gi, m: slice(head(gi, m) * P, head(gi, m) * P + P)
                    tcols = lambda gi: slice(tok(gi) * P, tok(gi) * P + P)
                    xcols = lambda gi: slice((tok(gi) - TT) * P, (tok(gi) - TT) * P + P)
                    quarter = lambda m: slice(m * P, m * P + P)

                    with ExitStack() as inner:
                        ssem = stage_sems(inner, f"chunk{step}_")
                        rowed, argued, dm_exp, dm_masked, erowed = (ssem(n) for n in ("rowed", "argued", "dm_exp", "dm_masked", "erowed"))
                        kk_done, qk_done, nt_done, sc_done = (ssem(n) for n in ("kk_done", "qk_done", "nt_done", "sc_done"))
                        with nc.Block() as block:
                            @block.tensor
                            def _(pe):
                                for gi in range(GRP):
                                    d, t = gi // 2, tok(gi)
                                    if gi >= 2:
                                        pe.wait_ge(erowed, gi - 1)
                                    for m in range(4):
                                        u = unit(gi, m)
                                        ins = pe.matmul(ps[:, gi % 2, quarter(m)], glog[:, t, u:u + 1].to_broadcast([P, P]), tri[:, d],
                                                        start=True, stop=True)
                                    ins.then_inc(rowed, 1)
                                    if gi >= 2:
                                        pe.wait_ge(nt_done, gi - 1)
                                    for m in range(4):
                                        k = kT[:, head(gi, m), tcols(gi)]
                                        ins = pe.matmul(ps[:, 2 + gi % 2, quarter(m)], k, k, start=True, stop=True)
                                    ins.then_inc(kk_done, 1)
                                    if on_x:
                                        if gi >= 2:
                                            pe.wait_ge(sc_done, gi - 1)
                                        for m in range(4):
                                            ins = pe.matmul(ps[:, 4 + gi % 2, quarter(m)], kT[:, head(gi, m), tcols(gi)],
                                                            qT[:, head(gi, m), xcols(gi)], start=True, stop=True)
                                        ins.then_inc(qk_done, 1)

                            @block.vector
                            def _(dve):
                                def products(gi):
                                    dve.wait_ge(dm_masked, gi + 1)
                                    dve.wait_ge(kk_done, gi + 1)
                                    dve.tensor_tensor(nt[:, units(gi)], ps[:, 2 + gi % 2].rearrange("p (u c) -> p u c", u=4), dm[:, units(gi)],
                                                      ALU.mult).then_inc(nt_done, 1)
                                    if on_x:
                                        dve.wait_ge(qk_done, gi + 1)
                                        dve.tensor_tensor(sc[:, units(gi)], ps[:, 4 + gi % 2].rearrange("p (u c) -> p u c", u=4), dm[:, units(gi)],
                                                          ALU.mult).then_inc(sc_done, 1)

                                for gi in range(GRP):
                                    dve.wait_ge(rowed, gi + 1)
                                    for m in range(4):
                                        u = unit(gi, m)
                                        ins = dve.tensor_scalar(dm[:, u], ps[:, gi % 2, quarter(m)], gsum[:, tok(gi), u:u + 1], 0.0,
                                                                ALU.subtract, ALU.min)
                                    ins.then_inc(argued, 1)
                                    if gi >= 1:
                                        products(gi - 1)
                                products(GRP - 1)

                            @block.scalar
                            def _(act):
                                for gi in range(GRP):
                                    last = P - 1 if gi < 2 else 0
                                    rows_t = ps[:, gi % 2].rearrange("p (u c) -> p u c", u=4)
                                    act.wait_ge(argued, gi + 1)
                                    act.activation(dm[:, units(gi)], dm[:, units(gi)], ACT.Exp).then_inc(dm_exp, 1)
                                    if on_x:
                                        act.activation(qd[:, units(gi)], rows_t, ACT.Exp)
                                    act.activation(glast[:, units(gi)], rows_t[:, :, last], ACT.Exp).then_inc(erowed, 1)

                            @block.gpsimd
                            def _(pool):
                                for gi in range(GRP):
                                    d, last = gi // 2, P - 1 if gi < 2 else 0
                                    pool.wait_ge(dm_exp, gi + 1)
                                    pool.tensor_tensor(dm[:, units(gi)], dm[:, units(gi)], tri[:, d].unsqueeze(1).to_broadcast([P, 4, P]),
                                                       ALU.mult).then_inc(dm_masked, 1)
                                    if on_x:
                                        pool.wait_ge(erowed, gi + 1)
                                        h0 = 4 * (gi % 2)
                                        pool.tensor_tensor(qd[:, units(gi)], qd[:, units(gi)], qT[:, h0:h0 + 4, xcols(gi)], ALU.mult)
                                    pool.wait_ge(dm_masked, gi + 1)
                                    pool.tensor_copy(kdec[:, units(gi)], dm[:, units(gi), last])

                    with ExitStack() as inner:
                        ssem = stage_sems(inner, f"inverse{step}_")
                        t_init, x_done, xk_done, tx_done = (ssem(n) for n in ("t_init", "x_done", "xk_done", "tx_done"))
                        t_done, turned, tt_done = (ssem(n) for n in ("t_done", "turned", "tt_done"))
                        with nc.Block() as block:
                            @block.tensor
                            def _(pe):
                                for lv in range(LEVELS):
                                    for gi in range(GRP):
                                        if lv:
                                            pe.wait_ge(t_done, GRP * (lv - 1) + gi + 1)
                                            pe.wait_ge(tt_done, GRP * (lv - 1) + gi + 1)
                                        for m in range(4):
                                            u = unit(gi, m)
                                            rhs = half_cols(tm[:, u] if lv else ident, lv, gi // 2)
                                            ins = pe.matmul(ps[:, gi, 64 * m:64 * m + 64], nt[:, u], rhs, start=True, stop=True)
                                        ins.then_inc(x_done, 1)
                                    if lv:
                                        for gi in range(GRP):
                                            pe.wait_ge(xk_done, GRP * lv + gi + 1)
                                            for m in range(4):
                                                u = unit(gi, m)
                                                ins = pe.matmul(ps[:, 4 + gi, 64 * m:64 * m + 64], tt[:, u], xk[:, u], start=True, stop=True)
                                            ins.then_inc(tx_done, 1)
                                    for gi in range(GRP):
                                        pe.wait_ge(t_done, GRP * lv + gi + 1)
                                        transpose_in(pe, gi, lambda m: tm[:, unit(gi, m)], 4).then_inc(turned, 1)

                            @block.vector
                            def _(dve):
                                dve.wait_ge(t_init, 1)
                                for lv in range(LEVELS):
                                    for gi in range(GRP):
                                        d, t = gi // 2, tok(gi)
                                        dve.wait_ge(x_done, GRP * lv + gi + 1)
                                        for m in range(4):
                                            u = unit(gi, m)
                                            ins = dve.scalar_tensor_tensor(out=xk[:, u], in0=ps[:, gi, 64 * m:64 * m + 64], scalar=beta[:, t, u:u + 1],
                                                                           in1=lev[:, d, lv], op0=ALU.mult, op1=ALU.mult)
                                        ins.then_inc(xk_done, 1)
                                    for gi in range(GRP):
                                        if lv:
                                            dve.wait_ge(tx_done, GRP * (lv - 1) + gi + 1)
                                            term = ps[:, 4 + gi, 0:4 * 64].rearrange("p (u c) -> p u c", u=4)
                                        else:
                                            dve.wait_ge(xk_done, gi + 1)
                                            term = xk[:, units(gi)]
                                        part = half_cols(tm[:, units(gi)], lv, gi // 2)
                                        dve.tensor_tensor(part, part, packed_cols(term, lv), ALU.subtract).then_inc(t_done, 1)
                                for gi in range(GRP):
                                    dve.wait_ge(tt_done, GRP * (LEVELS - 1) + gi + 1)
                                    for m in range(4):
                                        u = unit(gi, m)
                                        dve.tensor_scalar(tm[:, u], tt[:, u], beta[:, tok(gi), u:u + 1], None, ALU.mult)

                            @block.scalar
                            def _(act):
                                for n in range(GRP * LEVELS):
                                    gi = n % GRP
                                    act.wait_ge(turned, n + 1)
                                    act.copy(tt[:, units(gi)], ps[:, gi].rearrange("p (u c) -> p u c", u=4)).then_inc(tt_done, 1)

                            @block.gpsimd
                            def _(pool):
                                pool.tensor_copy(tm[:, :, :], ident.unsqueeze(1).to_broadcast([P, 2 * H, P])).then_inc(t_init, 1)
                                for gi in range(GRP):
                                    pool.wait_ge(tt_done, GRP * (LEVELS - 1) + gi + 1)
                                    for m in range(4):
                                        u = unit(gi, m)
                                        pool.tensor_scalar(nt[:, u], tt[:, u], nbeg[:, tok(gi), u:u + 1], None, ALU.mult)

                    with ExitStack() as inner:
                        ssem = stage_sems(inner, f"scan{step}_")
                        w_done, wt_done, vn_done, vdec_done, vn_copied = (ssem(n) for n in ("w_done", "wt_done", "vn_done", "vdec_done", "vn_copied"))
                        o_done, o_added, s_done, s_added = (ssem(n) for n in ("o_done", "o_added", "s_done", "s_added"))
                        more = step < 2 * TT - 1
                        with nc.Block() as block:
                            @block.tensor
                            def _(pe):
                                def new_v(gi):
                                    pe.wait_ge(wt_done, gi + 1)
                                    if gi >= 2:
                                        pe.wait_ge(vn_copied if on_x else vdec_done, gi - 1)
                                    for m in range(4):
                                        u = unit(gi, m)
                                        ins = pe.matmul(ps[:, 2 + gi % 2, quarter(m)], tm[:, u], vtok[:, tok(gi), cols(gi, m)], start=True, stop=step == 0)
                                        if step:
                                            ins = pe.matmul(ps[:, 2 + gi % 2, quarter(m)], dm[:, u], state[:, u], start=False, stop=True)
                                    ins.then_inc(vn_done, 1)

                                def outputs(gi):
                                    pe.wait_ge(vn_copied, gi + 1)
                                    if gi >= 2:
                                        pe.wait_ge(o_added, gi - 1)
                                    for m in range(4):
                                        u = unit(gi, m)
                                        pe.matmul(ps[:, 6 + gi % 2, quarter(m)], qd[:, u], state[:, u], start=True, stop=False)
                                        ins = pe.matmul(ps[:, 6 + gi % 2, quarter(m)], sc[:, u], vn[:, gi % 2, m], start=False, stop=True)
                                    ins.then_inc(o_done, 1)

                                def next_state(gi):
                                    pe.wait_ge(vdec_done, gi + 1)
                                    if gi >= 2:
                                        pe.wait_ge(s_added, gi - 1)
                                    for m in range(4):
                                        ins = pe.matmul(ps[:, 4 + gi % 2, quarter(m)], ktok[:, tok(gi), cols(gi, m)], vdec[:, gi % 2, m],
                                                        start=True, stop=True)
                                    ins.then_inc(s_done, 1)

                                for gi in range(GRP):
                                    if gi >= 2:
                                        pe.wait_ge(wt_done, gi - 1)
                                    for m in range(4):
                                        ins = pe.matmul(ps[:, gi % 2, quarter(m)], ktok[:, tok(gi), cols(gi, m)], nt[:, unit(gi, m)], start=True, stop=True)
                                    ins.then_inc(w_done, 1)
                                new_v(0)
                                new_v(1)
                                for gi in range(GRP):
                                    if on_x:
                                        outputs(gi)
                                    if more:
                                        next_state(gi)
                                    if gi + 2 < GRP:
                                        new_v(gi + 2)

                            @block.scalar
                            def _(act):
                                for gi in range(GRP):
                                    act.wait_ge(w_done, gi + 1)
                                    act.copy(dm[:, units(gi)], ps[:, gi % 2].rearrange("p (u c) -> p u c", u=4)).then_inc(wt_done, 1)
                                if on_x:
                                    for gi in range(GRP):
                                        if more:
                                            act.wait_ge(vdec_done, gi + 1)
                                        else:
                                            act.wait_ge(vn_done, gi + 1)
                                        if gi >= 2:
                                            act.wait_ge(o_done, gi - 1)
                                        act.copy(vn[:, gi % 2], ps[:, 2 + gi % 2].rearrange("p (u c) -> p u c", u=4)).then_inc(vn_copied, 1)

                            @block.vector
                            def _(dve):
                                def decayed(gi):
                                    dve.wait_ge(vn_done, gi + 1)
                                    if gi >= 2:
                                        dve.wait_ge(s_done, gi - 1)
                                    dve.tensor_tensor(vdec[:, gi % 2], ps[:, 2 + gi % 2].rearrange("p (u c) -> p u c", u=4),
                                                      kdec[:, units(gi)].unsqueeze(2).to_broadcast([P, 4, P]), ALU.mult).then_inc(vdec_done, 1)

                                def finish(gi):
                                    if on_x:
                                        x_tile, h0 = tok(gi) - TT, 4 * (gi % 2)
                                        o = otok[:, x_tile, h0 * P:(h0 + 4) * P]
                                        dve.wait_ge(o_done, gi + 1)
                                        if step == TT:
                                            dve.tensor_copy(o, ps[:, 6 + gi % 2]).then_inc(o_added, 1)
                                        else:
                                            dve.tensor_tensor(o, ps[:, 6 + gi % 2], o, ALU.add).then_inc(o_added, 1)
                                    if more:
                                        dve.wait_ge(s_done, gi + 1)
                                        for m in range(4):
                                            u = unit(gi, m)
                                            if step == 0:
                                                ins = dve.tensor_copy(state[:, u], ps[:, 4 + gi % 2, quarter(m)])
                                            else:
                                                ins = dve.scalar_tensor_tensor(out=state[:, u], in0=state[:, u], scalar=glast[:, u:u + 1],
                                                                               in1=ps[:, 4 + gi % 2, quarter(m)], op0=ALU.mult, op1=ALU.add)
                                        ins.then_inc(s_added, 1)

                                if more:
                                    decayed(0)
                                    decayed(1)
                                for gi in range(GRP):
                                    finish(gi)
                                    if more and gi + 2 < GRP:
                                        decayed(gi + 2)
            qkv.close()

            mods = sb(first, "mods", [P, 4, D])
            branches = first.enter_context(ExitStack())
            gates = sb(branches, "gates", [P, 2, TT, D])
            ygT = sb(branches, "ygT", [P, KT, L])
            ysT = sb(branches, "ysT", [P, KT, L])
            with ExitStack() as scope:
                zs = sb(scope, "zs", [P, TT, D])
                uu = sb(scope, "uu", [P, TT, D])
                vv = sb(scope, "vv", [P, TT, D])
                spw = sb(scope, "spw", [P, H, P])
                spwT = sb(scope, "spwT", [P, H, P])
                spb_row = sb(scope, "spb_row", [H, P])
                spb = sb(scope, "spb", [P, H])
                ln_rows = sb(scope, "ln_rows", [P, 2, D])
                gn_row = sb(scope, "gn_row", [P, P])
                osq = sb(scope, "osq", [P, TT, D])
                orms = sb(scope, "orms", [P, TT * H])
                bn = sb(scope, "bn", [P, TT, 2, 6])
                mv = sb(scope, "mv", [P, TT, 2])
                ssem = stage_sems(scope, "zuvg_")
                loaded, turned, turned_copied, proj, moved = (ssem(n) for n in ("loaded", "turned", "turned_copied", "proj", "moved"))
                o_step, o_std, v_step, v_std, v_out = (ssem(n) for n in ("o_step", "o_std", "v_step", "v_std", "v_out"))
                bias_loaded = ssem("bias_loaded")
                dot, total, put = ada_side(scope, "rest", [(rest[k], [(cact[:, 0], mods[:, k // 2, k % 2 * PANEL:(k % 2 + 1) * PANEL])])
                                                           for k in range(8)], [0])
                BANKS = 6
                dests = [(zs, ACT.Silu)] * 2 + [(uu, ACT.Gelu_apprx_tanh)] * 2 + [(vv, ACT.Gelu_apprx_tanh)] * 2
                dests += [(gates[:, 0], ACT.Sigmoid)] * 2 + [(gates[:, 1], ACT.Sigmoid)] * 2
                oh = otok[:, :, :].rearrange("p t (h d) -> p (t h) d", h=H)
                with nc.Block() as block:
                    @block.sync
                    def _(sp):
                        sp.dma_start(spw[:, :, :], w["sgu_w"][0].rearrange("g p q -> p g q")).then_inc(loaded, 16)
                        sp.dma_start(spb_row[:, :], w["sgu_b"][0]).then_inc(loaded, 16)
                        sp.dma_start(ln_rows[:, 0], row_bcast(w["sgu_ln_g"][0])).then_inc(loaded, 16)
                        sp.dma_start(ln_rows[:, 1], row_bcast(w["sgu_ln_b"][0])).then_inc(loaded, 16)
                        sp.dma_start(gn_row[:, :], row_bcast(w["gdn_norm_g"][0])).then_inc(loaded, 16)
                        for r in range(4):
                            sp.dma_start(mods[:, r], row_bcast(w["ada_b"][0, (2 + r) * D:(3 + r) * D])).then_inc(bias_loaded, 16)
                        stream.issue(sp, merge[0] + RING)

                    @block.tensor
                    def _(pe):
                        pe.wait_ge(loaded, 80)
                        transpose_in(pe, 0, lambda i: spw[:, i], 4)
                        transpose_in(pe, 1, lambda i: spw[:, 4 + i], 4)
                        pe.transpose(ps[:, 2, 0:H], spb_row[:, :], ident[0:H, 0:H]).then_inc(turned, 1)
                        for i in range(10 * TT):
                            n, t = zuvg[i // TT], i % TT
                            if t == 0:
                                pe.wait_ge(*stream.arrive(n))
                            if i == 0:
                                pe.wait_ge(turned_copied, 1)
                            if i >= BANKS:
                                pe.wait_ge(moved, i - BANKS + 1)
                            for kt in range(KT):
                                ins = pe.matmul(ps[:, 2 + i % BANKS], hTx[:, kt, t * P:(t + 1) * P], stream.slot(n)[:, kt],
                                                start=(kt == 0), stop=(kt == KT - 1))
                            ins.then_inc(proj, 1)
                            if t == TT - 1:
                                pe.drain().then_inc(stream.used, 1)
                                if i // TT < 8:
                                    total(pe, i // TT)

                    @block.scalar
                    def _(act):
                        act.wait_ge(turned, 1)
                        for i in range(2):
                            act.copy(spwT[:, 4 * i:4 * i + 4], ps[:, i].rearrange("p (g q) -> p g q", g=4))
                        act.copy(spb[:, :], ps[:, 2, 0:H]).then_inc(turned_copied, 1)
                        act.wait_ge(o_step, 3)
                        act.activation(orms[:, :], orms[:, :], ACT.Sqrt).then_inc(o_std, 1)
                        for i in range(10 * TT):
                            dst, func = dests[i // TT]
                            half = slice(i // TT % 2 * PANEL, i // TT % 2 * PANEL + PANEL)
                            act.wait_ge(proj, i + 1)
                            act.activation(dst[:, i % TT, half], ps[:, 2 + i % BANKS], func).then_inc(moved, 1)
                        act.wait_ge(v_step, 2 * TT)
                        act.activation(mv[:, :, 1], mv[:, :, 1], ACT.Sqrt, bias=eps[:, 0:1]).then_inc(v_std, 1)

                    @block.vector
                    def _(dve):
                        dve.wait_ge(turned_copied, 1)
                        dve.wait_ge(bias_loaded, 64)
                        dot(dve, 0)
                        dve.tensor_tensor(osq[:, :, :], otok[:, :, :], otok[:, :, :], ALU.mult).then_inc(o_step, 1)
                        dve.wait_ge(o_step, 1)
                        dve.tensor_reduce(orms[:, :], osq[:, :, :].rearrange("p t (h d) -> p (t h) d", h=H), AX.X, ALU.add).then_inc(o_step, 1)
                        dve.wait_ge(o_step, 2)
                        dve.tensor_scalar(orms[:, :], orms[:, :], 1.0 / P, EPS, ALU.mult, ALU.add).then_inc(o_step, 1)
                        dve.wait_ge(o_std, 1)
                        dve.reciprocal(orms[:, :], orms[:, :]).then_inc(o_step, 1)
                        dve.wait_ge(o_step, 4)
                        dve.tensor_tensor(oh, oh, orms[:, :].unsqueeze(2).to_broadcast([P, TT * H, P]), ALU.mult).then_inc(o_step, 1)
                        dve.wait_ge(o_step, 5)
                        dve.wait_ge(loaded, 80)
                        dve.tensor_tensor(oh, oh, gn_row[:, :].unsqueeze(1).to_broadcast([P, TT * H, P]), ALU.mult).then_inc(o_step, 1)
                        dve.wait_ge(o_step, 6)
                        for k in range(1, 4):
                            dot(dve, k)
                            put(dve, k - 1)
                        dve.wait_ge(moved, 2 * TT)
                        dve.tensor_tensor(otok[:, :, :], otok[:, :, :], zs[:, :, :], ALU.mult)
                        for k in range(4, 7):
                            dot(dve, k)
                            put(dve, k - 1)
                        for t in range(TT):
                            dve.wait_ge(moved, 6 * TT)
                            for j in range(2):
                                ins = dve.bn_stats(bn[:, t, j], vv[:, t, j * 512:j * 512 + 512])
                            ins.then_inc(v_step, 1)
                            dve.wait_ge(v_step, 2 * t + 1)
                            dve.bn_aggr(mv[:, t], bn[:, t]).then_inc(v_step, 1)
                        dot(dve, 7)
                        put(dve, 6)
                        put(dve, 7)
                        dve.wait_ge(v_std, 1)
                        dve.reciprocal(mv[:, :, 1], mv[:, :, 1]).then_inc(v_out, 1)
                        dve.wait_ge(v_out, 1)
                        for t in range(TT):
                            dve.tensor_scalar(vv[:, t], vv[:, t], mv[:, t, 0:1], mv[:, t, 1:2], ALU.subtract, ALU.mult).then_inc(v_out, 1)
                            dve.wait_ge(v_out, 3 * t + 2)
                            dve.tensor_tensor(vv[:, t], vv[:, t], ln_rows[:, 0], ALU.mult).then_inc(v_out, 1)
                            dve.wait_ge(v_out, 3 * t + 3)
                            dve.tensor_tensor(vv[:, t], vv[:, t], ln_rows[:, 1], ALU.add).then_inc(v_out, 1)

                with ExitStack() as inner:
                    ssem = stage_sems(inner, "sgu_")
                    mixed, gated, turned, moved = (ssem(n) for n in ("mixed", "gated", "turned", "moved"))
                    with nc.Block() as block:
                        @block.tensor
                        def _(pe):
                            for i in range(2 * TT):
                                t, g0 = i // 2, 4 * (i % 2)
                                for m in range(4):
                                    ins = pe.matmul(ps[:, i, m * P:(m + 1) * P], spwT[:, g0 + m], vv[:, t, (g0 + m) * P:(g0 + m + 1) * P],
                                                    start=True, stop=True)
                                ins.then_inc(mixed, 1)
                            for i in range(KT):
                                src = otok if i < KT // 2 else uu
                                if i >= 4:
                                    pe.wait_ge(moved, i - 3)
                                if i == KT // 2:
                                    pe.wait_ge(gated, 2 * TT)
                                kt = 2 * (i % (KT // 2))
                                transpose_in(pe, 4 + i % 4, lambda m: src[:, m % TT, (kt + m // TT) * P:(kt + m // TT + 1) * P], 4).then_inc(turned, 1)

                        @block.vector
                        def _(dve):
                            for i in range(2 * TT):
                                t, g0 = i // 2, 4 * (i % 2)
                                dve.wait_ge(mixed, i + 1)
                                for m in range(4):
                                    g = g0 + m
                                    part = uu[:, t, g * P:(g + 1) * P]
                                    ins = dve.scalar_tensor_tensor(out=part, in0=ps[:, i, m * P:(m + 1) * P], scalar=spb[:, g:g + 1],
                                                                   in1=part, op0=ALU.add, op1=ALU.mult)
                                ins.then_inc(gated, 1)

                        @block.scalar
                        def _(act):
                            for i in range(KT):
                                dst = ygT if i < KT // 2 else ysT
                                kt = 2 * (i % (KT // 2))
                                act.wait_ge(turned, i + 1)
                                act.copy(dst[:, kt:kt + 2], ps[:, 4 + i % 4].rearrange("p (k t) -> p k t", k=2)).then_inc(moved, 1)

            mod2_x, mod2_c = ([high.enter_context(nc.sbuf_tensor(f"mod2_{n}0", [P, 3, D], F32, side="right"))] for n in "xc")
            half_row = lambda m, i: m[:, i // 2, i % 2 * PANEL:(i % 2 + 1) * PANEL]
            with ExitStack() as scope:
                merged = sb(scope, "merged", [P, TT, D])
                part_b = sb(scope, "part_b", [P, TT, D])
                mT = sb(scope, "mT", [P, KT, L])
                ssem = stage_sems(scope, "merge_")
                proj, gated, summed, turned, moved, outed, scaled, added = (
                    ssem(n) for n in ("proj", "gated", "summed", "turned", "moved", "outed", "scaled", "added"))
                bias_loaded = ssem("bias_loaded")
                BANKS = 6
                dot, total, put = ada_side(scope, "ada20", [(ada2[0][k], [(cact[:, 2], half_row(mod2_x[0], k)), (cact[:, 3], half_row(mod2_c[0], k))])
                                                            for k in range(6)], [6, 7])
                with nc.Block() as block:
                    @block.sync
                    def _(sp):
                        for m in (mod2_x[0], mod2_c[0]):
                            sp.dma_start(m[:, :, :].rearrange("p r d -> p (r d)"), row_bcast(w["b_ada_2"][0])).then_inc(bias_loaded, 16)
                        stream.issue(sp, MOE + RING)

                    @block.tensor
                    def _(pe):
                        for i in range(4):
                            n = merge[i]
                            pe.wait_ge(*stream.arrive(n))
                            for t in range(TT):
                                if TT * i + t >= BANKS:
                                    pe.wait_ge(gated, TT * i + t - BANKS + 1)
                                for kt in range(KT):
                                    ins = pe.matmul(ps[:, (TT * i + t) % BANKS], (ygT, ysT)[i // 2][:, kt, t * P:(t + 1) * P], stream.slot(n)[:, kt],
                                                    start=(kt == 0), stop=(kt == KT - 1))
                                ins.then_inc(proj, 1)
                            pe.drain().then_inc(stream.used, 1)
                            total(pe, i)
                        pe.wait_ge(summed, 2 * TT)
                        for i in range(4):
                            transpose_in(pe, i, lambda m: merged[:, m % TT, (2 * i + m // TT) * P:(2 * i + m // TT + 1) * P], 4).then_inc(turned, 1)
                        for i in range(2):
                            n = merge[4 + i]
                            pe.wait_ge(*stream.arrive(n))
                            pe.wait_ge(moved, 4)
                            for t in range(TT):
                                for kt in range(KT):
                                    ins = pe.matmul(ps[:, (4 + TT * i + t) % BANKS], mT[:, kt, t * P:(t + 1) * P], stream.slot(n)[:, kt],
                                                    start=(kt == 0), stop=(kt == KT - 1))
                                ins.then_inc(outed, 1)
                            pe.drain().then_inc(stream.used, 1)
                            total(pe, 4 + i)

                    @block.vector
                    def _(dve):
                        dve.wait_ge(bias_loaded, 32)
                        for i in range(4 * TT):
                            if i % TT == 0:
                                dot(dve, i // TT)
                                if i:
                                    put(dve, i // TT - 1)
                            b, half, t = i // (2 * TT), i // TT % 2, i % TT
                            cols = slice(half * PANEL, half * PANEL + PANEL)
                            dve.wait_ge(proj, i + 1)
                            dve.tensor_tensor((merged, part_b)[b][:, t, cols], ps[:, i % BANKS], gates[:, b, t, cols], ALU.mult).then_inc(gated, 1)
                        for i in range(2 * TT):
                            t, cols = i % TT, slice(i // TT * PANEL, i // TT * PANEL + PANEL)
                            dve.wait_ge(gated, 2 * TT + i + 1)
                            dve.tensor_tensor(merged[:, t, cols], merged[:, t, cols], part_b[:, t, cols], ALU.add).then_inc(summed, 1)
                        for i in range(2 * TT):
                            t, cols = i % TT, slice(i // TT * PANEL, i // TT * PANEL + PANEL)
                            if t == 0:
                                dot(dve, 4 + i // TT)
                                put(dve, 3 + i // TT)
                            dve.wait_ge(outed, i + 1)
                            dve.tensor_tensor(part_b[:, t, cols], ps[:, (4 + i) % BANKS], mods[:, 0, cols], ALU.mult).then_inc(scaled, 1)
                            dve.wait_ge(scaled, i + 1)
                            dve.tensor_tensor(xs[:, t, cols], xs[:, t, cols], part_b[:, t, cols], ALU.add).then_inc(added, 1)
                        put(dve, 5)

                    @block.scalar
                    def _(act):
                        for i in range(4):
                            act.wait_ge(turned, i + 1)
                            act.copy(mT[:, 2 * i:2 * i + 2], ps[:, i].rearrange("p (k t) -> p k t", k=2)).then_inc(moved, 1)
            branches.close()

            with ExitStack() as ffn:
                hS = sb(ffn, "hS", [P, KT, SLOTS])
                back = sb(ffn, "back", [P, SB, L])
                first_slot = sb(ffn, "first_slot", [P, N_EXPERTS], I32)
                extra_ids = sb(ffn, "extra_ids", [P, OVERFLOW], I32)
                with ExitStack() as scope:
                    grow = sb(scope, "grow", [P, D])
                    gm = sb(scope, "gm2", [P, D])
                    h2 = sb(scope, "h2", [P, TT, D])
                    h2T = sb(scope, "h2T", [P, KT, L])
                    slots = sb(scope, "slots", [P, SLOTS])
                    pick = sb(scope, "pick", [P, TT, SLOTS])
                    pick2 = sb(scope, "pick2", [P, SLOTS])
                    wide32 = lambda n: sb(scope, n, [P, TT, GROUPS, PER_GROUP])
                    full1, full2, either, rank, late = (wide32(n) for n in ("full1", "full2", "either", "rank", "late"))
                    row32 = lambda n: sb(scope, n, [P, N_EXPERTS])
                    count, kept, off, over, nth, alt = (row32(n) for n in ("count", "kept", "off", "over", "nth", "alt"))
                    extra_f = sb(scope, "extra_f", [P, OVERFLOW])
                    slot_of = [sb(scope, f"slot_of{j}", [P, TT, 1]) for j in range(TOP_K)]
                    sqr = sb(scope, "sqr", [P, D])
                    wr = sb(scope, "wr", [P, KT, ROUTER])
                    br = sb(scope, "br", [P, ROUTER])
                    logits = sb(scope, "logits", [P, TT, ROUTER])
                    order = sb(scope, "order", [P, PER_GROUP])
                    one = lambda n, k: sb(scope, n, [P, TT, k])
                    gtop, gdiff, gexp, ghot, gprob = one("gtop", 1), one("gdiff", GROUPS), one("gexp", GROUPS), one("ghot", GROUPS), one("gprob", 1)
                    chosen = sb(scope, "chosen", [P, TT, GROUPS, PER_GROUP])
                    lin, top, hot1, hot2, tie = (one("lin", PER_GROUP), one("top", 1), one("hot1", PER_GROUP), one("hot2", PER_GROUP),
                                                 one("tie", PER_GROUP))
                    e2, w_1, w_2 = one("e2", 1), one("w_1", 1), one("w_2", 1)
                    ssem = stage_sems(scope, "route_")
                    loaded, squares, steps, std, turned, moved, routed, ge_done, e2_done, chain, ordered, chosen_done, ranked, picked, gathered, got_a, got_v, gates_done, back_turned, back_moved = (
                        ssem(n) for n in ("loaded", "squares", "steps", "std", "turned", "moved", "routed", "ge_done", "e2_done", "chain", "ordered", "chosen_done",
                                          "ranked", "picked", "gathered", "got_a", "got_v", "gates_done", "back_turned", "back_moved"))
                    with nc.Block() as block:
                        @block.sync
                        def _(sp):
                            sp.dma_start(grow[:, :], row_bcast(w["norm_ffn_g"][0])).then_inc(loaded, 16)
                            sp.dma_start(wr[:, :, 0:GROUPS], ktp(w["router_group_w"][0])).then_inc(loaded, 16)
                            sp.dma_start(wr[:, :, GROUPS:], ktp(w["router_expert_w"][0])).then_inc(loaded, 16)
                            sp.dma_start(br[:, 0:GROUPS], row_bcast(w["router_group_b"][0])).then_inc(loaded, 16)
                            sp.dma_start(br[:, GROUPS:], row_bcast(w["router_expert_b"][0])).then_inc(loaded, 16)
                            at, n = parts["slots"]
                            sp.dma_start(slots[:, :], const_dram[:, at:at + n]).then_inc(loaded, 16)

                        @block.gpsimd
                        def _(pool):
                            for i in range(PER_GROUP):
                                ins = pool.memset(order[:, i:i + 1], float(PER_GROUP - i))
                            ins.then_inc(ordered, 1)

                        @block.scalar
                        def _(act):
                            for t in range(TT):
                                if t:
                                    act.wait_ge(squares, t)
                                act.activation(sqr[:, :], xs[:, t], ACT.Square, accum_out=stat[:, t:t + 1]).then_inc(squares, 1)
                            act.wait_ge(steps, 1)
                            act.activation(stat[:, 2:4], stat[:, 2:4], ACT.Sqrt).then_inc(std, 1)
                            for i in range(4):
                                act.wait_ge(turned, i + 1)
                                act.copy(h2T[:, 2 * i:2 * i + 2], ps[:, i].rearrange("p (k t) -> p k t", k=2)).then_inc(moved, 1)
                            act.wait_ge(chain, 3)
                            act.activation(gexp[:, :, :], gdiff[:, :, :], ACT.Exp).then_inc(ge_done, 1)
                            act.wait_ge(chain, 17)
                            act.activation(e2[:, :, :], top[:, :, :], ACT.Exp).then_inc(e2_done, 1)
                            for kt in range(KT):
                                act.wait_ge(gathered, 2 * kt + 1)
                                act.copy(hS[:, kt, 0:MAIN], ps[:, 2 * kt % 8]).then_inc(got_a, 1)
                            for i in range((SB + 1) // 2):
                                n = min(2, SB - 2 * i)
                                act.wait_ge(back_turned, i + 1)
                                act.copy(back[:, 2 * i:2 * i + n], ps[:, i, 0:n * L].rearrange("p (b t) -> p b t", b=n)).then_inc(back_moved, 1)

                        @block.tensor
                        def _(pe):
                            pe.wait_ge(steps, 3 + 2 * TT)
                            for i in range(4):
                                transpose_in(pe, i, lambda m: h2[:, m % TT, (2 * i + m // TT) * P:(2 * i + m // TT + 1) * P], 4).then_inc(turned, 1)
                            pe.wait_ge(moved, 4)
                            pe.wait_ge(loaded, 96)
                            for t in range(TT):
                                for kt in range(KT):
                                    ins = pe.matmul(ps[:, 4, ROUTER * t:ROUTER * (t + 1)], h2T[:, kt, t * P:(t + 1) * P], wr[:, kt],
                                                    start=(kt == 0), stop=(kt == KT - 1))
                            ins.then_inc(routed, 1)
                            pe.wait_ge(chosen_done, 1)
                            flat = either[:, :, :, :].rearrange("p t g e -> p t (g e)")
                            pe.matmul(ps[:, 5, 0:N_EXPERTS], tri[:, 0], flat[:, 0], start=True, stop=True)
                            pe.matmul(ps[:, 5, N_EXPERTS:2 * N_EXPERTS], tri[:, 0], flat[:, 1], start=True, stop=False)
                            pe.matmul(ps[:, 5, N_EXPERTS:2 * N_EXPERTS], ones, flat[:, 0], start=False, stop=True)
                            pe.matmul(ps[:, 5, 2 * N_EXPERTS:3 * N_EXPERTS], ones, flat[:, 0], start=True, stop=False)
                            pe.matmul(ps[:, 5, 2 * N_EXPERTS:3 * N_EXPERTS], ones, flat[:, 1], start=False, stop=True).then_inc(ranked, 1)
                            pe.wait_ge(picked, TT)
                            for i in range(2 * KT):
                                kt, part = i // 2, slice(0, MAIN) if i % 2 == 0 else slice(MAIN, SLOTS)
                                if i >= 8:
                                    pe.wait_ge(got_a if i % 2 == 0 else got_v, i // 2 - 3)
                                for t in range(TT):
                                    ins = pe.matmul(ps[:, i % 8, 0:part.stop - part.start], h2[:, t, kt * P:(kt + 1) * P], pick[:, t, part],
                                                    start=(t == 0), stop=(t == TT - 1))
                                ins.then_inc(gathered, 1)
                            pe.wait_ge(gates_done, TT)
                            pe.wait_ge(got_a, KT)
                            pe.wait_ge(got_v, KT)
                            for i in range((SB + 1) // 2):
                                n = min(2, SB - 2 * i)
                                transpose_in(pe, i, lambda m: pick[:, m % TT, (2 * i + m // TT) * P:(2 * i + m // TT + 1) * P], n * TT).then_inc(back_turned, 1)

                        @block.vector
                        def _(dve):
                            dve.wait_ge(squares, TT)
                            dve.tensor_scalar(stat[:, 2:4], stat[:, 0:2], 1.0 / D, EPS, ALU.mult, ALU.add).then_inc(steps, 1)
                            dve.wait_ge(loaded, 96)
                            dve.scalar_tensor_tensor(out=gm[:, :], in0=mods[:, 2], scalar=1.0, in1=grow[:, :], op0=ALU.add, op1=ALU.mult).then_inc(steps, 1)
                            dve.wait_ge(std, 1)
                            dve.reciprocal(stat[:, 4:6], stat[:, 2:4]).then_inc(steps, 1)
                            dve.wait_ge(steps, 3)
                            for t in range(TT):
                                norm_modulate(dve, steps, 3 + 2 * t, xs[:, t], stat[:, 4 + t:5 + t], gm[:, :], mods[:, 1],
                                              h2[:, t], h2[:, t]).then_inc(steps, 1)
                            link = chained(dve, chain)
                            wide = lambda a, n: a[:, :, :].to_broadcast([P, TT, n])
                            dve.wait_ge(routed, 1)
                            dve.wait_ge(ordered, 1)
                            link(dve.tensor_tensor(logits[:, :, :], ps[:, 4, 0:TT * ROUTER].rearrange("p (t r) -> p t r", t=TT),
                                                   br[:, :].unsqueeze(1).to_broadcast([P, TT, ROUTER]), ALU.add))
                            group, expert = logits[:, :, 0:GROUPS], logits[:, :, GROUPS:].rearrange("p t (g e) -> p t g e", g=GROUPS)
                            link(dve.tensor_reduce(gtop[:, :, :], group, AX.X, ALU.max))
                            link(dve.tensor_tensor(gdiff[:, :, :], group, wide(gtop, GROUPS), ALU.subtract))

                            def first_top(hot, diff, n):
                                weights = order[:, PER_GROUP - n:].unsqueeze(1).to_broadcast([P, TT, n])
                                link(dve.tensor_scalar(hot, diff, 0.0, None, ALU.is_ge))
                                link(dve.tensor_tensor(hot, hot, weights, ALU.mult))
                                link(dve.tensor_reduce(gtop[:, :, :], hot, AX.X, ALU.max))
                                link(dve.tensor_tensor(hot, hot, wide(gtop, n), ALU.is_equal))

                            first_top(ghot[:, :, :], gdiff[:, :, :], GROUPS)
                            link(dve.tensor_tensor(chosen[:, :, :, :], expert, ghot[:, :, :].unsqueeze(3).to_broadcast([P, TT, GROUPS, PER_GROUP]),
                                                   ALU.mult))
                            link(dve.tensor_reduce(lin[:, :, :], chosen[:, :, :, :].rearrange("p t g e -> p t e g"), AX.X, ALU.add))
                            link(dve.tensor_reduce(top[:, :, :], lin[:, :, :], AX.X, ALU.max))
                            link(dve.tensor_tensor(lin[:, :, :], lin[:, :, :], wide(top, PER_GROUP), ALU.subtract))
                            first_top(hot1[:, :, :], lin[:, :, :], PER_GROUP)
                            link(dve.scalar_tensor_tensor(out=lin[:, :, :], in0=hot1[:, :, :], scalar=MASKED, in1=lin[:, :, :],
                                                          op0=ALU.mult, op1=ALU.add))
                            link(dve.tensor_reduce(top[:, :, :], lin[:, :, :], AX.X, ALU.max))
                            link(dve.tensor_tensor(tie[:, :, :], lin[:, :, :], wide(top, PER_GROUP), ALU.subtract))
                            first_top(hot2[:, :, :], tie[:, :, :], PER_GROUP)
                            over_groups = lambda a: a.unsqueeze(2).to_broadcast([P, TT, GROUPS, PER_GROUP])
                            group_hot = ghot[:, :, :].unsqueeze(3).to_broadcast([P, TT, GROUPS, PER_GROUP])
                            link(dve.tensor_tensor(full1[:, :, :, :], group_hot, over_groups(hot1[:, :, :]), ALU.mult))
                            link(dve.tensor_tensor(full2[:, :, :, :], group_hot, over_groups(hot2[:, :, :]), ALU.mult))
                            dve.tensor_tensor(either[:, :, :, :], full1[:, :, :, :], full2[:, :, :, :], ALU.add).then_inc(chosen_done, 1)
                            dve.wait_ge(ge_done, 1)
                            link(dve.tensor_reduce(gprob[:, :, :], gexp[:, :, :], AX.X, ALU.add))
                            link(dve.reciprocal(gprob[:, :, :], gprob[:, :, :]))
                            dve.wait_ge(e2_done, 1)
                            link(dve.tensor_scalar(w_1[:, :, :], e2[:, :, :], 1.0, None, ALU.add))
                            link(dve.reciprocal(w_1[:, :, :], w_1[:, :, :]))
                            link(dve.tensor_tensor(w_1[:, :, :], w_1[:, :, :], gprob[:, :, :], ALU.mult))
                            link(dve.tensor_tensor(w_2[:, :, :], w_1[:, :, :], e2[:, :, :], ALU.mult))
                            dve.wait_ge(ranked, 1)
                            flat = lambda a: a[:, :, :, :].rearrange("p t g e -> p t (g e)")
                            link(dve.tensor_copy(flat(rank), ps[:, 5, 0:TT * N_EXPERTS].rearrange("p (t e) -> p t e", t=TT)))
                            link(dve.tensor_copy(count[:, :], ps[:, 5, TT * N_EXPERTS:(TT + 1) * N_EXPERTS]))
                            link(dve.tensor_scalar(kept[:, :], count[:, :], float(P), None, ALU.min))
                            link(dve.tensor_tensor_scan(off[:, :], ones[:, 0:N_EXPERTS], kept[:, :], 0.0, ALU.mult, ALU.add))
                            link(dve.tensor_tensor(off[:, :], off[:, :], kept[:, :], ALU.subtract))
                            link(dve.tensor_copy(first_slot[:, :], off[:, :]))
                            link(dve.tensor_scalar(over[:, :], count[:, :], float(P), None, ALU.is_gt))
                            link(dve.tensor_tensor_scan(nth[:, :], ones[:, 0:N_EXPERTS], over[:, :], 0.0, ALU.mult, ALU.add))
                            link(dve.tensor_scalar(alt[:, :], nth[:, :], float(P), float(MAIN - 2 * P), ALU.mult, ALU.add))
                            link(dve.tensor_tensor(alt[:, :], alt[:, :], off[:, :], ALU.subtract))
                            by_token = lambda a: a[:, :].unsqueeze(1).to_broadcast([P, TT, N_EXPERTS])
                            link(dve.tensor_scalar(late[:, :, :, :], rank[:, :, :, :], float(P), None, ALU.is_gt))
                            link(dve.tensor_tensor(flat(late), flat(late), by_token(alt), ALU.mult))
                            link(dve.scalar_tensor_tensor(out=rank[:, :, :, :], in0=rank[:, :, :, :], scalar=-1.0, in1=late[:, :, :, :],
                                                          op0=ALU.add, op1=ALU.add))
                            link(dve.tensor_tensor(flat(rank), flat(rank), by_token(off), ALU.add))
                            for j, full in enumerate((full1, full2)):
                                link(dve.tensor_tensor(full[:, :, :, :], full[:, :, :, :], rank[:, :, :, :], ALU.mult))
                                link(dve.tensor_reduce(slot_of[j][:, :, :], flat(full), AX.X, ALU.add))
                            for t in range(TT):
                                if t:
                                    dve.wait_ge(picked, t)
                                link(dve.tensor_scalar(pick2[:, :], slots[:, :], slot_of[1][:, t], None, ALU.is_equal))
                                dve.scalar_tensor_tensor(out=pick[:, t], in0=slots[:, :], scalar=slot_of[0][:, t], in1=pick2[:, :],
                                                         op0=ALU.is_equal, op1=ALU.add).then_inc(picked, 1)
                            for j in range(OVERFLOW):
                                link(dve.tensor_scalar(alt[:, :], nth[:, :], float(j + 1), None, ALU.is_equal))
                                link(dve.tensor_tensor(alt[:, :], alt[:, :], over[:, :], ALU.mult))
                                link(dve.tensor_tensor(alt[:, :], alt[:, :], slots[:, 0:N_EXPERTS], ALU.mult))
                                link(dve.tensor_reduce(extra_f[:, j:j + 1], alt[:, :], AX.X, ALU.add))
                            link(dve.tensor_copy(extra_ids[:, :], extra_f[:, :]))
                            for kt in range(KT):
                                dve.wait_ge(gathered, 2 * kt + 2)
                                dve.tensor_copy(hS[:, kt, MAIN:], ps[:, (2 * kt + 1) % 8, 0:SLOTS - MAIN]).then_inc(got_v, 1)
                            for t in range(TT):
                                dve.wait_ge(gates_done, t) if t else dve.wait_ge(picked, TT)
                                link(dve.tensor_scalar(pick2[:, :], slots[:, :], slot_of[1][:, t], w_2[:, t], ALU.is_equal, ALU.mult))
                                link(dve.tensor_scalar(pick[:, t], slots[:, :], slot_of[0][:, t], w_1[:, t], ALU.is_equal, ALU.mult))
                                dve.tensor_tensor(pick[:, t], pick[:, t], pick2[:, :], ALU.add).then_inc(gates_done, 1)
                            dve.wait_ge(gates_done, TT)
                yS = sb(ffn, "yS", [P, KT, SLOTS])
                with ExitStack() as scope:
                    silu1 = sb(scope, "silu1", [P, 2, 2, P])
                    hid = sb(scope, "hid", [P, 2, 2, P])
                    xe = sb(scope, "xe", [P, 2, KT, P])
                    ssem = stage_sems(scope, "moe_")
                    x_copied = ssem("x_copied")
                    w1_done, w3_done, silu_done, hid_done, down_done, out_a, out_v = (
                        ssem(n) for n in ("w1_done", "w3_done", "silu_done", "hid_done", "down_done", "out_a", "out_v"))
                    ROUNDS = N_EXPERTS // 2
                    base = [stream.arrive(MOE + k)[1] - 32 for k in range(3)]
                    HK = KT // 2

                    def window(eng, r, j):
                        return bass.ds(eng.value_load(first_slot[0:1, bass.ds(2 * r + j, 1)], min_val=0, max_val=MAIN), P)

                    def behind(j):
                        return slice(MAIN + j * P, MAIN + (j + 1) * P)

                    with nc.Block() as block:
                        @block.sync
                        def _(sp):
                            assert stream.issued == MOE + RING == MOE + 3
                            with sp.Fori(0, ROUNDS - 1) as r:
                                for k in range(3):
                                    n = MOE + k
                                    sp.wait_ge(stream.used, 3 * r + (n + 1))
                                    slot, loaded = stream.slot(n), stream.loaded[n % RING]
                                    e = 2 * r + 2
                                    if k < 2:
                                        sp.dma_start(slot[:, :, 0:D_EXPERT], w1[e + k]).then_inc(loaded, 16)
                                        sp.dma_start(slot[:, :, D_EXPERT:], w3[e + k]).then_inc(loaded, 16)
                                    else:
                                        view = slot.rearrange("p (e f c) n -> p e f (c n)", e=2, f=2)
                                        for j in range(2):
                                            sp.dma_start(view[:, j], w2[e + j]).then_inc(loaded, 16)
                            stream.issued = EXTRA
                            for j in range(OVERFLOW):
                                extra[j] = sp.value_load(extra_ids[0:1, j:j + 1], min_val=0, max_val=N_EXPERTS - 1)
                            stream.issue(sp, EXTRA + 5)
                            extra.clear()
                            stream.issue(sp, ab_in[0] + RING)

                        @block.tensor
                        def _(pe):
                            def up(n, j, tokens):
                                for half, done in enumerate((w1_done, w3_done)):
                                    for f in range(2):
                                        col = half * D_EXPERT + f * P
                                        for kt in range(KT):
                                            ins = pe.matmul(ps[:, 2 * j + half, f * P:(f + 1) * P], stream.slot(n)[:, kt, col:col + P],
                                                            tokens(kt), start=(kt == 0), stop=(kt == KT - 1))
                                    ins.then_inc(done, 1)
                                pe.drain().then_inc(stream.used, 1)

                            def down(n, j):
                                view = stream.slot(n).rearrange("p (e f c) n -> p e f (c n)", e=2, f=2)
                                for k in range(KT):
                                    for f in range(2):
                                        ins = pe.matmul(ps[:, 4 + 2 * j + k // HK, k % HK * P:(k % HK + 1) * P], view[:, j, f, k * P:(k + 1) * P],
                                                        hid[:, j, f], start=(f == 0), stop=(f == 1))
                                    if k % HK == HK - 1:
                                        ins.then_inc(down_done, 1)

                            with pe.Fori(0, ROUNDS) as r:
                                for j in range(2):
                                    pe.wait_ge(stream.loaded[(MOE + j) % RING], 32 * r + (base[j] + 32))
                                    pe.wait_ge(hid_done, 2 * r + (j + 1))
                                    pe.wait_ge(x_copied, 2 * r + (j + 1))
                                    up(MOE + j, j, lambda kt: xe[:, j, kt])
                                pe.wait_ge(stream.loaded[(MOE + 2) % RING], 32 * r + (base[2] + 32))
                                for j in range(2):
                                    pe.wait_ge(hid_done, 2 * r + (j + 3))
                                    pe.wait_ge(out_a, 2 * r + (j + 1))
                                    pe.wait_ge(out_v, 2 * r + (j + 1))
                                    down(MOE + 2, j)
                                pe.drain().then_inc(stream.used, 1)
                            for m in range(OVERFLOW):
                                j, e = m % 2, N_EXPERTS + m
                                if m != 1:
                                    jobs = range(m, min(m + 2, OVERFLOW))
                                    for x in jobs:
                                        n = EXTRA + x + x // 2
                                        pe.wait_ge(*stream.arrive(n))
                                        pe.wait_ge(hid_done, N_EXPERTS + x + 1)
                                        up(n, x % 2, lambda kt: hS[:, kt, behind(x)])
                                    pe.wait_ge(*stream.arrive(EXTRA + (2 if m == 0 else 4)))
                                pe.wait_ge(hid_done, e + 3)
                                pe.wait_ge(out_a, e + 1)
                                pe.wait_ge(out_v, e + 1)
                                down(EXTRA + (2 if m < 2 else 4), j)
                                if m >= 1:
                                    pe.drain().then_inc(stream.used, 1)

                        @block.gpsimd
                        def _(pool):
                            for j in range(2):
                                pool.tensor_copy(xe[:, j], hS[:, :, window(pool, 0, j)]).then_inc(x_copied, 1)
                            with pool.Fori(0, ROUNDS - 1) as r:
                                for j in range(2):
                                    slots_in = window(pool, r + 1, j)
                                    pool.wait_ge(w3_done, 2 * r + (j + 1))
                                    pool.tensor_copy(xe[:, j], hS[:, :, slots_in]).then_inc(x_copied, 1)

                        @block.scalar
                        def _(act):
                            for i in range(2):
                                act.activation(yS[:, 2 * i:2 * i + 2], hS[:, 2 * i:2 * i + 2], ACT.Copy, scale=0.0).then_inc(out_a, 1)

                            def silu(e, j):
                                act.wait_ge(w1_done, e + 1)
                                act.wait_ge(hid_done, e + 1)
                                act.activation(silu1[:, j], ps[:, 2 * j, 0:2 * P].rearrange("p (f t) -> p f t", f=2), ACT.Silu).then_inc(silu_done, 1)

                            def move(e, j, slots_out):
                                act.wait_ge(down_done, 2 * e + 1)
                                act.wait_ge(out_a, e + 2)
                                act.copy(yS[:, 0:HK, slots_out], ps[:, 4 + 2 * j].rearrange("p (k t) -> p k t", k=HK)).then_inc(out_a, 1)

                            with act.Fori(0, ROUNDS) as r:
                                for j in range(2):
                                    silu(2 * r + j, j)
                                for j in range(2):
                                    move(2 * r + j, j, window(act, r, j))
                            for jobs in ((0, 1), (2,)):
                                for m in jobs:
                                    silu(N_EXPERTS + m, m % 2)
                                for m in jobs:
                                    move(N_EXPERTS + m, m % 2, behind(m))

                        @block.vector
                        def _(dve):
                            for j in range(2):
                                dve.memset(hid[:, j], 0.0).then_inc(hid_done, 1)
                            for i in range(2):
                                dve.memset(yS[:, HK + 2 * i:HK + 2 * i + 2], 0.0).then_inc(out_v, 1)

                            def multiply(e, j):
                                dve.wait_ge(w3_done, e + 1)
                                dve.wait_ge(silu_done, e + 1)
                                dve.wait_ge(hid_done, e + 2)
                                dve.tensor_tensor(hid[:, j], silu1[:, j], ps[:, 2 * j + 1, 0:2 * P].rearrange("p (f t) -> p f t", f=2),
                                                  ALU.mult).then_inc(hid_done, 1)

                            def move(e, j, slots_out):
                                dve.wait_ge(down_done, 2 * e + 2)
                                dve.wait_ge(out_v, e + 2)
                                dve.tensor_copy(yS[:, HK:, slots_out], ps[:, 5 + 2 * j].rearrange("p (k t) -> p k t", k=HK)).then_inc(out_v, 1)

                            with dve.Fori(0, ROUNDS) as r:
                                for j in range(2):
                                    multiply(2 * r + j, j)
                                for j in range(2):
                                    move(2 * r + j, j, window(dve, r, j))
                            for jobs in ((0, 1), (2,)):
                                for m in jobs:
                                    multiply(N_EXPERTS + m, m % 2)
                                for m in jobs:
                                    move(N_EXPERTS + m, m % 2, behind(m))

                with ExitStack() as scope:
                    grow = sb(scope, "grow3", [P, D])
                    sqr = sb(scope, "sqr3", [P, D])
                    acc = sb(scope, "acc", [P, TT, D])
                    yslot = hS[:, :, :].rearrange("p k s -> p (k s)").rearrange("p (b d) -> p b d", b=SB)
                    ssem = stage_sems(scope, "final_")
                    loaded, steps, squares, std, turned, moved_a, moved_v, back_done = (
                        ssem(n) for n in ("loaded", "steps", "squares", "std", "turned", "moved_a", "moved_v", "back_done"))
                    with nc.Block() as block:
                        @block.sync
                        def _(sp):
                            sp.dma_start(grow[:, :], row_bcast(w["final_norm_g"])).then_inc(loaded, 16)

                        @block.vector
                        def _(dve):
                            for b in range(SB):
                                dve.wait_ge(turned, 2 * b + 2)
                                dve.tensor_copy(yslot[:, b, PANEL:], ps[:, (2 * b + 1) % 4]).then_inc(moved_v, 1)
                            for t in range(TT):
                                dve.wait_ge(back_done, t + 1)
                                dve.tensor_tensor(acc[:, t].rearrange("p (c n) -> p c n", c=2), ps[:, 4 + 2 * t:6 + 2 * t],
                                                  mods[:, 3].rearrange("p (c n) -> p c n", c=2), ALU.mult).then_inc(steps, 1)
                                dve.wait_ge(steps, 2 * t + 1)
                                dve.tensor_tensor(xs[:, t], xs[:, t], acc[:, t], ALU.add).then_inc(steps, 1)
                            dve.wait_ge(squares, TT)
                            dve.tensor_scalar(stat[:, 2:4], stat[:, 0:2], 1.0 / D, EPS, ALU.mult, ALU.add).then_inc(steps, 1)
                            dve.wait_ge(std, 1)
                            dve.reciprocal(stat[:, 4:6], stat[:, 2:4]).then_inc(steps, 1)
                            dve.wait_ge(steps, 2 * TT + 2)
                            dve.wait_ge(loaded, 16)
                            for t in range(TT):
                                dve.scalar_tensor_tensor(out=xs[:, t], in0=xs[:, t], scalar=stat[:, 4 + t:5 + t], in1=grow[:, :],
                                                         op0=ALU.mult, op1=ALU.mult)

                        @block.tensor
                        def _(pe):
                            for i in range(2 * SB):
                                b, c = i // 2, i % 2
                                if i >= 4:
                                    pe.wait_ge((moved_a, moved_v)[c], b - 1)
                                transpose_in(pe, i % 4, lambda m: yS[:, 4 * c + m, b * P:(b + 1) * P], 4).then_inc(turned, 1)
                            pe.wait_ge(moved_a, SB)
                            pe.wait_ge(moved_v, SB)
                            for t in range(TT):
                                for c in range(2):
                                    for b in range(SB):
                                        ins = pe.matmul(ps[:, 4 + 2 * t + c], back[:, b, t * P:(t + 1) * P], yslot[:, b, c * PANEL:(c + 1) * PANEL],
                                                        start=(b == 0), stop=(b == SB - 1))
                                ins.then_inc(back_done, 1)

                        @block.scalar
                        def _(act):
                            for b in range(SB):
                                act.wait_ge(turned, 2 * b + 1)
                                act.copy(yslot[:, b, 0:PANEL], ps[:, 2 * b % 4]).then_inc(moved_a, 1)
                            for t in range(TT):
                                act.wait_ge(steps, 2 * t + 2)
                                if t:
                                    act.wait_ge(squares, t)
                                act.activation(sqr[:, :], xs[:, t], ACT.Square, accum_out=stat[:, t:t + 1]).then_inc(squares, 1)
                            act.wait_ge(steps, 2 * TT + 1)
                            act.activation(stat[:, 2:4], stat[:, 2:4], ACT.Sqrt).then_inc(std, 1)

        with ExitStack() as second:
            hT = sb(second, "hT", [P, KT, 2 * L])
            gate1 = sb(second, "gate1", [P, D])
            rows2 = second.enter_context(ExitStack())
            mod2_x.append(sb(rows2, "mod2_x1", [P, 3, D]))
            mod2_c.append(sb(rows2, "mod2_c1", [P, 2, D]))
            cs = sb(rows2, "cs2", [P, TT, D])

            def modulate_block(name, layer, load_ctx):
                with ExitStack() as scope:
                    hx = sb(scope, f"{name}_hx", [P, TT, D])
                    hc = sb(scope, f"{name}_hc", [P, TT, D])
                    ssem = stage_sems(scope, f"{name}_")
                    loaded, x_step, c_step, turned, moved_a, moved_v = (ssem(n) for n in ("loaded", "x_step", "c_step", "turned", "moved_a", "moved_v"))


                    with nc.Block() as block:
                        @block.sync
                        def _(sp):
                            if load_ctx:
                                sp.dma_start(cs[:, :, :], w["ctx_2"][0].rearrange("(t p) d -> p t d", p=P)).then_inc(loaded, 16)

                        @block.vector
                        def _(dve):
                            for t in range(TT):
                                dve.scalar_tensor_tensor(out=hx[:, t], in0=mod2_x[layer][:, 1], scalar=1.0, in1=xs[:, t],
                                                         op0=ALU.add, op1=ALU.mult).then_inc(x_step, 1)
                                dve.wait_ge(x_step, 2 * t + 1)
                                dve.tensor_tensor(hx[:, t], hx[:, t], mod2_x[layer][:, 0], ALU.add).then_inc(x_step, 1)
                            for kt in range(1, KT, 2):
                                dve.wait_ge(turned, kt + 1)
                                dve.tensor_copy(hT[:, kt], ps[:, kt]).then_inc(moved_v, 1)

                        @block.gpsimd
                        def _(pool):
                            link = chained(pool, c_step)
                            link(pool.tensor_scalar(mod2_c[layer][:, 1], mod2_c[layer][:, 1], 1.0, None, ALU.add))
                            if load_ctx:
                                pool.wait_ge(loaded, 16)
                            for t in range(TT):
                                link(pool.tensor_tensor(hc[:, t], cs[:, t], mod2_c[layer][:, 1], ALU.mult))
                                link(pool.tensor_tensor(hc[:, t], hc[:, t], mod2_c[layer][:, 0], ALU.add))

                        @block.scalar
                        def _(act):
                            for kt in range(0, KT, 2):
                                act.wait_ge(turned, kt + 1)
                                act.copy(hT[:, kt], ps[:, kt]).then_inc(moved_a, 1)

                        @block.tensor
                        def _(pe):
                            pe.wait_ge(x_step, 2 * TT)
                            pe.wait_ge(c_step, 2 * TT + 1)
                            for kt in range(KT):
                                transpose_in(pe, kt, lambda i: (hc, hx)[i // TT][:, i % TT, kt * P:(kt + 1) * P], 2 * TT).then_inc(turned, 1)

            def residual_block(name, layer, panel, lhs, targets, upto, store=None):
                with ExitStack() as scope:
                    n_t = len(targets)
                    gated = sb(scope, f"{name}_gated", [P, 2, PANEL])
                    bn = sb(scope, f"{name}_bn", [P, n_t, 2, 6])
                    mv = sb(scope, f"{name}_mv", [P, n_t, 2])
                    ln_rows = sb(scope, f"{name}_ln", [P, 2, D])
                    ssem = stage_sems(scope, f"{name}_")
                    proj, scaled, added, stats, std, steps, mv_done, loaded, normed, stored = (
                        ssem(n) for n in ("proj", "scaled", "added", "stats", "std", "steps", "mv_done", "loaded", "normed", "stored"))
                    with nc.Block() as block:
                        @block.sync
                        def _(sp):
                            for i, n in enumerate(("ln_g_2", "ln_b_2")):
                                sp.dma_start(ln_rows[:, i], row_bcast(w[n][layer])).then_inc(loaded, 16)
                            stream.issue(sp, upto)
                            if store:
                                for t in range(n_t):
                                    sp.wait_ge(normed, t + 1)
                                    sp.dma_start(store(t), targets[t][0]).then_inc(stored, 16)
                                sp.wait_ge(stored, 16 * n_t)

                        @block.tensor
                        def _(pe):
                            for i in range(2 * n_t):
                                n, t = panel + i // n_t, i % n_t
                                if t == 0:
                                    pe.wait_ge(*stream.arrive(n))
                                if i >= 8:
                                    pe.wait_ge(scaled, i - 7)
                                for kt in range(KT):
                                    ins = pe.matmul(ps[:, i % 8], lhs(t, kt), stream.slot(n)[:, kt], start=(kt == 0), stop=(kt == KT - 1))
                                ins.then_inc(proj, 1)
                                if t == n_t - 1:
                                    pe.drain().then_inc(stream.used, 1)

                        @block.vector
                        def _(dve):
                            for i in range(2 * n_t):
                                half, t = i // n_t, i % n_t
                                cols = slice(half * PANEL, half * PANEL + PANEL)
                                x, g = targets[t]
                                dve.wait_ge(proj, i + 1)
                                dve.tensor_tensor(gated[:, i % 2], ps[:, i % 8], g[:, cols], ALU.mult).then_inc(scaled, 1)
                                dve.wait_ge(scaled, i + 1)
                                dve.scalar_tensor_tensor(out=x[:, cols], in0=x[:, cols], scalar=DEEPNORM_ALPHA, in1=gated[:, i % 2],
                                                         op0=ALU.mult, op1=ALU.add).then_inc(added, 1)
                                dve.wait_ge(added, i + 1)
                                dve.bn_stats(bn[:, t, half], x[:, cols]).then_inc(stats, 1)
                            dve.wait_ge(stats, 2 * n_t)
                            for t in range(n_t):
                                dve.bn_aggr(mv[:, t], bn[:, t]).then_inc(mv_done, 1)
                            dve.wait_ge(std, 1)
                            dve.reciprocal(mv[:, :, 1], mv[:, :, 1]).then_inc(mv_done, 1)
                            dve.wait_ge(mv_done, n_t + 1)
                            dve.wait_ge(loaded, 32)
                            for t in range(n_t):
                                x = targets[t][0]
                                dve.tensor_scalar(x, x, mv[:, t, 0:1], mv[:, t, 1:2], ALU.subtract, ALU.mult).then_inc(steps, 1)
                                dve.wait_ge(steps, 2 * t + 1)
                                dve.tensor_tensor(x, x, ln_rows[:, 0], ALU.mult).then_inc(steps, 1)
                                dve.wait_ge(steps, 2 * t + 2)
                                dve.tensor_tensor(x, x, ln_rows[:, 1], ALU.add).then_inc(normed, 1)

                        @block.scalar
                        def _(act):
                            act.wait_ge(mv_done, n_t)
                            act.activation(mv[:, :, 1], mv[:, :, 1], ACT.Sqrt, bias=eps[:, 1:2]).then_inc(std, 1)

            modulate_block("mod0", 0, True)
            with ExitStack() as ab:
                big = sb(ab, "big", [P, const_dram.shape[1] - ffn_end])

                def bigc(name):
                    at, n = parts[name]
                    return big[:, at - ffn_end:at - ffn_end + n]

                AT = 4
                qa = sb(ab, "qa", [P, AT, 2 * L])
                ka = sb(ab, "ka", [P, KV_HEADS, 2 * L])
                kraw = sb(ab, "kraw", [P, 1, 2 * L])
                va = sb(ab, "va", [P, 2 * TT, KV_HEADS, 2, A_DIM])
                sga = sb(ab, "sga", [P, AT, 2 * L])
                sgb = sb(ab, "sgb", [P, AT, 2 * L])
                bg = sb(ab, "bg", [P, AT, 2 * L])
                up = sb(ab, "up", [P, AT, 2, L + 2])
                taps_row = sb(ab, "taps_row2", [3, AT * P])
                taps = sb(ab, "taps2", [P, AT, 3])
                sink = sb(ab, "sink", [P, A_HEADS])
                catT = hT
                seqs = lambda a: a.rearrange("p (s t) -> p s t", s=2)
                pieces = [("q", j) for j in range(AT)] + [("k", 0), ("v", 0)]
                pieces += [(n, j) for n in ("ga", "xb", "bg", "cg", "gb") for j in range(AT)]
                first_tile = {"q": 0, "k": 4, "v": 5, "ga": 6, "xb": 10, "bg": 14, "cg": 18, "gb": 22}
                with ExitStack() as scope:
                    ssem = stage_sems(scope, "ab_")
                    loaded, turned, taps_done, zeroed, proj, moved_a, moved_v = (
                        ssem(n) for n in ("loaded", "turned", "taps_done", "zeroed", "proj", "moved_a", "moved_v"))
                    on_dve = [n == "cg" for n, _ in pieces]
                    count = lambda i: sum(1 for m in range(i + 1) if on_dve[m] == on_dve[i])
                    BANKS = 6
                    dot, total, put = ada_side(scope, "ada21", [
                        (ada2[1][k], [(cact[:, v], half_row(m[1], k)) for v, m in ((2, mod2_x), (3, mod2_c)) if k // 2 < m[1].shape[1]]) for k in range(6)], [6, 7])
                    bias_loaded = ssem("bias_loaded")
                    with nc.Block() as block:
                        @block.sync
                        def _(sp):
                            sp.dma_start(big[:, :], const_dram[:, ffn_end:]).then_inc(loaded, 16)
                            sp.dma_start(taps_row[:, :], w["conv_ab_2"][0]).then_inc(loaded, 16)
                            sp.dma_start(sink[:, :], row_bcast(w["sink_ab_2"][0])).then_inc(loaded, 16)
                            sp.dma_start(mod2_x[1][:, :, :].rearrange("p r d -> p (r d)"), row_bcast(w["b_ada_2"][1])).then_inc(bias_loaded, 16)
                            sp.dma_start(mod2_c[1][:, :, :].rearrange("p r d -> p (r d)"), row_bcast(w["b_ada_2"][1, 0:2 * D])).then_inc(bias_loaded, 16)
                            stream.issue(sp, AB_OUT + RING)

                        @block.gpsimd
                        def _(pool):
                            pool.memset(up[:, :, :, :], 0.0).then_inc(zeroed, 1)

                        @block.tensor
                        def _(pe):
                            pe.wait_ge(loaded, 48)
                            for j in range(AT):
                                ins = pe.transpose(ps[:, 6, 3 * j:3 * j + 3], taps_row[:, j * P:(j + 1) * P], ident[0:3, 0:3])
                            ins.then_inc(turned, 1)
                            last_panel = -1
                            for i, (name, j) in enumerate(pieces):
                                tile = first_tile[name] + j
                                n, c0 = ab_in[tile // 4], tile % 4 * P
                                if tile // 4 != last_panel:
                                    if last_panel >= 0:
                                        pe.drain().then_inc(stream.used, 1)
                                        if last_panel == 0:
                                            pe.wait_ge(taps_done, 1)
                                        total(pe, last_panel)
                                    pe.wait_ge(*stream.arrive(n))
                                    last_panel = tile // 4
                                if i >= BANKS:
                                    pe.wait_ge(moved_v if on_dve[i - BANKS] else moved_a, count(i - BANKS))
                                bank, slot = ps[:, i % BANKS], stream.slot(n)
                                if name == "v":
                                    for t in range(2 * TT):
                                        for kt in range(KT):
                                            ins = pe.matmul(bank[:, t * P:(t + 1) * P], hT[:, kt, t * P:(t + 1) * P], slot[:, kt, c0:c0 + P],
                                                            start=(kt == 0), stop=(kt == KT - 1))
                                else:
                                    for kt in range(KT):
                                        ins = pe.matmul(bank, slot[:, kt, c0:c0 + P], hT[:, kt], start=(kt == 0), stop=(kt == KT - 1))
                                ins.then_inc(proj, 1)
                            pe.drain().then_inc(stream.used, 1)

                        @block.scalar
                        def _(act):
                            act.wait_ge(zeroed, 1)
                            for i, (name, j) in enumerate(pieces):
                                if on_dve[i]:
                                    continue
                                bank = ps[:, i % BANKS]
                                act.wait_ge(proj, i + 1)
                                if name == "v":
                                    heads = bank.rearrange("p (t g d) -> p (t g) d", t=2 * TT, g=KV_HEADS)
                                    ins = act.copy(va[:, :, :, :, :].rearrange("p t g c d -> p (t g) c d"),
                                                   heads.unsqueeze(2).to_broadcast([P, 2 * TT * KV_HEADS, 2, A_DIM]))
                                elif name == "xb":
                                    ins = act.copy(up[:, j, :, 1:1 + L], seqs(bank))
                                elif name in ("ga", "gb"):
                                    ins = act.activation((sga if name == "ga" else sgb)[:, j], bank, ACT.Silu)
                                else:
                                    ins = act.copy({"q": qa, "k": kraw, "bg": bg}[name][:, j], bank)
                                ins.then_inc(moved_a, 1)

                        @block.vector
                        def _(dve):
                            dve.wait_ge(turned, 1)
                            dve.tensor_copy(taps[:, :, :], ps[:, 6, 0:3 * AT].rearrange("p (j c) -> p j c", c=3)).then_inc(taps_done, 1)
                            dve.wait_ge(bias_loaded, 32)
                            dot(dve, 0)
                            for k in range(1, 4):
                                dot(dve, k)
                                put(dve, k - 1)
                            for i, (name, j) in enumerate(pieces):
                                if on_dve[i]:
                                    if j == 2:
                                        dot(dve, 4)
                                        put(dve, 3)
                                    part = up[:, j, :, 1:1 + L]
                                    dve.wait_ge(proj, i + 1)
                                    dve.wait_ge(moved_a, count(pieces.index(("xb", j))))
                                    dve.tensor_tensor(part, seqs(ps[:, i % BANKS]), part, ALU.mult).then_inc(moved_v, 1)
                            dot(dve, 5)
                            put(dve, 4)
                            put(dve, 5)

                with ExitStack() as scope:
                    rot_sin = sb(scope, "rot_sin", [P, 2, L])
                    conv = lambda j: seqs(catT[:, AT + j])
                    ssem = stage_sems(scope, "rope_")
                    rotated, sin_done, cos_done, rope_done, conv_step, gate_done, doubled, k_moved = (
                        ssem(n) for n in ("rotated", "sin_done", "cos_done", "rope_done", "conv_step", "gate_done", "doubled", "k_moved"))
                    items = [qa[:, j, L:] for j in range(AT)] + [ka[:, g, L:] for g in range(KV_HEADS)]
                    with nc.Block() as block:
                        @block.scalar
                        def _(act):
                            for g in range(KV_HEADS):
                                act.wait_ge(doubled, g + 1)
                                act.copy(ka[:, g], ps[:, 6 + g]).then_inc(k_moved, 1)

                        @block.tensor
                        def _(pe):
                            for g in range(KV_HEADS):
                                pe.matmul(ps[:, 6 + g], bigc("kdup").rearrange("p (g m) -> p g m", g=KV_HEADS)[:, g], kraw[:, 0],
                                          start=True, stop=True).then_inc(doubled, 1)
                            for i, a in enumerate(items):
                                if i == AT:
                                    pe.wait_ge(k_moved, KV_HEADS)
                                pe.matmul(ps[:, i, 0:L], bigc("rot"), a, start=True, stop=True).then_inc(rotated, 1)

                        @block.vector
                        def _(dve):
                            for i, a in enumerate(items):
                                dve.wait_ge(rotated, i + 1)
                                if i >= 2:
                                    dve.wait_ge(rope_done, i - 1)
                                dve.tensor_tensor(rot_sin[:, i % 2], ps[:, i, 0:L], bigc("sin"), ALU.mult).then_inc(sin_done, 1)
                                dve.tensor_tensor(a, a, bigc("cos"), ALU.mult).then_inc(cos_done, 1)
                                dve.wait_ge(sin_done, i + 1)
                                dve.wait_ge(cos_done, i + 1)
                                dve.tensor_tensor(a, a, rot_sin[:, i % 2], ALU.add).then_inc(rope_done, 1)
                            link = chained(dve, conv_step)
                            for j in range(AT):
                                for c in range(3):
                                    src = up[:, j, :, c:c + L]
                                    if c == 0:
                                        link(dve.tensor_scalar(conv(j), src, taps[:, j, 0:1], None, ALU.mult))
                                    else:
                                        link(dve.scalar_tensor_tensor(out=conv(j), in0=src, scalar=taps[:, j, c:c + 1], in1=conv(j),
                                                                      op0=ALU.mult, op1=ALU.add))

                        @block.gpsimd
                        def _(pool):
                            for j in range(AT):
                                pool.tensor_tensor(bg[:, j], bg[:, j], sgb[:, j], ALU.mult).then_inc(gate_done, 1)
                            for j in range(AT):
                                pool.wait_ge(gate_done, j + 1)
                                pool.wait_ge(conv_step, 3 * j + 3)
                                pool.tensor_tensor(catT[:, AT + j], catT[:, AT + j], bg[:, j], ALU.mult)

                with ExitStack() as scope:
                    BUF = 3
                    s_buf = up[:, :, :, :].rearrange("p j s t -> p (j s t)")[:, 0:BUF * 2 * L].rearrange("p (b k) -> p b k", b=BUF)
                    pT = bg[:, 0:BUF]
                    small_t = sb(scope, "softmax_rows", [P, 2 * TT * A_HEADS, 6])
                    ssem = stage_sems(scope, "att_")
                    scored, biased, maxed, summed, sunk, inverted, scaled, turned, moved, outed, gated, row_step = (
                        ssem(n) for n in ("scored", "biased", "maxed", "summed", "sunk", "inverted", "scaled", "turned", "moved", "outed", "gated",
                                          "row_step"))
                    work = [(t, h) for t in range(2 * TT) for h in range(A_HEADS)]
                    n_keys = lambda t: 2 * L if t >= TT else L
                    with nc.Block() as block:
                        @block.tensor
                        def _(pe):
                            def scores(i):
                                t, h = work[i]
                                at = slice(h % 2 * A_DIM, h % 2 * A_DIM + A_DIM)
                                if i >= 2:
                                    pe.wait_ge(biased, i - 1)
                                pe.matmul(ps[:, i % 2, 0:n_keys(t)], qa[at, h // 2, t * P:(t + 1) * P], ka[at, h // 4, 0:n_keys(t)],
                                          start=True, stop=True).then_inc(scored, 1)

                            def turn(i):
                                t, h = work[i]
                                pe.wait_ge(scaled, i + 1)
                                if i >= 2:
                                    pe.wait_ge(moved, i - 1)
                                transpose_in(pe, 2 + i % 2, lambda m: s_buf[:, i % BUF, m * P:(m + 1) * P], n_keys(t) // P).then_inc(turned, 1)

                            def outputs(i):
                                t, h = work[i]
                                pe.wait_ge(moved, i + 1)
                                if i >= 2:
                                    pe.wait_ge(gated, i - 1)
                                n = n_keys(t) // P
                                for m in range(n):
                                    ins = pe.matmul(ps[:, 4 + i % 2, 0:P], va[:, m, h // 4].rearrange("p c d -> p (c d)"), pT[:, i % BUF, m * P:(m + 1) * P],
                                                    start=(m == 0), stop=(m == n - 1))
                                ins.then_inc(outed, 1)

                            N = len(work)
                            for i in range(N + 3):
                                if i < N:
                                    scores(i)
                                if 2 <= i < N + 2:
                                    turn(i - 2)
                                if i >= 3:
                                    outputs(i - 3)

                        @block.vector
                        def _(dve):
                            def soft(i):
                                t, h = work[i]
                                keys, row = n_keys(t), small_t[:, i]
                                dve.wait_ge(scored, i + 1)
                                if i >= BUF:
                                    dve.wait_ge(turned, i - BUF + 1)
                                s = s_buf[:, i % BUF, 0:keys]
                                if t >= TT:
                                    win = bigc("win").rearrange("p (t k) -> p t k", t=TT)[:, t - TT]
                                    dve.scalar_tensor_tensor(out=s, in0=ps[:, i % 2, 0:keys], scalar=A_DIM ** -0.5, in1=win,
                                                             op0=ALU.mult, op1=ALU.add).then_inc(biased, 1)
                                else:
                                    dve.tensor_scalar(s, ps[:, i % 2, 0:keys], A_DIM ** -0.5, None, ALU.mult).then_inc(biased, 1)
                                dve.wait_ge(biased, i + 1)
                                dve.tensor_reduce(row[:, 0:1], s, AX.X, ALU.max).then_inc(row_step, 1)
                                dve.wait_ge(row_step, 2 * i + 1)
                                dve.tensor_tensor(row[:, 0:1], row[:, 0:1], sink[:, h:h + 1], ALU.max).then_inc(row_step, 1)
                                dve.wait_ge(row_step, 2 * i + 2)
                                dve.tensor_scalar(row[:, 1:2], row[:, 0:1], -1.0, None, ALU.mult).then_inc(maxed, 1)

                            def invert(i):
                                row = small_t[:, i]
                                dve.wait_ge(summed, i + 1)
                                dve.wait_ge(sunk, i + 1)
                                dve.tensor_tensor(row[:, 4:5], row[:, 2:3], row[:, 3:4], ALU.add).then_inc(inverted, 1)
                                dve.wait_ge(inverted, 2 * i + 1)
                                dve.reciprocal(row[:, 4:5], row[:, 4:5]).then_inc(inverted, 1)

                            def gate(i):
                                t, h = work[i]
                                at = slice(h % 2 * A_DIM, h % 2 * A_DIM + A_DIM)
                                dve.wait_ge(outed, i + 1)
                                dve.tensor_tensor(catT[at, h // 2, t * P:(t + 1) * P], ps[at, 4 + i % 2, 0:P], sga[at, h // 2, t * P:(t + 1) * P],
                                                  ALU.mult).then_inc(gated, 1)

                            N = len(work)
                            for i in range(N + 3):
                                if i < N:
                                    soft(i)
                                if 1 <= i < N + 1:
                                    invert(i - 1)
                                if i >= 3:
                                    gate(i - 3)

                        @block.scalar
                        def _(act):
                            def exps(i):
                                t, h = work[i]
                                s, row = s_buf[:, i % BUF, 0:n_keys(t)], small_t[:, i]
                                act.wait_ge(maxed, i + 1)
                                act.activation(s, s, ACT.Exp, bias=row[:, 1:2], accum_out=row[:, 2:3]).then_inc(summed, 1)
                                act.activation(row[:, 3:4], sink[:, h:h + 1], ACT.Exp, bias=row[:, 1:2]).then_inc(sunk, 1)

                            def move(i):
                                t, h = work[i]
                                act.wait_ge(turned, i + 1)
                                if i >= BUF:
                                    act.wait_ge(outed, i - BUF + 1)
                                act.copy(pT[:, i % BUF, 0:n_keys(t)], ps[:, 2 + i % 2, 0:n_keys(t)]).then_inc(moved, 1)

                            N = len(work)
                            for i in range(N + 2):
                                if i < N:
                                    exps(i)
                                if i >= 2:
                                    move(i - 2)

                        @block.gpsimd
                        def _(pool):
                            for i, (t, h) in enumerate(work):
                                s = s_buf[:, i % BUF, 0:n_keys(t)]
                                pool.wait_ge(inverted, 2 * i + 2)
                                pool.wait_ge(summed, i + 1)
                                pool.tensor_scalar(s, s, small_t[:, i, 4:5], None, ALU.mult).then_inc(scaled, 1)
            targets = [(cs[:, t], mod2_c[0][:, 2]) for t in range(TT)] + [(xs[:, t], mod2_x[0][:, 2]) for t in range(TT)]
            residual_block("res0", 0, AB_OUT, lambda i, kt: hT[:, kt, i * P:(i + 1) * P], targets, C_IN + RING)

            modulate_block("mod1", 1, False)
            with nc.Block() as block:
                @block.vector
                def _(dve):
                    dve.tensor_copy(gate1[:, :], mod2_x[1][:, 2])
            rows2.close()
            high.close()
            with ExitStack() as rec:
                qT = sb(rec, "cqT", [P, H, L])
                kT = [sb(rec, f"ckT{d}", [P, H, 2 * L]) for d in range(2)]
                bT = [sb(rec, f"cbT{d}", [P, H, 2 * L]) for d in range(2)]
                vtok = sb(rec, "cvtok", [P, 2 * TT, D])
                state = sb(rec, "cstate", [P, 2 * H, P])
                sg = sb(rec, "csg", [P, TT, D])
                otok = hT[:, 0:KT // 2].rearrange("p k (t c) -> p (k t c)", t=2).rearrange("p (t d) -> p t d", t=TT)
                with ExitStack() as scope:
                    near1 = sb(scope, "near1", [P, H, 2 * L])
                    ssem = stage_sems(scope, "cproj_")
                    proj, moved_a, moved_v, sig = (ssem(n) for n in ("proj", "moved_a", "moved_v", "sig"))
                    abs_done, near1_done, ln_done, logf_done = (ssem(n) for n in ("abs_done", "near1_done", "ln_done", "logf_done"))
                    LN = 2
                    pieces = [("zf", j) for j in range(H)] + [("zb", j) for j in range(H)] + [("q", j) for j in range(H)]
                    pieces += [("i", j) for j in range(2 * 2 * TT)] + [("g", j) for j in range(2 * TT)]
                    on_dve = [n in ("zf", "zb") or (n == "i" and j % 2 == 1) for n, j in pieces]
                    count = lambda i: sum(1 for m in range(i + 1) if on_dve[m] == on_dve[i])
                    n_sig = lambda i: sum(1 for n, _ in pieces[:i + 1] if n in ("zf", "zb"))
                    with nc.Block() as block:
                        @block.sync
                        def _(sp):
                            stream.issue(sp, END)

                        @block.tensor
                        def _(pe):
                            for i, (name, j) in enumerate(pieces):
                                of = TT if name == "g" else 4
                                first_of, last_of = j % of == 0, j % of == of - 1
                                n = C_IN + {"zf": 0, "zb": 2, "q": 4, "i": 6, "g": 8}[name] + j // of
                                if first_of:
                                    pe.wait_ge(*stream.arrive(n))
                                if i >= 8:
                                    pe.wait_ge(moved_v if on_dve[i - 8] else moved_a, count(i - 8))
                                bank, slot = ps[:, i % 8], stream.slot(n)
                                for kt in range(KT):
                                    edge = dict(start=(kt == 0), stop=(kt == KT - 1))
                                    if name == "i":
                                        ins = pe.matmul(bank, hT[:, kt, j % 4 * P:(j % 4 + 1) * P], slot[:, kt], **edge)
                                    elif name == "g":
                                        ins = pe.matmul(bank, hT[:, kt, L + j % TT * P:L + (j % TT + 1) * P], slot[:, kt], **edge)
                                    elif name == "q":
                                        ins = pe.matmul(bank[:, 0:L], slot[:, kt, j % 4 * P:(j % 4 + 1) * P], hT[:, kt, L:], **edge)
                                    else:
                                        ins = pe.matmul(bank, slot[:, kt, j % 4 * P:(j % 4 + 1) * P], hT[:, kt], **edge)
                                ins.then_inc(proj, 1)
                                if last_of:
                                    pe.drain().then_inc(stream.used, 1)

                        @block.scalar
                        def _(act):
                            def logs(d):
                                for m in range(d * H, d * H + H, LN):
                                    act.wait_ge(near1_done, m + LN)
                                    part = near1[:, m % H:m % H + LN]
                                    act.activation(part, part, ACT.Ln).then_inc(ln_done, 1)

                            for i, (name, j) in enumerate(pieces):
                                if name in ("zb", "q") and j == 0:
                                    logs(name == "q")
                                if name == "i" and on_dve[i]:
                                    continue
                                bank = ps[:, i % 8]
                                act.wait_ge(proj, i + 1)
                                if name == "q":
                                    act.activation(qT[:, j], bank[:, 0:L], ACT.Silu).then_inc(moved_a, 1)
                                elif name == "i":
                                    act.copy(vtok[:, j % 4, j // 4 * PANEL:(j // 4 + 1) * PANEL], bank).then_inc(moved_a, 1)
                                elif name == "g":
                                    act.activation(sg[:, j % TT, j // TT * PANEL:(j // TT + 1) * PANEL], bank, ACT.Silu).then_inc(moved_a, 1)
                                else:
                                    if name == "zb":
                                        act.wait_ge(logf_done, j + 1)
                                    act.activation(near1[:, j], bank, ACT.Abs).then_inc(abs_done, 1)
                                    act.activation(kT[name == "zb"][:, j], bank, ACT.Sigmoid, scale=-1.0).then_inc(sig, 1)
                                    act.wait_ge(abs_done, i + 1)
                                    act.activation(near1[:, j], near1[:, j], ACT.Sigmoid).then_inc(near1_done, 1)

                        @block.vector
                        def _(dve):
                            def cumulate(d):
                                for h in range(H):
                                    dve.wait_ge(ln_done, (d * H + h) // LN + 1)
                                    dve.wait_ge(moved_v, d * H + h + 1)
                                    dve.tensor_tensor(bT[d][:, h], bT[d][:, h], near1[:, h], ALU.add).then_inc(logf_done, 1)
                                    dve.wait_ge(logf_done, d * H + h + 1)
                                    for t in range(2 * TT):
                                        chunk = bT[d][:, h, t * P:(t + 1) * P]
                                        if d:
                                            chunk = chunk[:, ::-1]
                                        dve.tensor_tensor_scan(chunk, ones, chunk, 0.0, ALU.mult, ALU.add)

                            for i, (name, j) in enumerate(pieces):
                                if not on_dve[i]:
                                    continue
                                if name == "zb" and j == 0:
                                    cumulate(0)
                                if name == "i" and j == 1:
                                    cumulate(1)
                                dve.wait_ge(proj, i + 1)
                                if name == "i":
                                    dve.tensor_copy(vtok[:, j % 4, j // 4 * PANEL:(j // 4 + 1) * PANEL], ps[:, i % 8]).then_inc(moved_v, 1)
                                else:
                                    dve.wait_ge(sig, n_sig(i))
                                    dve.tensor_scalar(bT[name == "zb"][:, j], ps[:, i % 8], 0.0, None, ALU.min).then_inc(moved_v, 1)
                            dve.wait_ge(moved_a, H)
                            dve.tensor_scalar(qT[:, :, :], qT[:, :, :], P ** -0.5, None, ALU.mult)

                with ExitStack() as scope:
                    spare = stream.slot(C_OUT + 2).rearrange("p k n -> p (k n)")
                    heads_of = lambda a: a.rearrange("p (h c) -> p h c", h=H)
                    ksf = [sb(scope, "ksf", [P, H, P])[:, :, :], heads_of(spare[:, 0:D])]
                    kst = [sb(scope, "kst", [P, H, P])[:, :, :], heads_of(spare[:, D:2 * D])]
                    scT = [sb(scope, "scT", [P, H, P])[:, :, :], heads_of(hT[:, KT // 2:KT // 2 + 2].rearrange("p k t -> p (k t)"))]
                    lb = [sb(scope, "lb", [P, 2, H, P])[:, :, :, :],
                          spare[:, 2 * D:].rearrange("p (l h c) -> p l h c", l=2, h=H)]
                    dn = sb(scope, "dn", [P, 2, H])
                    DIRS = range(2)
                    for step in range(2 * TT):
                        on_x, more = step >= TT, step < 2 * TT - 1
                        tiles = (step, step ^ 1)
                        chunk = lambda a, d: a[:, :, tiles[d] * P:(tiles[d] + 1) * P]
                        b, k = [chunk(bT[d], d) for d in DIRS], [chunk(kT[d], d) for d in DIRS]
                        q = [qT[:, :, (t - TT) * P:(t - TT + 1) * P] if on_x else None for t in tiles]
                        S = [state[:, d * H:(d + 1) * H] for d in DIRS]
                        last = (P - 1, 0)
                        k_side, q_side = (0, 1), (1, 0)
                        v = lambda d, h: vtok[:, tiles[d], h * P:(h + 1) * P]
                        two = lambda d, n: ps[:, 4 * d + 2 * n:4 * d + 2 * n + 2].rearrange("p b (h c) -> p (b h) c", h=4)
                        one = lambda d, n, h: ps[:, 4 * d + 2 * n + h // 4, h % 4 * P:(h % 4 + 1) * P]
                        level_bank = lambda d, lv: ps[:, 4 * d + 2 + lv % 2]

                        def border(d, lv):
                            return half_cols(b[d], lv, k_side[d])[:, :, :, (0 if d else (1 << lv) - 1)]

                        with ExitStack() as inner:
                            ssem = stage_sems(inner, f"rec{step}_")
                            both = lambda name: [ssem(f"{name}{d}") for d in DIRS]
                            (ks_arg, ks_exp, ks_done, kst_turned, kst_moved, q_exp, q_done, diag, diag_done, arg, lexp, lk, lq, level, put_done,
                             o_done, o_added, s_done, dn_done) = (both(n) for n in (
                                 "ks_arg", "ks_exp", "ks_done", "kst_turned", "kst_moved", "q_exp", "q_done", "diag", "diag_done", "arg", "lexp",
                                 "lk", "lq", "level", "put_done", "o_done", "o_added", "s_done", "dn_done"))
                            with nc.Block() as block:
                                @block.vector
                                def _(dve):
                                    def args(d, lv):
                                        if lv >= 2:
                                            dve.wait_ge(level[d], lv - 1)
                                        n, j = P >> (lv + 1), 1 << lv
                                        at = border(d, lv).unsqueeze(3).to_broadcast([P, H, n, j])
                                        keys, queries = (half_cols(lb[d][:, lv % 2], lv, side[d]) for side in (k_side, q_side))
                                        dve.tensor_tensor(keys, at, half_cols(b[d], lv, k_side[d]), ALU.subtract)
                                        dve.tensor_tensor(queries, half_cols(b[d], lv, q_side[d]), at, ALU.subtract).then_inc(arg[d], 1)

                                    def times_q(d, lv):
                                        part = half_cols(lb[d][:, lv % 2], lv, q_side[d])
                                        dve.wait_ge(lexp[d], lv + 1)
                                        dve.tensor_tensor(part, part, half_cols(q[d], lv, q_side[d]), ALU.mult).then_inc(lq[d], 1)

                                    def put(d, lv):
                                        mask = lev[:, 1 - d, lv].unsqueeze(1).to_broadcast([P, H, P // 2]).bitcast(I32)
                                        dve.wait_ge(level[d], lv + 1)
                                        if lv == 0:
                                            dve.wait_ge(diag_done[d], 1)
                                        else:
                                            dve.wait_ge(put_done[d], lv)
                                        dve.copy_predicated(half_cols(scT[d], lv, q_side[d]), packed_cols(mask, lv),
                                                            packed_cols(heads_of(level_bank(d, lv)), lv)).then_inc(put_done[d], 1)

                                    if more:
                                        for d in DIRS:
                                            dve.tensor_tensor(ksf[d], b[d][:, :, last[d]:last[d] + 1].to_broadcast([P, H, P]), b[d],
                                                              ALU.subtract).then_inc(ks_arg[d], 1)
                                    if on_x:
                                        for lv in range(2):
                                            for d in DIRS:
                                                args(d, lv)
                                        for d in DIRS:
                                            dve.wait_ge(diag[d], 1)
                                            dve.tensor_tensor(scT[d], two(d, 0), ident.unsqueeze(1).to_broadcast([P, H, P]), ALU.mult).then_inc(diag_done[d], 1)
                                        for lv in range(LEVELS):
                                            for d in DIRS:
                                                times_q(d, lv)
                                                if lv >= 1:
                                                    put(d, lv - 1)
                                            for d in DIRS:
                                                if lv + 2 < LEVELS:
                                                    args(d, lv + 2)
                                        for d in DIRS:
                                            put(d, LEVELS - 1)
                                        for d in DIRS:
                                            x_tile = tiles[d] - TT
                                            o = heads_of(otok[:, x_tile])
                                            dve.wait_ge(o_done[d], 1)
                                            if step == TT:
                                                dve.tensor_copy(o, two(d, 0)).then_inc(o_added[d], 1)
                                            else:
                                                dve.tensor_tensor(o, two(d, 0), o, ALU.add).then_inc(o_added[d], 1)
                                    if more:
                                        for d in DIRS:
                                            dve.wait_ge(s_done[d], 1)
                                            dve.wait_ge(dn_done[d], 1)
                                            for h in range(H):
                                                if step:
                                                    dve.scalar_tensor_tensor(out=S[d][:, h], in0=S[d][:, h], scalar=dn[:, d, h:h + 1], in1=one(d, 1, h),
                                                                             op0=ALU.mult, op1=ALU.add)
                                                else:
                                                    dve.tensor_copy(S[d][:, h], one(d, 1, h))

                                @block.scalar
                                def _(act):
                                    if more:
                                        for d in DIRS:
                                            act.activation(dn[:, d], b[d][:, :, last[d]], ACT.Exp).then_inc(dn_done[d], 1)
                                            act.wait_ge(ks_arg[d], 1)
                                            act.activation(ksf[d], ksf[d], ACT.Exp).then_inc(ks_exp[d], 1)

                                    def move_keys():
                                        for d in DIRS:
                                            act.wait_ge(kst_turned[d], 1)
                                            act.copy(kst[d], two(d, 0)).then_inc(kst_moved[d], 1)

                                    if on_x:
                                        for lv in range(LEVELS):
                                            for d in DIRS:
                                                act.wait_ge(arg[d], lv + 1)
                                                act.activation(lb[d][:, lv % 2], lb[d][:, lv % 2], ACT.Exp).then_inc(lexp[d], 1)
                                            if lv == 3 and more:
                                                move_keys()
                                        for d in DIRS:
                                            act.activation(ksf[d], b[d], ACT.Exp).then_inc(q_exp[d], 1)
                                    else:
                                        move_keys()

                                @block.gpsimd
                                def _(pool):
                                    if more:
                                        for d in DIRS:
                                            pool.wait_ge(ks_exp[d], 1)
                                            pool.tensor_tensor(ksf[d], ksf[d], k[d], ALU.mult).then_inc(ks_done[d], 1)
                                    if on_x:
                                        for lv in range(LEVELS):
                                            for d in DIRS:
                                                part = half_cols(lb[d][:, lv % 2], lv, k_side[d])
                                                pool.wait_ge(lexp[d], lv + 1)
                                                pool.tensor_tensor(part, part, half_cols(k[d], lv, k_side[d]), ALU.mult).then_inc(lk[d], 1)
                                        for d in DIRS:
                                            pool.wait_ge(q_exp[d], 1)
                                            pool.tensor_tensor(ksf[d], ksf[d], q[d], ALU.mult).then_inc(q_done[d], 1)

                                @block.tensor
                                def _(pe):
                                    def turn_keys():
                                        for d in DIRS:
                                            pe.wait_ge(ks_done[d], 1)
                                            if on_x:
                                                pe.wait_ge(diag_done[d], 1)
                                            transpose_in(pe, 4 * d, lambda i: ksf[d][:, i], 4)
                                            transpose_in(pe, 4 * d + 1, lambda i: ksf[d][:, 4 + i], 4).then_inc(kst_turned[d], 1)

                                    if on_x:
                                        for d in DIRS:
                                            for h in range(H):
                                                ins = pe.matmul(one(d, 0, h), k[d][:, h], q[d][:, h], start=True, stop=True)
                                            ins.then_inc(diag[d], 1)
                                        for lv in range(LEVELS):
                                            for d in DIRS:
                                                pe.wait_ge(lk[d], lv + 1)
                                                pe.wait_ge(lq[d], lv + 1)
                                                if lv >= 2:
                                                    pe.wait_ge(put_done[d], lv - 1)
                                                for h in range(H):
                                                    ins = pe.matmul(level_bank(d, lv)[:, 64 * h:64 * h + 64], lb[d][:, lv % 2, h],
                                                                    half_cols(lb[d][:, lv % 2, h], lv, q_side[d]), start=True, stop=True)
                                                ins.then_inc(level[d], 1)
                                            if lv == 1 and more:
                                                turn_keys()
                                        for d in DIRS:
                                            pe.wait_ge(put_done[d], LEVELS)
                                            pe.wait_ge(q_done[d], 1)
                                            if more:
                                                pe.wait_ge(kst_moved[d], 1)
                                            for h in range(H):
                                                pe.matmul(one(d, 0, h), ksf[d][:, h], S[d][:, h], start=True, stop=False)
                                                ins = pe.matmul(one(d, 0, h), scT[d][:, h], v(d, h), start=False, stop=True)
                                            ins.then_inc(o_done[d], 1)
                                    else:
                                        turn_keys()
                                    if more:
                                        for d in DIRS:
                                            pe.wait_ge(kst_moved[d], 1)
                                            for h in range(H):
                                                ins = pe.matmul(one(d, 1, h), kst[d][:, h], v(d, h), start=True, stop=True)
                                            ins.then_inc(s_done[d], 1)

                yT = hT[:, KT // 2:].rearrange("p k t -> p (k t)").rearrange("p (k t) -> p k t", k=KT)
                with ExitStack() as scope:
                    sq = sb(scope, "csq", [P, TT, D])
                    rms = sb(scope, "crms", [P, TT * H])
                    gn = sb(scope, "cgn", [P, P])
                    ssem = stage_sems(scope, "cout_")
                    loaded, squared, steps, std, scaled, gained, gated, turned, moved = (
                        ssem(n) for n in ("loaded", "squared", "steps", "std", "scaled", "gained", "gated", "turned", "moved"))
                    per_head = lambda a: a.rearrange("p t (h c) -> p (t h) c", h=H)
                    with nc.Block() as block:
                        @block.sync
                        def _(sp):
                            sp.dma_start(gn[:, :], row_bcast(w["gnorm_c_2"][0])).then_inc(loaded, 16)

                        @block.scalar
                        def _(act):
                            act.activation(sq[:, :, :], otok, ACT.Square).then_inc(squared, 1)
                            act.wait_ge(steps, 1)
                            act.activation(rms[:, :], rms[:, :], ACT.Sqrt, bias=eps[:, 0:1], scale=1.0 / P).then_inc(std, 1)
                            for b in range(4):
                                act.wait_ge(turned, b + 1)
                                act.copy(yT[:, 2 * b:2 * b + 2], ps[:, b].rearrange("p (k t) -> p k t", k=2)).then_inc(moved, 1)

                        @block.vector
                        def _(dve):
                            dve.wait_ge(squared, 1)
                            dve.tensor_reduce(rms[:, :], per_head(sq[:, :, :]), AX.X, ALU.add).then_inc(steps, 1)
                            dve.wait_ge(std, 1)
                            dve.reciprocal(rms[:, :], rms[:, :]).then_inc(steps, 1)
                            dve.wait_ge(steps, 2)
                            for t in range(TT):
                                o, r = otok[:, t].rearrange("p (h c) -> p h c", h=H), rms[:, t * H:(t + 1) * H]
                                dve.tensor_tensor(o, o, r.unsqueeze(2).to_broadcast([P, H, P]), ALU.mult).then_inc(scaled, 1)

                        @block.gpsimd
                        def _(pool):
                            pool.wait_ge(loaded, 16)
                            for t in range(TT):
                                g = sg[:, t].rearrange("p (h c) -> p h c", h=H)
                                pool.tensor_tensor(g, g, gn[:, :].unsqueeze(1).to_broadcast([P, H, P]), ALU.mult).then_inc(gained, 1)
                            for t in range(TT):
                                pool.wait_ge(gained, t + 1)
                                pool.wait_ge(scaled, t + 1)
                                pool.tensor_tensor(otok[:, t], otok[:, t], sg[:, t], ALU.mult).then_inc(gated, 1)

                        @block.tensor
                        def _(pe):
                            pe.wait_ge(gated, TT)
                            for b in range(4):
                                transpose_in(pe, b, lambda i: otok[:, i % TT, (2 * b + i // TT) * P:(2 * b + i // TT + 1) * P], 2 * TT).then_inc(turned, 1)

                residual_block("res1", 1, C_OUT, lambda i, kt: yT[:, kt, i * P:(i + 1) * P], [(xs[:, t], gate1[:, :]) for t in range(TT)], END,
                               store=lambda t: out[0, t * P:(t + 1) * P, :])


_INS = ["x", "c", "ctx", "c_ctx", "ada_w", "ada_b", "norm_mix_g", "w_in", "conv_w", "a_log", "dt_bias",
        "gdn_norm_g", "sgu_ln_g", "sgu_ln_b", "sgu_w", "sgu_b", "w_branch_a", "w_branch_b", "w_out",
        "norm_ffn_g", "router_group_w", "router_group_b", "router_expert_w", "router_expert_b",
        "expert_w1", "expert_w3", "expert_w2", "final_norm_g", "c_2", "ctx_2", "c_ctx_2", "w_ada_2",
        "b_ada_2", "ln_g_2", "ln_b_2", "w_in_ab_2", "w_out_ab_2", "sink_ab_2", "conv_ab_2", "w_in_c_2",
        "w_out_c_2", "lb_c_2", "gnorm_c_2"]


def kernel(**inputs):
    import concourse.bacc as bacc
    from concourse.bass_utils import run_bass_kernel_spmd

    nc = bacc.Bacc("TRN2", target_bir_lowering=False, num_devices=1)
    arrays, w = {}, {}
    for name in _INS:
        a = np.ascontiguousarray(inputs[name])
        arrays["in_" + name] = a
        w[name] = nc.dram_tensor("in_" + name, a.shape, mybir.dt.from_np(a.dtype), kind="ExternalInput").ap()
    table = shape_constants()[0]
    arrays["shape_constants"] = table
    consts = nc.dram_tensor("shape_constants", table.shape, F32, kind="ExternalInput").ap()
    out = nc.dram_tensor("out", (1, L, D), F32, kind="ExternalOutput").ap()
    build(nc, w, out, consts)
    r = run_bass_kernel_spmd(nc, [arrays], core_ids=[0])
    return r.results[0]["out"]
```
